# Optimizing a Trainium2 kernel written in Bass

```python
import jax, jax.numpy as jnp
from jax import lax
import numpy as np

D_MODEL = 1024
BATCH = 1
SEQ = 1024
DEPTH = 1
DEC_BATCH = 1
DEC_SEQ = 64
PAST_LEN = 2048

CHUNK = 64
Q_BLOCK = 128
A_HEADS = 8
NOPE_DIM = 64
ROPE_DIM = 32
V_DIM = 64
Q_LORA = 384
KV_LORA = 256
ROPE_THETA = 10000.0
SM_SCALE = (NOPE_DIM + ROPE_DIM) ** -0.5
R_HEADS = 8
R_HEAD_DIM = 64
R_WIDTH = R_HEADS * R_HEAD_DIM
DECAY_LORA = 64
AAA_LORA = 64
GATE_LORA = 128
RW_COLS = 3 * R_WIDTH + DECAY_LORA + AAA_LORA + GATE_LORA
MLA_COLS = Q_LORA + KV_LORA + ROPE_DIM
IN_COLS = MLA_COLS + RW_COLS
D_MIX = A_HEADS * V_DIM + R_WIDTH
D_FF = -(-8 * D_MODEL // (3 * 256)) * 256
RMS_EPS = 1e-6
LNX_EPS = 64e-5

kernel_name = 'hybrid_mla_rwkv7_stream_step'

def rms_norm(x, g):
    xf = x.astype(jnp.float32)
    y = xf * lax.rsqrt(jnp.mean(xf * xf, axis=-1, keepdims=True) + RMS_EPS)
    return (y * g.astype(jnp.float32)).astype(x.dtype)

def rope_tables(pos):
    inv = ROPE_THETA ** (-jnp.arange(0, ROPE_DIM, 2, dtype=jnp.float32) / ROPE_DIM)
    ang = pos.astype(jnp.float32)[:, None] * inv[None, :]
    return jnp.cos(ang), jnp.sin(ang)

def apply_rope(x, cos, sin):
    xf = x.astype(jnp.float32)
    x1, x2 = jnp.split(xf, 2, axis=-1)
    return jnp.concatenate([x1 * cos - x2 * sin, x1 * sin + x2 * cos], axis=-1).astype(x.dtype)

def mla_attend(q_lat, q_rope, ckv, krope, mask):
    s = (jnp.einsum('bqhc,bkc->bhqk', q_lat, ckv, preferred_element_type=jnp.float32)
         + jnp.einsum('bqhr,bkr->bhqk', q_rope, krope, preferred_element_type=jnp.float32)) * SM_SCALE
    if mask is not None:
        s = jnp.where(mask, s, -jnp.inf)
    p = jax.nn.softmax(s, axis=-1).astype(ckv.dtype)
    return jnp.einsum('bhqk,bkc->bqhc', p, ckv)

def prompt_attention(q_lat, q_rope, ckv, krope):
    B, T = q_lat.shape[:2]
    n_blocks = T // Q_BLOCK
    k_chunk = jnp.arange(T) // CHUNK

    def one_block(i):
        q0 = i * Q_BLOCK
        ql = lax.dynamic_slice_in_dim(q_lat, q0, Q_BLOCK, axis=1)
        qr = lax.dynamic_slice_in_dim(q_rope, q0, Q_BLOCK, axis=1)
        q_chunk = (q0 + jnp.arange(Q_BLOCK)) // CHUNK
        mask = k_chunk[None, :] <= q_chunk[:, None]
        return mla_attend(ql, qr, ckv, krope, mask)

    out = lax.map(one_block, jnp.arange(n_blocks))
    return jnp.moveaxis(out, 0, 1).reshape(B, T, A_HEADS, KV_LORA)

def wkv_scan(S0, r, decay, k, v, kk, a):
    def step(S, inp):
        r_t, w_t, k_t, v_t, kk_t, a_t = inp
        sa = jnp.einsum('bhvk,bhk->bhv', S, -kk_t)
        S = (S * w_t[:, :, None, :] + sa[..., None] * (kk_t * a_t)[:, :, None, :]
             + v_t[..., None] * k_t[:, :, None, :])
        return S, jnp.einsum('bhvk,bhk->bhv', S, r_t)
    xs = tuple(jnp.moveaxis(t.astype(jnp.float32), 1, 0) for t in (r, decay, k, v, kk, a))
    S, ys = lax.scan(step, S0.astype(jnp.float32), xs)
    return S.astype(S0.dtype), jnp.moveaxis(ys, 0, 1)

def head_group_norm(y, g, b):
    mu = jnp.mean(y, axis=-1, keepdims=True)
    var = jnp.mean(jnp.square(y - mu), axis=-1, keepdims=True)
    yn = (y - mu) * lax.rsqrt(var + LNX_EPS)
    B, T = y.shape[:2]
    return yn.reshape(B, T, R_WIDTH) * g.astype(jnp.float32) + b.astype(jnp.float32)

def mixer(h, pos, ckv_past, krope_past, wkv0, shift0, lw):
    B, T, _ = h.shape
    proj = h @ lw['w_in']
    c_q, c_kv, k_r, rw = jnp.split(proj, [Q_LORA, Q_LORA + KV_LORA, MLA_COLS], axis=-1)
    cos, sin = rope_tables(pos)
    q = (rms_norm(c_q, lw['q_norm_g']) @ lw['w_uq']).reshape(B, T, A_HEADS, NOPE_DIM + ROPE_DIM)
    q_nope, q_rope = jnp.split(q, [NOPE_DIM], axis=-1)
    q_rope = apply_rope(q_rope, cos[:, None, :], sin[:, None, :])
    ckv_new = rms_norm(c_kv, lw['kv_norm_g'])
    krope_new = apply_rope(k_r, cos, sin)
    q_lat = jnp.einsum('bqhd,chd->bqhc', q_nope, lw['w_uk'])
    if ckv_past is None:
        o_lat = prompt_attention(q_lat, q_rope, ckv_new, krope_new)
    else:
        ckv_all = jnp.concatenate([ckv_past, ckv_new], axis=1)
        krope_all = jnp.concatenate([krope_past, krope_new], axis=1)
        o_lat = mla_attend(q_lat, q_rope, ckv_all, krope_all, None)
    o_attn = jnp.einsum('bqhc,chd->bqhd', o_lat, lw['w_uv']).reshape(B, T, A_HEADS * V_DIM)
    rw_prev = jnp.concatenate([shift0[:, None, :].astype(rw.dtype), rw[:, :-1]], axis=1)
    rw_mix = rw + (rw_prev - rw) * lw['rw_mu']
    shift_new = rw[:, -1]
    r, k, v, w_lo, a_lo, g_lo = jnp.split(
        rw_mix, [R_WIDTH, 2 * R_WIDTH, 3 * R_WIDTH, 3 * R_WIDTH + DECAY_LORA,
                 3 * R_WIDTH + DECAY_LORA + AAA_LORA], axis=-1)
    w_raw = (lw['rw_w0'] + jnp.tanh(w_lo) @ lw['rw_w2']).astype(jnp.float32)
    decay = jnp.exp(-jnp.exp(-jax.nn.softplus(-w_raw) - 0.5))
    a = jax.nn.sigmoid(lw['rw_a0'] + a_lo @ lw['rw_a2'])
    g = jax.nn.sigmoid(g_lo) @ lw['rw_g2']
    heads = lambda t: t.reshape(B, T, R_HEADS, R_HEAD_DIM)
    kk = heads(k * lw['rw_kk']).astype(jnp.float32)
    kk = kk / jnp.maximum(jnp.sqrt(jnp.sum(kk * kk, axis=-1, keepdims=True)), 1e-12)
    k = k * (1 + (a - 1) * lw['rw_ka'])
    S_new, y = wkv_scan(wkv0, heads(r), heads(decay), heads(k), heads(v), kk, heads(a))
    y = head_group_norm(y, lw['lnx_g'], lw['lnx_b']).astype(h.dtype)
    bonus = jnp.sum(heads(r) * heads(k) * lw['rw_rk'], axis=-1, keepdims=True) * heads(v)
    o_rw = (y + bonus.reshape(B, T, R_WIDTH)) * g
    out = jnp.concatenate([o_attn, o_rw], axis=-1) @ lw['w_out']
    return out, ckv_new, krope_new, S_new, shift_new

def trunk_layer(x, mod, pos, ckv_past, krope_past, wkv0, shift0, lw):
    sh_a, sc_a, gt_a, sh_f, sc_f, gt_f = jnp.split(mod[:, None, :], 6, axis=-1)
    h = rms_norm(x, lw['norm_g'][0]) * (1 + sc_a) + sh_a
    m, ckv_new, krope_new, S_new, shift_new = mixer(h, pos, ckv_past, krope_past, wkv0, shift0, lw)
    x = x + gt_a * rms_norm(m, lw['norm_g'][1])
    h = rms_norm(x, lw['norm_g'][2]) * (1 + sc_f) + sh_f
    f = (jax.nn.silu(h @ lw['w_gate']) * (h @ lw['w_up'])) @ lw['w_down']
    x = x + gt_f * rms_norm(f, lw['norm_g'][3])
    return x, ckv_new, krope_new, S_new, shift_new

def setup_inputs(seed: int = 0) -> dict:
    key = jax.random.key(seed)
    ks = jax.random.split(key, 32)

    def nrm(i, shape, scale=1.0, shift=0.0):
        return shift + scale * jax.random.normal(ks[i], shape, jnp.float32)

    return {
        'x_prompt': nrm(0, (BATCH, SEQ, D_MODEL)),
        'x_sample': nrm(1, (DEC_BATCH, DEC_SEQ, D_MODEL)),
        'c_prompt': nrm(2, (BATCH, D_MODEL)),
        'c_sample': nrm(3, (DEC_BATCH, D_MODEL)),
        'cache_ckv': nrm(4, (DEPTH, DEC_BATCH, PAST_LEN, KV_LORA)),
        'cache_krope': nrm(5, (DEPTH, DEC_BATCH, PAST_LEN, ROPE_DIM)),
        'state_wkv': nrm(6, (DEPTH, DEC_BATCH, R_HEADS, R_HEAD_DIM, R_HEAD_DIM), 0.5),
        'state_shift': nrm(7, (DEPTH, DEC_BATCH, RW_COLS)),
        'ada_w': nrm(8, (DEPTH, D_MODEL, 6 * D_MODEL), 0.5 * D_MODEL ** -0.5),
        'ada_b': nrm(9, (DEPTH, 6 * D_MODEL), 0.01),
        'norm_g': nrm(10, (DEPTH, 4, D_MODEL), 0.05, 1.0),
        'w_in': nrm(11, (DEPTH, D_MODEL, IN_COLS), D_MODEL ** -0.5),
        'q_norm_g': nrm(12, (DEPTH, Q_LORA), 0.05, 1.0),
        'kv_norm_g': nrm(13, (DEPTH, KV_LORA), 0.05, 1.0),
        'w_uq': nrm(14, (DEPTH, Q_LORA, A_HEADS * (NOPE_DIM + ROPE_DIM)), Q_LORA ** -0.5),
        'w_uk': nrm(15, (DEPTH, KV_LORA, A_HEADS, NOPE_DIM), KV_LORA ** -0.5),
        'w_uv': nrm(16, (DEPTH, KV_LORA, A_HEADS, V_DIM), KV_LORA ** -0.5),
        'rw_mu': jax.random.uniform(ks[17], (DEPTH, RW_COLS), jnp.float32),
        'rw_w0': nrm(18, (DEPTH, R_WIDTH), 0.5, -1.0),
        'rw_w2': nrm(19, (DEPTH, DECAY_LORA, R_WIDTH), DECAY_LORA ** -0.5),
        'rw_a0': nrm(20, (DEPTH, R_WIDTH), 0.5),
        'rw_a2': nrm(21, (DEPTH, AAA_LORA, R_WIDTH), AAA_LORA ** -0.5),
        'rw_g2': nrm(22, (DEPTH, GATE_LORA, R_WIDTH), GATE_LORA ** -0.5),
        'rw_kk': nrm(23, (DEPTH, R_WIDTH), 0.05, 0.85),
        'rw_ka': nrm(24, (DEPTH, R_WIDTH), 0.05, 1.0),
        'rw_rk': nrm(25, (DEPTH, R_HEADS, R_HEAD_DIM), 0.1),
        'lnx_g': nrm(26, (DEPTH, R_WIDTH), 0.05, 1.0),
        'lnx_b': nrm(27, (DEPTH, R_WIDTH), 0.01),
        'w_out': nrm(28, (DEPTH, D_MIX, D_MODEL), D_MIX ** -0.5),
        'w_gate': nrm(29, (DEPTH, D_MODEL, D_FF), D_MODEL ** -0.5),
        'w_up': nrm(30, (DEPTH, D_MODEL, D_FF), D_MODEL ** -0.5),
        'w_down': nrm(31, (DEPTH, D_FF, D_MODEL), D_FF ** -0.5),
    }

def reference(x_prompt, x_sample, c_prompt, c_sample, cache_ckv, cache_krope, state_wkv, state_shift,
              ada_w, ada_b, norm_g, w_in, q_norm_g, kv_norm_g, w_uq, w_uk, w_uv,
              rw_mu, rw_w0, rw_w2, rw_a0, rw_a2, rw_g2, rw_kk, rw_ka, rw_rk, lnx_g, lnx_b,
              w_out, w_gate, w_up, w_down):
    xp, xs = x_prompt, x_sample
    Bp, Tp = xp.shape[0], xp.shape[1]
    Ts = xs.shape[1]
    past = cache_ckv.shape[2]
    pos_p = jnp.arange(Tp)
    pos_s = past + jnp.arange(Ts)
    wkv_zero = jnp.zeros((Bp, R_HEADS, R_HEAD_DIM, R_HEAD_DIM), xp.dtype)
    shift_zero = jnp.zeros((Bp, RW_COLS), xp.dtype)
    ckv_p, kr_p, wkv_p, sh_p = [], [], [], []
    ckv_s, kr_s, wkv_s, sh_s = [], [], [], []
    for l in range(DEPTH):
        lw = {'norm_g': norm_g[l], 'w_in': w_in[l], 'q_norm_g': q_norm_g[l], 'kv_norm_g': kv_norm_g[l],
              'w_uq': w_uq[l], 'w_uk': w_uk[l], 'w_uv': w_uv[l], 'rw_mu': rw_mu[l], 'rw_w0': rw_w0[l],
              'rw_w2': rw_w2[l], 'rw_a0': rw_a0[l], 'rw_a2': rw_a2[l], 'rw_g2': rw_g2[l],
              'rw_kk': rw_kk[l], 'rw_ka': rw_ka[l], 'rw_rk': rw_rk[l], 'lnx_g': lnx_g[l],
              'lnx_b': lnx_b[l], 'w_out': w_out[l], 'w_gate': w_gate[l], 'w_up': w_up[l],
              'w_down': w_down[l]}
        mod_p = jax.nn.silu(c_prompt) @ ada_w[l] + ada_b[l]
        mod_s = jax.nn.silu(c_sample) @ ada_w[l] + ada_b[l]
        xp, c1, k1, s1, h1 = trunk_layer(xp, mod_p, pos_p, None, None, wkv_zero, shift_zero, lw)
        xs, c2, k2, s2, h2 = trunk_layer(xs, mod_s, pos_s, cache_ckv[l], cache_krope[l],
                                         state_wkv[l], state_shift[l], lw)
        ckv_p.append(c1); kr_p.append(k1); wkv_p.append(s1); sh_p.append(h1)
        ckv_s.append(c2); kr_s.append(k2); wkv_s.append(s2); sh_s.append(h2)
    ckv_prompt = jnp.stack(ckv_p)
    krope_prompt = jnp.stack(kr_p)
    wkv_prompt = jnp.stack(wkv_p)
    shift_prompt = jnp.stack(sh_p)
    ckv_sample = jnp.stack(ckv_s)
    krope_sample = jnp.stack(kr_s)
    wkv_sample = jnp.stack(wkv_s)
    shift_sample = jnp.stack(sh_s)
    return (xp, xs, ckv_prompt, krope_prompt, wkv_prompt, shift_prompt,
            ckv_sample, krope_sample, wkv_sample, shift_sample)


_drawn_inputs = setup_inputs


def setup_inputs(seed=0):
    import zlib

    import numpy as np

    out = dict(_drawn_inputs(seed))
    spreads = {}
    factors = {'cache_ckv': 3.189,
     'cache_krope': 5.842,
     'q_norm_g': 8.0,
     'rw_kk': 2.926,
     'lnx_g': 4.607,
     'lnx_b': 8.0}
    for name, (base, spread) in spreads.items():
        noise = np.random.default_rng([zlib.crc32(name.encode()), seed]).standard_normal(out[name].shape)
        drawn = base * np.exp(spread * noise) if base else spread * noise
        out[name] = __import__('jax').numpy.asarray(drawn.astype(out[name].dtype))
    for name, factor in factors.items():
        out[name] = (out[name] * factor).astype(out[name].dtype)
    return out
```

```python
from contextlib import ExitStack, contextmanager

import numpy as np

import concourse.bass as bass
from concourse import mybir

F32 = mybir.dt.float32
F32R = mybir.dt.float32r
ALU = mybir.AluOpType
ACT = mybir.ActivationFunctionType
AX_X = mybir.AxisListType.X

P = 128
D = 1024
KD = D // P
TP = 1024
TS = 64
T = TP + TS
PAST = 2048
C = 64
HEADS = 8
PAIRS = HEADS // 2
DH = 64
ROPE = 32
QL, KVL = 384, 256
KQ, KKV = QL // P, KVL // P
RW = 512
KR = RW // P
RW_TILES = 14
MLA_TILES = 6
DFF = 2816
GROUPS = DFF // (2 * P)
TM = T + 1
SAMPLE_COL = TP + 1
KEYS = T + PAST
SCALE = (DH + ROPE) ** -0.5
DECAY = float(np.exp(-0.5))
NEG = -1e30
CH = [(0, 364), (364, 364), (728, 360)]
CM = 363
LEVELS = 6

K_IDENT, K_ONES, K_BLOCK, K_GMASK, K_LEVEL, K_EYE2 = 0, 128, 256, 384, 512, 512 + LEVELS * 64
K_EPS = K_EYE2 + 64
K_CS = K_EPS + 4
K_ALL = K_CS + T
V_NORM, V_QG, V_KVG, V_MU, V_W0, V_A0, V_KK, V_KA, V_RK, V_LG, V_LB = 0, 32, 35, 37, 51, 55, 59, 63, 67, 71, 75
V_ADAB, V_C, V_SHIFT = 79, 127, 143
V_ALL = 157


K_CHUNKS = CH + [(T + 512 * j, 512) for j in range(PAST // 512)]
V_GROUPS = [[0, 1, 2, 3], [4, 5, 6, 7], [8]] + [list(range(9 + 4 * j, 13 + 4 * j)) for j in range(4)]
PJOBS = 2 * (TP // P)
JOBS = PJOBS + 2
QTILES = JOBS // 2
T_PLAN = [[(a, min(a + 4, jb // 2 + 1)) for a in range(0, jb // 2 + 1, 4)] for jb in range(PJOBS)] + 2 * [[(0, 8), (8, 16), (16, 17)]]
T_FIRST = [sum(len(x) for x in T_PLAN[:jb]) for jb in range(JOBS + 1)]
T_GROUPS = T_FIRST[-1]


class Steps:

    def __init__(self, eng, sem):
        self.eng, self.sem, self.base, self.n = eng, sem, 0, 0

    def mark(self, ins):
        ins.then_inc(self.sem, 1)
        self.n += 1

    def wait(self):
        self.eng.wait_ge(self.sem, self.base + self.n)

    def done(self, ins):
        self.mark(ins)
        self.wait()

    @contextmanager
    def loop(self, count, per):
        start = self.base + self.n
        with self.eng.Fori(0, count) as i:
            self.base, self.n = (i * per + start if per else start), 0
            yield i
            assert self.n == per, f"the body makes {self.n} steps, not {per}"
        self.base, self.n = start + count * per, 0


def build(nc, d):
    with ExitStack() as ctx:
        def sem(name):
            return ctx.enter_context(nc.semaphore(name))

        def place(start, *tensors):
            out = []
            for name, shape, *dt in tensors:
                out.append(nc.alloc_sbuf_tensor_at(name, shape, dt[0] if dt else F32, offset=start))
                start += -(-int(np.prod(shape[1:])) * 4 // 32) * 32
            return *out, start

        (con, vec, mod, gains, cs_c, omm, oma, sh_out, sm, rstd, krope, WA) = place(
            17 * 1024,
            ("con", [P, K_ALL]), ("vec", [P, V_ALL]), ("mod", [P, 48, 2]),
            ("gains", [P, 4, 8, 2]),
            ("cs_c", [P, 8, 2]), ("omm", [P, 14]), ("oma", [P, 4]),
            ("sh_out", [P, 14, 2]), ("sm", [P, 3, 2]),
            ("rstd", [P, T]), ("krope", [P, T]))
        tile = [P, KD, P]
        wraw0, wraw1, whi0, whi1, wlo0, wlo1, R1 = place(
            WA, ("wraw0", tile), ("wraw1", tile), ("whi0", tile, F32R), ("whi1", tile, F32R), ("wlo0", tile, F32R), ("wlo1", tile, F32R))
        wraw, whi, wlo = [wraw0, wraw1], [whi0, whi1], [wlo0, wlo1]
        hhi, hlo, R2 = place(R1, ("hhi", [P, KD, T], F32R), ("hlo", [P, KD, T], F32R))
        END = nc.sbuf_usable_end

        sq = [P, 4, 364]
        x1, s0, s1, sl0, sl1, end = place(R2, ("x1", [P, KD, T]), ("sq1_0", sq), ("sq1_1", sq), ("slab0", [P, KD, 512]), ("slab1", [P, KD, 512]))
        sq1, slab = [s0, s1], [sl0, sl1]
        assert end <= END
        cq, ckv, raw0, raw1, mix, end = place(R2, ("cq", [P, KQ, T]), ("ckv", [P, KKV, T]), ("raw0", [P, TM + 1]), ("raw1", [P, TM + 1]),
                                              ("mix", [P, RW_TILES, TM]))
        raw = [raw0, raw1]
        assert end <= END
        RAW_AT = R2 + (KQ + KKV) * T * 4
        MIX_AT = RAW_AT + 2 * (-(-(TM + 1) * 4 // 32) * 32)
        lw, kk, bb, sqr, rn, w2a2, g2, vz, end = place(R1, ("lw", [P, KR, TM]), ("kk", [P, KR, TM]), ("bb", [P, KR, TM]), ("sqr", [P, TM]),
                                                   ("rn", [P, TM]), ("w2a2", [P, RW]), ("g2", [P, RW]),
                                                   ("vz", [P, PAIRS, P]))
        assert end <= R2
        lwf = lw[:, :, :].rearrange("p a b -> p (a b)")
        cum, pinc, pneg, bk, ar, vv, gm, tt, xt, bktm, uv, st, rhs, end = place(
            WA, ("cum", [P, PAIRS, C + 1]), ("pinc", [P, PAIRS, C + 1]), ("pneg", [P, PAIRS, C]), ("bk", [P, PAIRS, 2 * C]),
            ("ar", [P, PAIRS, 2 * C]), ("vv", [P, PAIRS, 2, C]), ("gm", [P, 2, PAIRS, 2 * C]),
            ("tt", [P, 2, PAIRS, C]),
            ("xt", [P, PAIRS, C]), ("bktm", [P, PAIRS, P]), ("uv", [P, PAIRS, P]), ("st", [P, PAIRS, DH]), ("rhs", [P, PAIRS, C]))
        assert end <= R1
        tmp, _ = place(WA + 2 * 1056 + 1024 + 3 * 2048, ("tmp", [P, TM]))
        nlev, end = place(RAW_AT, ("nlev", [P, LEVELS, PAIRS, C]))
        assert end <= MIX_AT
        past, kt0, kt1, qt0, qt1, vt, aw, end = place(
            R1, ("past", [P, KKV, PAST]), ("kt0", [P, KEYS]), ("kt1", [P, KEYS]), ("qt0", [P, T]), ("qt1", [P, T]), ("vt", [P, 25, P]), ("aw", [P, 1280]))
        kt, qt = [kt0, kt1], [qt0, qt1]
        assert end <= R2
        AT = MIX_AT + KR * TM * 4 + 32
        pr0, pr1, pt0, pt1, oatt, rt0, rt1, end = place(
            AT // 32 * 32, ("pr0", [P, TS + PAST]), ("pr1", [P, TS + PAST]), ("pt0", [P, 1088]), ("pt1", [P, 1088]), ("oatt", [P, PAIRS, T]),
            ("rt0", [P, 364]), ("rt1", [P, 364]))
        probs, pt, rtmp = [pr0, pr1], [pt0, pt1], [rt0, rt1]
        sl0, sl1, _ = place(AT // 32 * 32, ("sq_lat0", sq), ("sq_lat1", sq))
        sq_lat = [sl0, sl1]
        assert end <= END
        m1, x2, s0, s1, end = place(R2, ("m1", [P, KD, T]), ("x2", [P, KD, T]), ("sq2_0", sq), ("sq2_1", sq))
        sq2 = [s0, s1]
        assert end <= END
        acc, ahi, alo, draw, dhi0, dhi1, dlo0, dlo1, sil0, sil1, sil2, end = place(
            R2, ("acc", [P, KD, T]), ("ahi", [P, 4, T], F32R), ("alo", [P, 4, T], F32R), ("draw", [P, D]),
            ("dhi0", [P, D], F32R), ("dhi1", [P, D], F32R), ("dlo0", [P, D], F32R), ("dlo1", [P, D], F32R),
            ("sil0", [P, 364]), ("sil1", [P, 364]), ("sil2", [P, 364]))
        dhi, dlo, sil = [dhi0, dhi1], [dlo0, dlo1], [sil0, sil1, sil2]
        assert end <= END
        x3, _ = place(R1, ("x3", [P, KD, T]))
        s0, s1, _ = place(R2 + KD * T * 4, ("sq3_0", sq), ("sq3_1", sq))
        sq3 = [s0, s1]

        ps = ctx.enter_context(nc.psum_tensor("ps", [P, 8, 512], F32))

        ident = con[:, K_IDENT:K_IDENT + P]
        ones = con[:, K_ONES:K_ONES + P]
        block64 = con[:, K_BLOCK:K_BLOCK + P]
        gmask = con[:, K_GMASK:K_GMASK + P]
        eye2 = con[:, K_EYE2:K_EYE2 + C]
        eps_rms = con[:, K_EPS:K_EPS + 1]
        eps_ln = con[:, K_EPS + 1:K_EPS + 2]
        zero = con[:, K_EPS + 2:K_EPS + 3]
        cs = con[:, K_CS:K_CS + T]

        const_in, vec_in = sem("const_in"), sem("vec_in")
        x_in = [sem(f"x_in{c}") for c in range(3)]
        slab_in = [sem(f"slab_in{u}") for u in range(2)]
        silu_c, waited, pool_waited = sem("silu_c"), sem("waited"), sem("pool_waited")
        slab_mm, mod_done = sem("slab_mm"), sem("mod_done")
        gains_done = sem("gains_done")
        w_in_sem = [sem(f"w_loaded{u}") for u in range(2)]
        w_hi, w_lo = sem("w_hi"), sem("w_lo")
        out_ready = [sem(f"out_ready{u}") for u in range(2)]
        bank_free = [sem(f"bank_free{u}") for u in range(2)]
        sq_ready, sq_used = sem("sq_ready"), sem("sq_used")
        root_ready, rstd_ready = sem("root_ready"), sem("rstd_ready")
        xn_ready, affine_done, hi_ready, lo_ready = sem("xn_ready"), sem("affine_done"), sem("hi_ready"), sem("lo_ready")
        v_step, s_step, g_step = sem("vector_step"), sem("scalar_step"), sem("pool_step")
        raw_zero, raw_ready, mix_done = sem("raw_zero"), sem("raw_ready"), sem("mix_done")
        shift_sent = sem("shift_sent")
        lora_in, lora_act, lora_mm, lora_ev = sem("lora_in"), sem("lora_act"), sem("lora_mm"), sem("lora_evicted")
        kk_raw, kk_sq, kk_mm, kk_root, pre_done = sem("kk_raw"), sem("kk_sq"), sem("kk_mm"), sem("kk_root"), sem("pre_done")
        state_in, state_ready = sem("state_in"), sem("state_ready")
        c_cum, c_exp_a, c_exp, c_ab, c_k, c_v = sem("c_cum"), sem("c_exp_a"), sem("c_exp"), sem("c_ab"), sem("c_k"), sem("c_v")
        c_gmm, c_tr, c_gm, c_tm, c_lev = sem("c_gmm"), sem("c_tr"), sem("c_gm"), sem("c_tm"), sem("c_lev")
        c_xmm, c_xev, c_tmm, c_tev = sem("c_xmm"), sem("c_xev"), sem("c_tmm"), sem("c_tev")
        c_rmm, c_rev, c_umm, c_uev, c_ymm, c_yev, c_smm, c_sev = (sem(n) for n in (
            "c_rmm", "c_rev", "c_umm", "c_uev", "c_ymm", "c_yev", "c_smm", "c_sev"))
        c_uvv = sem("c_uvv")
        state_out = sem("state_out")
        p_mm, p_ev, post_step = sem("post_mm"), sem("post_evicted"), sem("post_step")
        rw_done = sem("rw_done")
        qkv_norm = sem("qkv_norm")
        past_in, aw_in = sem("past_in"), sem("aw_in")
        krope_put = sem("krope_put")
        ka_ev, kd_ev, kp_mm = sem("k_even_evicted"), sem("k_odd_evicted"), sem("k_mm")
        qp_mm, qa_ev, qd_ev = sem("q_mm"), sem("q_nope_evicted"), sem("q_rope_evicted")
        vp_mm, v_ev = sem("v_mm"), sem("v_evicted")
        s_mm, nmax, p_exp, p_norm = sem("scores_ready"), sem("negmax_ready"), sem("exp_ready"), sem("probs_ready")
        t_mm, t_ev, o_mm, o_ev = sem("probs_t_ready"), sem("probs_t_evicted"), sem("out_heads_ready"), sem("out_evicted")
        osplit_hi, osplit_lo = sem("osplit_hi"), sem("osplit_lo")
        x2_in, x2_done, x2_out = sem("x2_in"), sem("x2_done"), sem("x2_out")
        acc_zero = sem("acc_zero")
        d_in, d_hi, d_lo, down_ready = sem("d_loaded"), sem("d_hi"), sem("d_lo"), sem("down_ready")
        d_added = sem("down_added")
        sil_ready, act_hi, act_lo, prod_ready = sem("silu_ready"), sem("act_hi"), sem("act_lo"), sem("product_ready")
        krope_copied = sem("krope_copied")
        x3_in, y_done, stored = sem("x3_in"), sem("y_done"), sem("stored")

        def start_at_one(eng, *sems):
            for x in sems:
                eng.sem_inc(x, 1)

        OUT_M = (MLA_TILES + RW_TILES) // 2
        FF_M = OUT_M + KD // 2
        A_TILES = 2 * FF_M + 4 * GROUPS

        def segments(c):
            a, n = CH[c]
            b = a + n
            return [(a, n, 0)] if b <= TP else [(a, TP - a, 0), (TP, b - TP, 1)]

        def o_parts(h):
            return [(h[:, 0:KR, :], oatt[:, :, :]), (h[:, KR:KD, 0:TP], mix[:, 0:KR, 0:TP]), (h[:, KR:KD, TP:T], mix[:, 0:KR, SAMPLE_COL:TM])]

        def load_weight(eng, m, u, first=False):
            if not first:
                eng.wait_ge(w_lo, 2 * m + u - 1)
            eng.dma_start(wraw[u][:, :, :].rearrange("p a b -> p (a b)"), d["w_tiles"][2 * m + u, :, :]).then_inc(w_in_sem[u], 16)

        def split_hi(act, m, u, first=False):
            act.wait_ge(w_in_sem[u], 16 * (m + 1))
            if not first:
                act.wait_ge(out_ready[u], 3 * m)
            nc.scalar.copy(whi[u][:, :, :], wraw[u][:, :, :]).then_inc(w_hi, 1)

        def split_lo(dve, m, u):
            dve.wait_ge(w_hi, 2 * m + u + 1)
            nc.vector.tensor_tensor(wlo[u][:, :, :], wraw[u][:, :, :], whi[u][:, :, :].bitcast(F32), ALU.subtract).then_inc(w_lo, 1)

        def project(pe, m, u, first=False):
            pe.wait_ge(w_lo, 2 * m + u + 1)
            for c, (a, n) in enumerate(CH):
                if not first:
                    pe.wait_ge(bank_free[u], 3 * (m - 1) + c + 1)
                out = ps[:, 3 * u + c, 0:n]
                for k in range(KD):
                    for w, x in ((whi, hhi), (whi, hlo), (wlo, hhi)):
                        mm = nc.tensor.matmul(out, w[u][:, k, :], x[:, k, a:a + n],
                                              start=(k == 0 and w is whi and x is hhi), stop=(k == KD - 1 and w is wlo))
                mm.then_inc(out_ready[u], 1)

        NORMS = {"n1": (KD, D), "q": (KQ, QL), "kv": (KKV, KVL), "m": (KD, D), "n2": (KD, D), "f": (KD, D)}
        pieces, first_piece, chunk_no = 0, {}, {}
        for r, (name, (k, _)) in enumerate(NORMS.items()):
            chunk_no[name] = 3 * r
            first_piece[name] = pieces
            pieces += 3 * (-(-k // 4))

        def norm_squares(act, name, src, sqbuf, c):
            k = NORMS[name][0]
            per = -(-k // 4)
            a, n = CH[c]
            for j in range(per):
                piece = first_piece[name] + c * per + j
                k0, k1 = 4 * j, min(4 * j + 4, k)
                if piece >= 2:
                    act.wait_ge(sq_used, piece - 1)
                nc.scalar.activation(sqbuf[piece % 2][:, 0:k1 - k0, 0:n], src[:, k0:k1, a:a + n], ACT.Square).then_inc(sq_ready, 1)

        def norm_sum(pe, name, sqbuf, c):
            k = NORMS[name][0]
            per = -(-k // 4)
            a, n = CH[c]
            q = chunk_no[name] + c
            if q >= 2:
                pe.wait_ge(root_ready, q - 1)
            for j in range(per):
                piece = first_piece[name] + c * per + j
                pe.wait_ge(sq_ready, piece + 1)
                for i in range(4 * j, min(4 * j + 4, k)):
                    mm = nc.tensor.matmul(ps[:, 6 + q % 2, 0:n], ones, sqbuf[piece % 2][:, i - 4 * j, 0:n], start=(i == 0), stop=(i == k - 1))
                mm.then_inc(sq_used, 1)

        def norm_root(act, name, c):
            k, width = NORMS[name]
            per = -(-k // 4)
            a, n = CH[c]
            q = chunk_no[name] + c
            act.wait_ge(sq_used, first_piece[name] + (c + 1) * per)
            used = {"q": (xn_ready, c + 1), "kv": (qkv_norm, c + 1), "m": (qkv_norm, c + 4), "n2": (x2_done, c + 1), "f": (xn_ready, c + 4)}
            if name in used:
                act.wait_ge(*used[name])
            nc.scalar.activation(rstd[:, a:a + n], ps[:, 6 + q % 2, 0:n], ACT.Sqrt, bias=eps_rms, scale=1.0 / width).then_inc(root_ready, 1)

        def norm_recip(dve, name, c):
            a, n = CH[c]
            q = chunk_no[name] + c
            dve.wait_ge(root_ready, q + 1)
            nc.vector.reciprocal(rstd[:, a:a + n], rstd[:, a:a + n]).then_inc(rstd_ready, 1)
            dve.wait_ge(rstd_ready, q + 1)

        def over_tiles(ap2, k):
            return ap2.unsqueeze(1).broadcast_to([P, k, ap2.shape[1]])

        block = ctx.enter_context(nc.Block())

        @block.sync
        def _(sp):
            sp.dma_start(con[:, :], d["table"]).then_inc(const_in, 16)
            sp.dma_start(vec[:, :], d["vectors"]).then_inc(vec_in, 16)
            for c, (a, n) in enumerate(CH):
                sp.dma_start(x1[:, :, a:a + n], d["x_t"].rearrange("(k p) t -> p k t", p=P)[:, :, a:a + n]).then_inc(x_in[c], 16)
            load_weight(sp, 0, 0, first=True)
            load_weight(sp, 0, 1, first=True)
            ada = d["ada_w"].rearrange("(k p) n -> p k n", p=P)
            for u in range(2):
                sp.dma_start(slab[u][:, :, :], ada[:, :, 512 * u:512 * u + 512]).then_inc(slab_in[u], 16)
            with sp.Fori(1, 6) as i:
                for u in range(2):
                    sp.wait_ge(slab_mm, 2 * i + u - 1)
                    sp.dma_start(slab[u][:, :, :], ada[:, :, bass.ds(1024 * i + 512 * u, 512)]).then_inc(slab_in[u], 16)
            with sp.Fori(1, OUT_M) as m:
                for u in range(2):
                    load_weight(sp, m, u)
            sp.wait_ge(raw_ready, RW_TILES)
            sp.dma_start(d["shift"], sh_out[:, :, :].rearrange("p a b -> p (a b)")).then_inc(stored, 16)
            for u in range(2):
                sp.wait_ge(out_ready[u], 3 * OUT_M)
            sp.dma_start(w2a2[:, :], d["w2a2"]).then_inc(lora_in, 16)
            sp.dma_start(g2[:, :], d["g2"]).then_inc(lora_in, 16)
            sp.wait_ge(c_sev, TP // C + 1)
            sp.dma_start(d["wkv"][0, :, :], st[:, :, :].rearrange("p a b -> p (a b)")).then_inc(state_out, 16)
            sp.wait_ge(state_out, 16)
            sp.dma_start(st[:, :, :].rearrange("p a b -> p (a b)"), d["state0"]).then_inc(state_in, 16)
            sp.wait_ge(c_sev, TP // C + 1 + 1)
            sp.dma_start(d["wkv"][1, :, :], st[:, :, :].rearrange("p a b -> p (a b)")).then_inc(state_out, 16)
            sp.wait_ge(rw_done, KR)
            sp.dma_start(past[:, :, :], d["ckv_t"].rearrange("(k p) t -> p k t", p=P)).then_inc(past_in, 16)
            for e in range(2):
                sp.dma_start(kt[e][64:96, T:KEYS], d["krope_t"]).then_inc(past_in, 16)
            sp.dma_start(aw[:, :], d["att_w"][0, :, :]).then_inc(aw_in, 16)
            sp.wait_ge(qkv_norm, 6)
            sp.dma_start(d["ckv_out"].rearrange("(k p) t -> p k t", p=P), ckv[:, :, :]).then_inc(stored, 16)
            sp.dma_start(d["krope_out"], krope[64:96, :]).then_inc(stored, 16)
            sp.wait_ge(state_out, 32)
            for u in range(2):
                load_weight(sp, OUT_M, u)
            with sp.Fori(1, PAIRS) as hp:
                sp.wait_ge(vp_mm, 7 * hp)
                sp.dma_start(aw[:, :], d["att_w"][hp, :, :]).then_inc(aw_in, 16)
            sp.wait_ge(osplit_lo, 3)
            for c, (a, n) in enumerate(CH):
                sp.dma_start(x2[:, :, a:a + n], d["x_t"].rearrange("(k p) t -> p k t", p=P)[:, :, a:a + n]).then_inc(x2_in, 16)
            with sp.Fori(OUT_M + 1, FF_M) as m:
                for u in range(2):
                    load_weight(sp, m, u)
            for u in range(2):
                load_weight(sp, FF_M, u)
            for c, (a, n) in enumerate(CH):
                sp.wait_ge(x2_done, c + 1)
                sp.dma_start(d["x_mid"].rearrange("(k p) t -> p k t", p=P)[:, :, a:a + n], x2[:, :, a:a + n]).then_inc(x2_out, 16)
            sp.wait_ge(sq_used, first_piece["n2"] + 6)
            def load_down(g, u, first=False):
                if not first:
                    sp.wait_ge(d_lo, 2 * g + u)
                sp.dma_start(draw[:, :], d["w_down"][bass.ds((2 * g + u) * P, P), :]).then_inc(d_in, 16)

            load_weight(sp, FF_M + 1, 0)
            load_weight(sp, FF_M + 1, 1)
            load_down(0, 0, first=True)
            with sp.Fori(1, GROUPS) as g:
                for j in range(2):
                    for u in range(2):
                        load_weight(sp, 2 * g + FF_M + j, u)
                load_down(g - 1, 1)
                load_down(g, 0)
            load_down(GROUPS - 1, 1)
            for u in range(2):
                sp.wait_ge(out_ready[u], 3 * (FF_M + 2 * GROUPS))
            sp.wait_ge(x2_out, 48)
            sp.dma_start(x3[:, :, :], d["x_mid"].rearrange("(k p) t -> p k t", p=P)).then_inc(x3_in, 16)
            for c, (a, n) in enumerate(CH):
                sp.wait_ge(y_done, c + 1)
                sp.dma_start(d["y"].rearrange("(k p) t -> p k t", p=P)[:, :, a:a + n], x3[:, :, a:a + n]).then_inc(stored, 16)
            sp.wait_ge(stored, 16 * 6)
            sp.wait_ge(state_out, 32)

        @block.gpsimd
        def _(pool):
            step = Steps(pool, g_step)
            start_at_one(pool, c_k, c_lev)
            pool.wait_ge(lo_ready, 3)
            for u in range(2):
                nc.gpsimd.memset(raw[u][:, 0:1], 0.0).then_inc(raw_zero, 1)
            for u in range(2):
                pool.wait_ge(out_ready[u], 3 * OUT_M)
            nc.gpsimd.memset(st[:, :, :], 0.0).then_inc(state_ready, 1)
            nc.gpsimd.memset(vz[:, :, :], 0.0).then_inc(state_ready, 1)
            nc.gpsimd.memset(cum[:, :, 0:1], 0.0).then_inc(state_ready, 1)

            def keys_and_levels(i, col):
                pool.wait_ge(c_exp, i + 1 + 1)
                pool.wait_ge(c_tr, i + 1)
                pool.wait_ge(pre_done, KR)
                for e in range(2):
                    r = slice(64 * e, 64 * e + 64)
                    k_half = bk[r, :, C * (1 - e):C * (1 - e) + C]
                    nc.gpsimd.tensor_tensor(k_half, mix[r, KR:2 * KR, bass.ds(col, C)], pneg[r, :, :], ALU.mult).then_inc(c_k, 1)
                pool.wait_ge(c_gm, 2 * i + 2 + 1)
                pool.wait_ge(c_xmm, LEVELS * i + 1)
                for e in range(2):
                    r = slice(64 * e, 64 * e + 64)
                    g = gm[r, e, :, 0:C].unsqueeze(1).broadcast_to([64, LEVELS, PAIRS, C])
                    lv = con[r, K_LEVEL:K_LEVEL + LEVELS * C].rearrange("p (l t) -> p l t", l=LEVELS)
                    for l in range(LEVELS):
                        nc.gpsimd.tensor_tensor(nlev[r, l, :, :], gm[r, e, :, 0:C],
                                                lv[:, l, :].unsqueeze(1).broadcast_to([64, PAIRS, C]), ALU.mult).then_inc(c_lev, 1)

                pool.wait_ge(c_tm, i + 1 + 1)
                pool.wait_ge(c_ymm, i + 1)
                pool.sem_inc(pool_waited, 1)
                nc.gpsimd.tensor_copy(uv[0:64, :, 64:128], vz[0:64, :, 64:128]).then_inc(c_uvv, 1)
                nc.gpsimd.tensor_copy(uv[64:128, :, 0:64], vz[64:128, :, 0:64]).then_inc(c_uvv, 1)

            with pool.Fori(0, TP // C) as i:
                keys_and_levels(i, i * C)
            keys_and_levels(TP // C, SAMPLE_COL)
            pool.wait_ge(hi_ready, 6)
            pool.wait_ge(lo_ready, 6)
            nc.gpsimd.memset(acc[:, :, :], 0.0).then_inc(acc_zero, 1)

        @block.scalar
        def _(act):
            step = Steps(act, s_step)
            start_at_one(act, c_exp, c_tm, c_yev)
            act.wait_ge(vec_in, 16)
            nc.scalar.activation(cs_c[:, :, :].rearrange("p a b -> p (a b)"), vec[:, V_C:V_C + 16], ACT.Silu).then_inc(silu_c, 1)
            act.wait_ge(const_in, 16)
            for c in range(3):
                act.wait_ge(x_in[c], 16)
                norm_squares(act, "n1", x1, sq1, c)
                norm_root(act, "n1", c)

            def affine_split(src, c, gain, shift, count):
                act.wait_ge(xn_ready, count + 1)
                a, n = CH[c]
                for k in range(KD):
                    for b, w, s in segments(c):
                        step.mark(nc.scalar.activation(src[:, k, b:b + w], src[:, k, b:b + w], ACT.Identity,
                                                       bias=mod[:, shift + k, s:s + 1], scale=gains[:, gain, k, s:s + 1]))
                step.wait()
                nc.scalar.copy(hhi[:, :, a:a + n], src[:, :, a:a + n]).then_inc(hi_ready, 1)

            act.wait_ge(gains_done, 4)
            act.wait_ge(mod_done, 12)
            for c in range(3):
                affine_split(x1, c, 0, 0, c)

            def put_chunks(u, m, place):
                for c in range(3):
                    act.wait_ge(out_ready[u], 3 * m + c + 1)
                    parts = place(c)
                    for j, (dst, a, n) in enumerate(parts):
                        ins = nc.scalar.copy(dst, ps[:, 3 * u + c, a:a + n])
                        if j == len(parts) - 1:
                            ins.then_inc(bank_free[u], 1)
                        else:
                            step.mark(ins)

            split_hi(act, 0, 0, first=True)
            split_hi(act, 0, 1, first=True)
            act.wait_ge(lo_ready, 3)
            act.wait_ge(mod_done, 12)
            for n in range(MLA_TILES):
                m, u = n // 2, n % 2
                if n < KQ:
                    put_chunks(u, m, lambda c: [(cq[:, n, CH[c][0]:CH[c][0] + CH[c][1]], 0, CH[c][1])])
                elif n < KQ + KKV:
                    put_chunks(u, m, lambda c: [(ckv[:, n - KQ, CH[c][0]:CH[c][0] + CH[c][1]], 0, CH[c][1])])
                else:
                    put_chunks(u, m, lambda c: [(mix[:, 12, CH[c][0]:CH[c][0] + CH[c][1]], 0, CH[c][1])])
                split_hi(act, m + 1, u)

            def raw_place(u):
                def place(c):
                    a, n = CH[c]
                    if c < 2:
                        return [(raw[u][:, 1 + a:1 + a + n], 0, n)]
                    return [(raw[u][:, 1 + a:1 + TP], 0, TP - a), (raw[u][:, TM + 1 - TS:TM + 1], TP - a, TS)]
                return place

            def raw_rows(m, j, u, first=False):
                if not first:
                    act.wait_ge(mix_done, j - 1)
                step.mark(nc.scalar.copy(raw[u][:, TP + 1:TP + 2], vec[:, bass.ds(j + V_SHIFT, 1)]))
                put_chunks(u, m, raw_place(u))
                step.wait()
                act.wait_ge(bank_free[u], 3 * m + 3)
                step.mark(nc.scalar.copy(sh_out[:, bass.ds(j, 1), :].rearrange("p a b -> p (a b)"), raw[u][:, TP:TM + 1:TM - TP]))
                nc.scalar.mul(mix[:, bass.ds(j, 1), :].rearrange("p a b -> p (a b)"), raw[u][:, 0:TM],
                              vec[:, bass.ds(j + V_MU, 1)]).then_inc(raw_ready, 1)

            act.wait_ge(raw_zero, 2)
            act.wait_ge(mod_done, 12)
            RM = MLA_TILES // 2
            for u in range(2):
                raw_rows(RM, u, u, first=True)
                split_hi(act, RM + 1, u)
            with step.loop(RW_TILES // 2 - 2, 6) as i:
                for u in range(2):
                    raw_rows(i + RM + 1, 2 * i + 2 + u, u)
                    split_hi(act, i + RM + 2, u)
            for u in range(2):
                raw_rows(OUT_M - 1, RW_TILES - 2 + u, u)

            act.wait_ge(mix_done, RW_TILES)
            nc.scalar.activation(mix[0:64, 12, :], mix[0:64, 12, :], ACT.Tanh).then_inc(lora_act, 1)
            nc.scalar.activation(mix[:, 13, :], mix[:, 13, :], ACT.Sigmoid).then_inc(lora_act, 1)
            for j in range(KR):
                for s, (dst, vcol) in enumerate(((lw, V_W0), (bb, V_A0))):
                    act.wait_ge(lora_mm, 2 * j + s + 1)
                    nc.scalar.activation(dst[:, j, :].rearrange("p (c n) -> p c n", c=3), ps[:, 3 * s:3 * s + 3, 0:CM], ACT.Sigmoid,
                                         bias=vec[:, vcol + j:vcol + j + 1]).then_inc(lora_ev, 1)
            for j in range(KR):
                act.wait_ge(kk_raw, j + 1)
                if j:
                    act.wait_ge(kk_mm, j)
                nc.scalar.activation(sqr[:, :], kk[:, j, :], ACT.Square).then_inc(kk_sq, 1)
                act.wait_ge(kk_mm, j + 1)
                if j:
                    act.wait_ge(pre_done, j)
                nc.scalar.activation(rn[:, :].rearrange("p (c n) -> p c n", c=3), ps[:, 3 * (j % 2):3 * (j % 2) + 3, 0:CM], ACT.Sqrt).then_inc(kk_root, 1)

            def chunk_scalar(i, col):
                act.wait_ge(c_cum, i + 1)
                act.wait_ge(c_k, 2 * i + 1)
                act.wait_ge(c_sev, i + 1)
                nc.scalar.activation(pinc[:, :, :], cum[:, :, :], ACT.Exp, scale=-DECAY).then_inc(c_exp_a, 1)
                nc.scalar.activation(pneg[:, :, :], cum[:, :, 1:C + 1], ACT.Exp, scale=DECAY).then_inc(c_exp, 1)
                act.wait_ge(c_tr, i + 1)
                step.mark(nc.scalar.copy(vv[:, :, 0, :], mix[:, 2 * KR:3 * KR, bass.ds(col, C)]))
                nc.scalar.copy(vv[:, :, 1, :], mix[:, 2 * KR:3 * KR, bass.ds(col, C)]).then_inc(c_v, 1)
                step.wait()
                act.wait_ge(c_tr, i + 1 + 1)
                act.wait_ge(c_smm, i + 1)
                step.mark(nc.scalar.copy(bktm[:, :, :].rearrange("p a b -> p (a b)"), ps[:, 2, :]))
                v3 = ps[:, 3, :].rearrange("p (a b) -> p a b", a=PAIRS)
                step.mark(nc.scalar.copy(vz[0:64, :, 64:128], v3[0:64, :, 64:128]))
                nc.scalar.copy(vz[64:128, :, 0:64], v3[64:128, :, 0:64]).then_inc(c_tm, 1)
                for l in range(LEVELS - 1):
                    act.wait_ge(c_xmm, LEVELS * i + l + 2 + 1)
                    act.wait_ge(c_tmm, (LEVELS - 1) * i + l + 1)
                    nc.scalar.copy(xt[:, :, :].rearrange("p a b -> p (a b)"), ps[:, 4, 0:PAIRS * C]).then_inc(c_xev, 1)
                act.wait_ge(c_rmm, i + 1)
                nc.scalar.mul(rhs[:, :, :].rearrange("p a b -> p (a b)"), ps[:, 6, 0:PAIRS * C], -1.0).then_inc(c_rev, 1)
                act.wait_ge(c_umm, i + 1 + 1)
                u3 = ps[:, 7, 0:PAIRS * DH].rearrange("p (a b) -> p a b", a=PAIRS)
                act.wait_ge(c_ymm, i + 1)
                step.mark(nc.scalar.copy(uv[0:64, :, 0:64], u3[0:64, :, :]))
                nc.scalar.copy(uv[64:128, :, 64:128], u3[64:128, :, :]).then_inc(c_uev, 1)
                step.wait()
                act.wait_ge(c_ymm, i + 1 + 1)
                nc.scalar.copy(lw[:, :, bass.ds(col, C)], ps[:, 7, 0:PAIRS * C].rearrange("p (a b) -> p a b", a=PAIRS)).then_inc(c_yev, 1)

            with step.loop(TP // C, 4) as i:
                chunk_scalar(i, i * C)
            chunk_scalar(TP // C, SAMPLE_COL)

            act.wait_ge(c_yev, TP // C + 1 + 1)
            for j in range(KR):
                b0 = 4 * j
                act.wait_ge(post_step, b0 + 1)
                nc.scalar.activation(sqr[:, :], lw[:, j, :], ACT.Square).then_inc(p_ev, 1)
                act.wait_ge(p_mm, b0 + 2)
                nc.scalar.activation(rn[:, :].rearrange("p (c n) -> p c n", c=3), ps[:, 3:6, 0:CM], ACT.Sqrt, bias=eps_ln, scale=1.0 / DH).then_inc(p_ev, 1)
                act.wait_ge(post_step, b0 + 2)
                nc.scalar.activation(lw[:, j, :], lw[:, j, :], ACT.Identity, bias=vec[:, V_LB + j:V_LB + j + 1],
                                     scale=vec[:, V_LG + j:V_LG + j + 1]).then_inc(p_ev, 1)

            for name, src in (("q", cq), ("kv", ckv)):
                for c in range(3):
                    if name == "q" and c == 0:
                        act.wait_ge(rw_done, KR)
                    norm_squares(act, name, src, sq_lat, c)
                    norm_root(act, name, c)

            act.wait_ge(past_in, 48)
            act.wait_ge(krope_put, 1)
            for e in range(2):
                nc.scalar.copy(kt[e][64:96, 0:T], krope[64:96, :]).then_inc(krope_copied, 1)

            split_hi(act, OUT_M, 0)
            split_hi(act, OUT_M, 1)

            def attend_scalar(hp):
                for l, (dst, n) in enumerate(K_CHUNKS):
                    act.wait_ge(kp_mm, 7 * hp + l + 1)
                    nc.scalar.copy(kt[0][0:64, dst:dst + n], ps[0:64, l % 4, 0:n]).then_inc(ka_ev, 1)
                for e in range(2):
                    for c, (a, n) in enumerate(CH):
                        l = 3 * e + c
                        act.wait_ge(qp_mm, 6 * hp + l + 1)
                        nc.scalar.mul(qt[e][0:64, a:a + n], ps[0:64, 4 + l % 4, 0:n], SCALE).then_inc(qa_ev, 1)
                for g, tiles in enumerate(V_GROUPS):
                    act.wait_ge(vp_mm, 7 * hp + g + 1)
                    rows = TS if tiles == [8] else P
                    nc.scalar.copy(vt[0:rows, tiles[0]:tiles[-1] + 1, :],
                                   ps[0:rows, (7 + g) % 4, 0:P * len(tiles)].rearrange("p (a b) -> p a b", b=P)).then_inc(v_ev, 1)
                for jb in range(PJOBS):
                    exponentials(jb, hp)
                    if jb:
                        put_probs(jb - 1, hp)
                put_probs(PJOBS - 1, hp)
                for jb in range(PJOBS, JOBS):
                    exponentials(jb, hp)
                    put_probs(jb, hp)

            def exponentials(jb, hp):
                u = jb % 2
                act.wait_ge(nmax, JOBS * hp + jb + 1)
                act.wait_ge(t_mm, T_GROUPS * hp + (T_FIRST[jb - 1] if jb >= 2 else 0) + 1)
                if jb < PJOBS:
                    n = P * (jb // 2 + 1)
                    dst, src, r = probs[u][:, 0:n], ps[:, 2 * u:2 * u + 2, :].rearrange("p a b -> p (a b)")[:, 0:n], slice(0, P)
                else:
                    dst, src, r = probs[u][0:TS, :].rearrange("p (a b) -> p a b", a=6), ps[0:TS, 0:6, 0:352], slice(0, TS)
                nc.scalar.activation(dst, src, ACT.Exp, bias=sm[r, 0, u:u + 1], accum_out=sm[r, 1, u:u + 1]).then_inc(p_exp, 1)

            def put_probs(jb, hp):
                u = jb % 2
                act.wait_ge(o_mm, JOBS * hp + max(jb - 1, 0) + 1)
                for g, (t0, t1) in enumerate(T_PLAN[jb]):
                    act.wait_ge(t_mm, T_GROUPS * hp + T_FIRST[jb] + g + 1 + 1)
                    w = P if jb < PJOBS else TS
                    bank = 4 + (T_FIRST[jb] + g) % 2
                    if jb >= PJOBS and g == 0:
                        step.mark(nc.scalar.copy(pt[u][0:TS, 0:w], ps[0:TS, bank, 0:w]))
                        nc.scalar.copy(pt[u][:, w:t1 * w], ps[:, bank, w:t1 * w]).then_inc(t_ev, 1)
                    else:
                        nc.scalar.copy(pt[u][:, t0 * w:t1 * w], ps[:, bank, 0:(t1 - t0) * w]).then_inc(t_ev, 1)

            with step.loop(PAIRS, 2) as hp:
                attend_scalar(hp)

            act.wait_ge(o_ev, QTILES * PAIRS + 1)
            for dst, src in o_parts(hhi):
                nc.scalar.copy(dst, src).then_inc(osplit_hi, 1)

            act.wait_ge(osplit_lo, 3)
            for n in range(KD):
                m, u = OUT_M + n // 2, n % 2
                put_chunks(u, m, lambda c: [(m1[:, n, CH[c][0]:CH[c][0] + CH[c][1]], 0, CH[c][1])])
                split_hi(act, m + 1, u)
            for u in range(2):
                act.wait_ge(bank_free[u], 3 * FF_M)
            for c in range(3):
                norm_squares(act, "m", m1, sq2, c)
                norm_root(act, "m", c)
            for c in range(3):
                act.wait_ge(x2_done, c + 1)
                norm_squares(act, "n2", x2, sq2, c)
                norm_root(act, "n2", c)
            for c in range(3):
                affine_split(m1, c, 2, 24, 3 + c)

            def down_hi(g, u):
                act.wait_ge(d_in, 16 * (2 * g + u + 1))
                act.wait_ge(down_ready, 24 * g + 1)
                nc.scalar.copy(dhi[u][:, :], draw[:, :]).then_inc(d_hi, 1)

            def gate(g, slot, j, first=False, last=False):
                m = 2 * g + FF_M + j
                q = 6 * g + 3 * j
                for c, (a, n) in enumerate(CH):
                    act.wait_ge(out_ready[0], 3 * m + c + 1)
                    if not (first and j == 0):
                        act.wait_ge(act_lo, q + c - 2)
                    nc.scalar.activation(sil[c][:, 0:n], ps[:, c, 0:n], ACT.Silu).then_inc(sil_ready, 1)
                if not last:
                    split_hi(act, m + 1, 0)
                if not first:
                    act.wait_ge(down_ready, 24 * (g - 1) + 1)
                for c, (a, n) in enumerate(CH):
                    act.wait_ge(prod_ready, q + c + 1)
                    nc.scalar.copy(ahi[:, slot + j, a:a + n], sil[c][:, 0:n]).then_inc(act_hi, 1)
                if not last:
                    split_hi(act, m + 1, 1)

            act.wait_ge(x2_out, 48)
            gate(0, 0, 0, first=True)
            gate(0, 0, 1, first=True)

            def group(g, slot, last=False):
                gate(g, slot, 0)
                down_hi(g - 1, 0)
                down_hi(g - 1, 1)
                gate(g, slot, 1, last=last)

            with act.Fori(0, (GROUPS - 3) // 2) as it:
                group(2 * it + 1, 2)
                group(2 * it + 2, 0)
            group(GROUPS - 2, 2)
            group(GROUPS - 1, 0, last=True)
            down_hi(GROUPS - 1, 0)
            down_hi(GROUPS - 1, 1)

            act.wait_ge(d_added, 24 * GROUPS + 1)
            for c in range(3):
                norm_squares(act, "f", acc, sq3, c)
                norm_root(act, "f", c)

        @block.vector
        def _(dve):
            step = Steps(dve, v_step)
            start_at_one(dve, c_gm, c_sev, o_ev, qd_ev, d_added)
            dve.wait_ge(vec_in, 16)
            dve.wait_ge(const_in, 16)
            step.mark(nc.vector.tensor_scalar(omm[:, :], vec[:, V_MU:V_MU + 14], -1.0, 1.0, ALU.mult, ALU.add))
            step.mark(nc.vector.tensor_scalar(oma[:, :], vec[:, V_KA:V_KA + 4], -1.0, 1.0, ALU.mult, ALU.add))

            def times_rstd(dst, src, c):
                a, n = CH[c]
                nc.vector.tensor_tensor(dst[:, :, a:a + n], src[:, :, a:a + n], over_tiles(rstd[:, a:a + n], KD), ALU.mult).then_inc(xn_ready, 1)

            def rest(src, c, count):
                a, n = CH[c]
                dve.wait_ge(hi_ready, count + 1)
                nc.vector.tensor_tensor(hlo[:, :, a:a + n], src[:, :, a:a + n], hhi[:, :, a:a + n].bitcast(F32), ALU.subtract).then_inc(lo_ready, 1)

            for c in range(3):
                norm_recip(dve, "n1", c)
                dve.wait_ge(x_in[c], 16)
                times_rstd(x1, x1, c)

            def modulation(i, u):
                dve.wait_ge(slab_mm, 2 * i + u + 1)
                bias = vec[:, bass.ds(8 * i + (V_ADAB + 4 * u), 4)].unsqueeze(2).broadcast_to([P, 4, 2])
                nc.vector.tensor_tensor(mod[:, bass.ds(8 * i + 4 * u, 4), :], ps[:, u, 0:8].rearrange("p (a b) -> p a b", b=2),
                                        bias, ALU.add).then_inc(mod_done, 1)

            with dve.Fori(0, 6) as i:
                for u in range(2):
                    modulation(i, u)
            dve.wait_ge(mod_done, 12)

            def gain(which, at0, plus, last=False):
                g = vec[:, V_NORM + 8 * which:V_NORM + 8 * which + 8].unsqueeze(2).broadcast_to([P, 8, 2])
                ins = nc.vector.scalar_tensor_tensor(out=gains[:, which, :, :], in0=mod[:, at0:at0 + 8, :], scalar=plus, in1=g,
                                                     op0=ALU.add, op1=ALU.mult)
                ins.then_inc(gains_done, 1)

            gain(0, 8, 1.0)
            gain(1, 16, 0.0)
            gain(2, 32, 1.0)
            gain(3, 40, 0.0)
            split_lo(dve, 0, 0)
            split_lo(dve, 0, 1)
            for c in range(3):
                rest(x1, c, c)

            for n in range(MLA_TILES):
                m, u = n // 2, n % 2
                split_lo(dve, m + 1, u)
                if n == MLA_TILES - 1:
                    dve.wait_ge(bank_free[u], 3 * m + 3)
                    step.mark(nc.vector.tensor_tensor(krope[64:96, :], mix[64:96, 12, 0:T], cs[64:96, :], ALU.mult))
                    step.done(nc.vector.tensor_tensor(mix[64:96, 13, 0:T], mix[96:128, 12, 0:T], cs[96:128, :], ALU.mult))
                    nc.vector.tensor_tensor(krope[64:96, :], krope[64:96, :], mix[64:96, 13, 0:T], ALU.add).then_inc(krope_put, 1)
                    dve.wait_ge(krope_put, 1)

            def shift_mix(j, u):
                dve.wait_ge(raw_ready, j + 1)
                m2 = mix[:, bass.ds(j, 1), :].rearrange("p a b -> p (a b)")
                nc.vector.scalar_tensor_tensor(out=m2, in0=raw[u][:, 1:TM + 1], scalar=omm[:, bass.ds(j, 1)], in1=m2,
                                               op0=ALU.mult, op1=ALU.add).then_inc(mix_done, 1)

            step.wait()
            for u in range(2):
                split_lo(dve, MLA_TILES // 2 + 1, u)
                shift_mix(u, u)
            with dve.Fori(0, RW_TILES // 2 - 2) as i:
                for u in range(2):
                    split_lo(dve, i + MLA_TILES // 2 + 2, u)
                    shift_mix(2 * i + 2 + u, u)
            for u in range(2):
                shift_mix(RW_TILES - 2 + u, u)

            dve.wait_ge(mix_done, RW_TILES)
            for u in range(2):
                dve.wait_ge(out_ready[u], 3 * OUT_M)
            for j in range(KR):
                nc.vector.tensor_scalar(kk[:, j, :], mix[:, KR + j, :], vec[:, V_KK + j:V_KK + j + 1], None, ALU.mult).then_inc(kk_raw, 1)
                dve.wait_ge(lora_ev, 2 * j + 2)
                step.done(nc.vector.tensor_scalar(tmp[:, :], bb[:, j, :], vec[:, V_KA + j:V_KA + j + 1], oma[:, j:j + 1], ALU.mult, ALU.add))
                step.mark(nc.vector.tensor_tensor(mix[:, KR + j, :], mix[:, KR + j, :], tmp[:, :], ALU.mult))
                dve.wait_ge(kk_root, j + 1)
                step.done(nc.vector.tensor_scalar(rn[:, :], rn[:, :], 1e-12, None, ALU.max))
                step.done(nc.vector.reciprocal(rn[:, :], rn[:, :]))
                dve.wait_ge(kk_sq, j + 1)
                step.done(nc.vector.tensor_tensor(kk[:, j, :], kk[:, j, :], rn[:, :], ALU.mult))
                nc.vector.tensor_tensor(bb[:, j, :], bb[:, j, :], kk[:, j, :], ALU.mult).then_inc(pre_done, 1)
            dve.wait_ge(pre_done, KR)

            def chunk_vector(i, col):
                dve.wait_ge(c_exp, i + 1)
                for p in range(PAIRS):
                    ins = nc.vector.tensor_tensor_scan(cum[:, p, 1:C + 1], ones[:, 0:C], lwf[:, bass.ds(col + p * TM, C)],
                                                       0.0, ALU.mult, ALU.add)
                    if p < PAIRS - 1:
                        step.mark(ins)
                    else:
                        ins.then_inc(c_cum, 1)
                dve.wait_ge(c_exp, i + 1 + 1)
                dve.wait_ge(c_ymm, i + 1)
                step.mark(nc.vector.tensor_tensor(ar[:, :, 0:C], kk[:, :, bass.ds(col, C)], pinc[:, :, 0:C], ALU.mult))
                step.mark(nc.vector.tensor_tensor(ar[:, :, C:2 * C], mix[:, 0:KR, bass.ds(col, C)], pinc[:, :, 1:C + 1], ALU.mult))
                step.mark(nc.vector.tensor_tensor(bk[0:64, :, 0:C], bb[0:64, :, bass.ds(col, C)], pneg[0:64, :, :], ALU.mult))
                nc.vector.tensor_tensor(bk[64:128, :, C:2 * C], bb[64:128, :, bass.ds(col, C)], pneg[64:128, :, :], ALU.mult).then_inc(c_ab, 1)
                dve.wait_ge(c_lev, 2 * LEVELS * i + 1)
                for e in range(2):
                    dve.wait_ge(c_gmm, 2 * i + e + 1)
                    nc.vector.tensor_tensor(gm[:, e, :, :], ps[:, e, :].rearrange("p (a b) -> p a b", a=PAIRS),
                                            gmask.unsqueeze(1).broadcast_to([P, PAIRS, P]), ALU.mult).then_inc(c_gm, 1)
                eye4 = eye2.unsqueeze(1).broadcast_to([P, PAIRS, C])
                dve.wait_ge(c_lev, 2 * LEVELS * (i + 1) + 1)
                dve.wait_ge(c_umm, i + 1)
                step.mark(nc.vector.tensor_tensor(tt[:, 0, :, :], nlev[:, 0, :, :], eye4, ALU.add))
                dve.wait_ge(c_xmm, LEVELS * i + 1 + 1)
                nc.vector.tensor_tensor(tt[:, 1, :, :], ps[:, 4, 0:PAIRS * C].rearrange("p (a b) -> p a b", a=PAIRS), eye4, ALU.add).then_inc(c_tev, 1)
                step.wait()
                for l in range(1, LEVELS):
                    n = 2 if l < LEVELS - 1 else 1
                    dve.wait_ge(c_tev, LEVELS * i + l)
                    dve.wait_ge(c_tmm, (LEVELS - 1) * i + l + 1)
                    t2 = tt[:, 0:n, :, :].rearrange("p a b c -> p (a b c)")
                    nc.vector.tensor_tensor(t2, t2, ps[:, 5, 0:n * PAIRS * C], ALU.add).then_inc(c_tev, 1)
                dve.wait_ge(c_smm, i + 1 + 1)
                dve.wait_ge(c_ymm, i + 1 + 1)
                step.done(nc.vector.tensor_tensor(st[:, :, :], st[:, :, :], ps[:, 6, 0:PAIRS * DH].rearrange("p (a b) -> p a b", a=PAIRS), ALU.add))
                nc.vector.tensor_tensor(st[:, :, :], st[:, :, :], pinc[:, :, C:C + 1].broadcast_to([P, PAIRS, DH]), ALU.mult).then_inc(c_sev, 1)

            dve.wait_ge(state_ready, 3)
            with step.loop(TP // C, 8) as i:
                chunk_vector(i, i * C)
            dve.wait_ge(state_in, 16)
            chunk_vector(TP // C, SAMPLE_COL)

            banks = lambda b: ps[:, b:b + 3, 0:CM]
            thirds = lambda ap: ap.rearrange("p (c n) -> p c n", c=3)
            dve.wait_ge(c_yev, TP // C + 1 + 1)
            for j in range(KR):
                dve.wait_ge(p_mm, 4 * j + 1)
                nc.vector.scalar_tensor_tensor(out=thirds(lw[:, j, :]), in0=banks(0), scalar=-1.0 / DH, in1=thirds(lw[:, j, :]),
                                               op0=ALU.mult, op1=ALU.add).then_inc(post_step, 1)
                dve.wait_ge(p_ev, 3 * j + 2)
                step.done(nc.vector.reciprocal(rn[:, :], rn[:, :]))
                dve.wait_ge(post_step, 4 * j + 1)
                nc.vector.tensor_tensor(lw[:, j, :], lw[:, j, :], rn[:, :], ALU.mult).then_inc(post_step, 1)
                nc.vector.scalar_tensor_tensor(out=kk[:, j, :], in0=mix[:, j, :], scalar=vec[:, V_RK + j:V_RK + j + 1], in1=mix[:, KR + j, :],
                                               op0=ALU.mult, op1=ALU.mult).then_inc(post_step, 1)
                dve.wait_ge(p_mm, 4 * j + 3)
                step.done(nc.vector.tensor_tensor(thirds(kk[:, j, :]), banks(0), thirds(mix[:, 2 * KR + j, :]), ALU.mult))
                dve.wait_ge(p_ev, 3 * j + 3)
                nc.vector.tensor_tensor(kk[:, j, :], kk[:, j, :], lw[:, j, :], ALU.add).then_inc(post_step, 1)
                dve.wait_ge(post_step, 4 * j + 4)
                dve.wait_ge(p_mm, 4 * j + 4)
                nc.vector.tensor_tensor(thirds(mix[:, j, :]), thirds(kk[:, j, :]), banks(3), ALU.mult).then_inc(rw_done, 1)

            for name, src, k, v0 in (("q", cq, KQ, V_QG), ("kv", ckv, KKV, V_KVG)):
                for c, (a, n) in enumerate(CH):
                    norm_recip(dve, name, c)
                    dve.wait_ge(sq_used, first_piece[name] + c + 1)
                    for t in range(k):
                        ins = nc.vector.scalar_tensor_tensor(out=src[:, t, a:a + n], in0=src[:, t, a:a + n], scalar=vec[:, v0 + t:v0 + t + 1],
                                                             in1=rstd[:, a:a + n], op0=ALU.mult, op1=ALU.mult)
                        if t < k - 1:
                            step.mark(ins)
                        else:
                            ins.then_inc(qkv_norm, 1)

            def job_max(jb, hp):
                u = jb % 2
                dve.wait_ge(s_mm, JOBS * hp + jb + 1)
                if jb < PJOBS:
                    n = P * (jb // 2 + 1)
                    scores = ps[:, 2 * u:2 * u + 2, :].rearrange("p a b -> p (a b)")
                    step.done(nc.vector.memset(scores[0:C, n - C:n], NEG))
                    nc.vector.tensor_reduce(sm[:, 0, u:u + 1], scores[:, 0:n], AX_X, ALU.max, negate=True).then_inc(nmax, 1)
                else:
                    nc.vector.tensor_reduce(sm[0:TS, 0, u:u + 1], ps[0:TS, 0:6, 0:352], mybir.AxisListType.XY, ALU.max, negate=True).then_inc(nmax, 1)

            def job_norm(jb, hp):
                u = jb % 2
                r = slice(0, P if jb < PJOBS else TS)
                n = P * (jb // 2 + 1) if jb < PJOBS else TS + PAST
                dve.wait_ge(p_exp, JOBS * hp + jb + 1)
                step.done(nc.vector.reciprocal(sm[r, 2, u:u + 1], sm[r, 1, u:u + 1]))
                nc.vector.tensor_scalar(probs[u][r, 0:n], probs[u][r, 0:n], sm[r, 2, u:u + 1], None, ALU.mult).then_inc(p_norm, 1)

            def put_out(i, hp):
                a, w = (P * i, P) if i < QTILES - 1 else (TP, TS)
                dve.wait_ge(o_mm, JOBS * hp + 2 * i + 2 + 1)
                nc.vector.tensor_copy(oatt[:, bass.ds(hp, 1), a:a + w].rearrange("p a b -> p (a b)"), ps[:, 6 + i % 2, 0:w]).then_inc(o_ev, 1)

            with step.loop(PAIRS, 12 + PJOBS + JOBS) as hp:
                for l, (dst, n) in enumerate(K_CHUNKS):
                    dve.wait_ge(kp_mm, 7 * hp + l + 1)
                    nc.vector.tensor_copy(kt[1][0:64, dst:dst + n], ps[64:128, l % 4, 0:n]).then_inc(kd_ev, 1)
                for e in range(2):
                    for c, (a, n) in enumerate(CH):
                        l = 3 * e + c
                        dve.wait_ge(qp_mm, 6 * hp + l + 1)
                        dve.wait_ge(qd_ev, 6 * hp + l + 1)
                        step.mark(nc.vector.scalar_tensor_tensor(out=rtmp[0][64:96, 0:n], in0=ps[64:96, 4 + l % 4, 0:n], scalar=SCALE,
                                                                 in1=cs[64:96, a:a + n], op0=ALU.mult, op1=ALU.mult))
                        step.done(nc.vector.scalar_tensor_tensor(out=rtmp[1][64:96, 0:n], in0=ps[96:128, 4 + l % 4, 0:n], scalar=SCALE,
                                                                 in1=cs[96:128, a:a + n], op0=ALU.mult, op1=ALU.mult))
                        nc.vector.tensor_tensor(qt[e][64:96, a:a + n], rtmp[0][64:96, 0:n], rtmp[1][64:96, 0:n], ALU.add).then_inc(qd_ev, 1)
                for jb in range(PJOBS):
                    job_max(jb, hp)
                    if jb:
                        job_norm(jb - 1, hp)
                    if jb >= 3 and jb % 2:
                        put_out((jb - 3) // 2, hp)
                job_norm(PJOBS - 1, hp)
                put_out(QTILES - 2, hp)
                for jb in range(PJOBS, JOBS):
                    job_max(jb, hp)
                    job_norm(jb, hp)
                put_out(QTILES - 1, hp)

            dve.wait_ge(o_ev, QTILES * PAIRS + 1)
            for i, (dst, src) in enumerate(o_parts(hlo)):
                dve.wait_ge(osplit_hi, i + 1)
                hi = o_parts(hhi)[i][0].bitcast(F32)
                nc.vector.tensor_tensor(dst, src, hi, ALU.subtract).then_inc(osplit_lo, 1)

            split_lo(dve, OUT_M, 0)
            split_lo(dve, OUT_M, 1)
            for n in range(KD):
                split_lo(dve, OUT_M + 1 + n // 2, n % 2)

            def residual(dst, src, which, c, signal):
                parts = [(k, b, w, s) for k in range(KD) for b, w, s in segments(c)]
                for i, (k, b, w, s) in enumerate(parts):
                    ins = nc.vector.scalar_tensor_tensor(out=dst[:, k, b:b + w], in0=src[:, k, b:b + w], scalar=gains[:, which, k, s:s + 1],
                                                         in1=dst[:, k, b:b + w], op0=ALU.mult, op1=ALU.add)
                    if i < len(parts) - 1:
                        step.mark(ins)
                    else:
                        ins.then_inc(signal, 1)

            dve.wait_ge(x2_in, 48)
            for c, (a, n) in enumerate(CH):
                norm_recip(dve, "m", c)
                step.done(nc.vector.tensor_tensor(m1[:, :, a:a + n], m1[:, :, a:a + n], over_tiles(rstd[:, a:a + n], KD), ALU.mult))
                residual(x2, m1, 1, c, x2_done)
            step.wait()
            dve.wait_ge(x2_done, 3)
            for c in range(3):
                norm_recip(dve, "n2", c)
                times_rstd(m1, x2, c)
            for c in range(3):
                rest(m1, c, 3 + c)

            def down_lo(g, u):
                dve.wait_ge(d_hi, 2 * g + u + 1)
                nc.vector.tensor_tensor(dlo[u][:, :], draw[:, :], dhi[u][:, :].bitcast(F32), ALU.subtract).then_inc(d_lo, 1)

            def product(g, slot, j, last=False):
                m = 2 * g + FF_M + j
                q = 6 * g + 3 * j
                if not last:
                    split_lo(dve, m + 1, 0)
                for c, (a, n) in enumerate(CH):
                    dve.wait_ge(sil_ready, q + c + 1)
                    dve.wait_ge(out_ready[1], 3 * m + c + 1)
                    nc.vector.tensor_tensor(sil[c][:, 0:n], sil[c][:, 0:n], ps[:, 3 + c, 0:n], ALU.mult).then_inc(prod_ready, 1)
                for c, (a, n) in enumerate(CH):
                    dve.wait_ge(act_hi, q + c + 1)
                    nc.vector.tensor_tensor(alo[:, slot + j, a:a + n], sil[c][:, 0:n], ahi[:, slot + j, a:a + n].bitcast(F32),
                                            ALU.subtract).then_inc(act_lo, 1)
                if not last:
                    split_lo(dve, m + 1, 1)

            def add_down(g):
                for x in range(24):
                    k, (a, n) = x // 3, CH[x % 3]
                    dve.wait_ge(down_ready, 24 * g + x + 1 + 1)
                    nc.vector.tensor_tensor(acc[:, k, a:a + n], acc[:, k, a:a + n], ps[:, 6 + x % 2, 0:n], ALU.add).then_inc(d_added, 1)

            def group(g, slot, last=False):
                product(g, slot, 0)
                down_lo(g - 1, 0)
                down_lo(g - 1, 1)
                product(g, slot, 1, last=last)
                dve.wait_ge(d_added, 24 * (g - 1) + 1)
                add_down(g - 1)

            dve.wait_ge(acc_zero, 1)
            product(0, 0, 0)
            product(0, 0, 1)
            with dve.Fori(0, (GROUPS - 3) // 2) as it:
                group(2 * it + 1, 2)
                group(2 * it + 2, 0)
            group(GROUPS - 2, 2)
            group(GROUPS - 1, 0, last=True)
            down_lo(GROUPS - 1, 0)
            down_lo(GROUPS - 1, 1)
            dve.wait_ge(d_added, 24 * (GROUPS - 1) + 1)
            add_down(GROUPS - 1)

            dve.wait_ge(d_added, 24 * GROUPS + 1)
            dve.wait_ge(x3_in, 16)
            for c, (a, n) in enumerate(CH):
                norm_recip(dve, "f", c)
                dve.wait_ge(sq_used, first_piece["f"] + 2 * c + 2)
                step.done(nc.vector.tensor_tensor(acc[:, :, a:a + n], acc[:, :, a:a + n], over_tiles(rstd[:, a:a + n], KD), ALU.mult))
                residual(x3, acc, 3, c, y_done)

        @block.tensor
        def _(pe):
            def before_small():
                pe.sem_inc(waited, 1)

            start_at_one(pe, c_tr, c_xmm, c_ymm, c_smm, c_tmm, c_umm, t_mm, o_mm, down_ready)
            pe.wait_ge(const_in, 16)
            for c in range(3):
                norm_sum(pe, "n1", sq1, c)
            pe.wait_ge(silu_c, 1)

            def ada(i, u, first=False):
                pe.wait_ge(slab_in[u], 16 * (i + 1))
                if not first:
                    pe.wait_ge(mod_done, 2 * i + u - 1)
                for j in range(4):
                    for k in range(KD):
                        mm = nc.tensor.matmul(ps[:, u, 2 * j:2 * j + 2], slab[u][:, k, P * j:P * j + P], cs_c[:, k, :], start=(k == 0), stop=(k == KD - 1))
                mm.then_inc(slab_mm, 1)

            ada(0, 0, first=True)
            ada(0, 1, first=True)
            with pe.Fori(1, 6) as i:
                for u in range(2):
                    ada(i, u)
            pe.wait_ge(mod_done, 12)

            pe.wait_ge(lo_ready, 3)
            project(pe, 0, 0, first=True)
            project(pe, 0, 1, first=True)
            with pe.Fori(1, OUT_M) as m:
                for u in range(2):
                    project(pe, m, u)
            for u in range(2):
                pe.wait_ge(bank_free[u], 3 * OUT_M)

            pe.wait_ge(lora_act, 2)
            pe.wait_ge(mix_done, RW_TILES)
            pe.wait_ge(lora_in, 32)
            for j in range(KR):
                for s in range(2):
                    if j:
                        pe.wait_ge(lora_ev, 2 * j + s - 1)
                    for c in range(3):
                        mm = nc.tensor.matmul(ps[:, 3 * s + c, 0:CM], w2a2[64 * s:64 * s + 64, P * j:P * j + P],
                                              mix[64 * s:64 * s + 64, 12, CM * c:CM * c + CM], start=True, stop=True)
                    mm.then_inc(lora_mm, 1)

            def block_sum(src, b, signal):
                for c in range(3):
                    mm = nc.tensor.matmul(ps[:, b + c, 0:CM], block64, src[:, CM * c:CM * c + CM], start=True, stop=True)
                mm.then_inc(signal, 1)

            pe.wait_ge(lora_ev, 2 * KR)
            for j in range(KR):
                pe.wait_ge(kk_sq, j + 1)
                if j >= 2:
                    pe.wait_ge(kk_root, j - 1)
                block_sum(sqr, 3 * (j % 2), kk_mm)
            pe.wait_ge(kk_root, KR)
            pe.wait_ge(pre_done, KR)
            pe.wait_ge(state_ready, 3)

            def per_head():
                return [(p, e, slice(64 * e, 64 * e + 64)) for p in range(PAIRS) for e in range(2)]

            def chunk_tensor(i):
                pe.wait_ge(c_ab, i + 1)
                pe.wait_ge(c_k, 2 * i + 2 + 1)
                pe.wait_ge(c_gm, 2 * i + 1)
                before_small()
                for e in range(2):
                    r = slice(64 * e, 64 * e + 64)
                    for p in range(PAIRS):
                        mm = nc.tensor.matmul(ps[:, e, P * p:P * p + P], bk[r, p, :], ar[r, p, :], start=True, stop=True)
                    mm.then_inc(c_gmm, 1)
                pe.wait_ge(c_v, i + 1)
                pe.wait_ge(c_tm, i + 1)
                for p in range(PAIRS):
                    nc.tensor.transpose(ps[:, 2, P * p:P * p + P], bk[:, p, :], ident)
                for p in range(PAIRS):
                    mm = nc.tensor.transpose(ps[:, 3, P * p:P * p + P], vv[:, p, :, :].rearrange("p a b -> p (a b)"), ident)
                mm.then_inc(c_tr, 1)
                pe.wait_ge(c_lev, 2 * LEVELS * (i + 1) + 1)
                for l in range(LEVELS):
                    if l:
                        pe.wait_ge(c_tev, LEVELS * i + l)
                    before_small()
                    before_small()
                    for p, e, r in per_head():
                        x = tt[r, 1, p, :] if l else con[r, K_EYE2:K_EYE2 + C]
                        mm = nc.tensor.matmul(ps[r, 4, C * p:C * p + C], nlev[r, l, p, :], x, start=True, stop=True)
                    mm.then_inc(c_xmm, 1)
                    if l:
                        pe.wait_ge(c_xev, (LEVELS - 1) * i + l)
                        before_small()
                        for p, e, r in per_head():
                            mm = nc.tensor.matmul(ps[r, 5, C * p:C * p + C], xt[r, p, :], tt[r, 0, p, :], start=True, stop=True)
                        if l < LEVELS - 1:
                            for p, e, r in per_head():
                                mm = nc.tensor.matmul(ps[r, 5, C * (PAIRS + p):C * (PAIRS + p) + C], tt[r, 0, p, :], xt[r, p, :], start=True, stop=True)
                        mm.then_inc(c_tmm, 1)
                pe.wait_ge(c_tm, i + 1 + 1)
                pe.wait_ge(c_gm, 2 * i + 2 + 1)
                pe.wait_ge(c_sev, i + 1)
                before_small()
                for p, e, r in per_head():
                    nc.tensor.matmul(ps[r, 6, C * p:C * p + C], ar[r, p, 0:C], st[r, p, :], start=True, stop=False)
                    mm = nc.tensor.matmul(ps[r, 6, C * p:C * p + C], gm[:, e, p, 0:C], vz[:, p, C * e:C * e + C], start=False, stop=True)
                mm.then_inc(c_rmm, 1)
                pe.wait_ge(c_rev, i + 1)
                pe.wait_ge(c_tev, LEVELS * (i + 1))
                pe.wait_ge(c_yev, i + 1)
                before_small()
                for p, e, r in per_head():
                    mm = nc.tensor.matmul(ps[r, 7, C * p:C * p + C], tt[r, 0, p, :], rhs[r, p, :], start=True, stop=True)
                mm.then_inc(c_umm, 1)
                pe.wait_ge(c_uev, i + 1)
                pe.wait_ge(c_uvv, 2 * i + 2)
                before_small()
                for p, e, r in per_head():
                    mm = nc.tensor.matmul(ps[r, 6, C * p:C * p + C], bktm[:, p, C * e:C * e + C], uv[:, p, C * e:C * e + C], start=True, stop=True)
                mm.then_inc(c_smm, 1)
                for p, e, r in per_head():
                    nc.tensor.matmul(ps[r, 7, C * p:C * p + C], st[r, p, :], ar[r, p, C:2 * C], start=True, stop=False)
                    mm = nc.tensor.matmul(ps[r, 7, C * p:C * p + C], uv[:, p, C * e:C * e + C], gm[:, e, p, C:2 * C], start=False, stop=True)
                mm.then_inc(c_ymm, 1)

            with pe.Fori(0, TP // C) as i:
                chunk_tensor(i)
            pe.wait_ge(state_in, 16)
            chunk_tensor(TP // C)

            pe.wait_ge(c_yev, TP // C + 1 + 1)
            for j in range(KR):
                if j:
                    pe.wait_ge(post_step, 4 * j)
                block_sum(lw[:, j, :], 0, p_mm)
                pe.wait_ge(p_ev, 3 * j + 1)
                if j:
                    pe.wait_ge(rw_done, j)
                block_sum(sqr, 3, p_mm)
                pe.wait_ge(post_step, 4 * j + 3)
                block_sum(kk[:, j, :], 0, p_mm)
                pe.wait_ge(p_ev, 3 * j + 2)
                for c in range(3):
                    mm = nc.tensor.matmul(ps[:, 3 + c, 0:CM], g2[:, P * j:P * j + P], mix[:, 13, CM * c:CM * c + CM], start=True, stop=True)
                mm.then_inc(p_mm, 1)

            for name in ("q", "kv"):
                for c in range(3):
                    norm_sum(pe, name, sq_lat, c)

            pe.wait_ge(qkv_norm, 6)
            pe.wait_ge(past_in, 48)
            pe.wait_ge(krope_copied, 2)

            def scores(jb, hp):
                e, u, i = jb % 2, jb % 2, jb // 2
                if jb >= PJOBS:
                    pe.wait_ge(p_exp, JOBS * hp + jb)
                    pe.wait_ge(t_ev, T_GROUPS * hp + T_FIRST[jb])
                    for b in range(6):
                        mm = nc.tensor.matmul(ps[0:TS, b, 0:352], qt[e][0:96, TP:T], kt[e][0:96, TP + 352 * b:TP + 352 * b + 352], start=True, stop=True)
                else:
                    if jb >= 2:
                        pe.wait_ge(p_exp, JOBS * hp + jb - 1)
                    n = P * (i + 1)
                    for b, n0 in enumerate(range(0, n, 512)):
                        w = min(512, n - n0)
                        mm = nc.tensor.matmul(ps[:, 2 * u + b, 0:w], qt[e][0:96, P * i:P * i + P], kt[e][0:96, n0:n0 + w], start=True, stop=True)
                mm.then_inc(s_mm, 1)

            def turn(jb, hp):
                u = jb % 2
                pe.wait_ge(p_norm, JOBS * hp + jb + 1)
                for g, (t0, t1) in enumerate(T_PLAN[jb]):
                    tg = T_FIRST[jb] + g
                    if tg >= 2:
                        pe.wait_ge(t_ev, T_GROUPS * hp + tg - 1)
                    if jb >= PJOBS:
                        before_small()
                    for t in range(t0, t1):
                        if jb < PJOBS:
                            mm = nc.tensor.transpose(ps[:, 4 + tg % 2, P * (t - t0):P * (t - t0) + P], probs[u][:, P * t:P * t + P], ident)
                        else:
                            k0, rows = (0, TS) if t == 0 else (TS + P * (t - 1), P)
                            mm = nc.tensor.transpose(ps[0:rows, 4 + tg % 2, TS * (t - t0):TS * (t - t0) + TS], probs[u][0:TS, k0:k0 + rows], con[0:TS, 0:TS])
                    mm.then_inc(t_mm, 1)

            def values(jb, hp):
                e, u, i = jb % 2, jb % 2, jb // 2
                pe.wait_ge(t_ev, T_GROUPS * hp + T_FIRST[jb + 1])
                if i >= 2:
                    pe.wait_ge(o_ev, QTILES * hp + i - 1 + 1)
                r = slice(64 * e, 64 * e + 64)
                if jb >= PJOBS:
                    before_small()
                if jb < PJOBS:
                    for t in range(i + 1):
                        mm = nc.tensor.matmul(ps[r, 6 + i % 2, 0:P], vt[:, t, r], pt[u][:, P * t:P * t + P], start=(t == 0), stop=(t == i))
                else:
                    for t in range(17):
                        rows = slice(0, TS if t == 0 else P)
                        mm = nc.tensor.matmul(ps[r, 6 + i % 2, 0:TS], vt[rows, 8 + t, r], pt[u][rows, TS * t:TS * t + TS], start=(t == 0), stop=(t == 16))
                mm.then_inc(o_mm, 1)

            with pe.Fori(0, PAIRS) as hp:
                pe.wait_ge(aw_in, 16 * hp + 16)
                pe.wait_ge(o_ev, QTILES * hp + 1)
                wq = lambda e, k: aw[:, 384 * e + P * k:384 * e + P * k + P]
                wk = lambda k: aw[:, 768 + P * k:768 + P * k + P]
                wv = lambda k: aw[:, 1024 + P * k:1024 + P * k + P]
                for l, (dst, n) in enumerate(K_CHUNKS):
                    if l >= 4:
                        pe.wait_ge(ka_ev, 7 * hp + l - 3)
                        pe.wait_ge(kd_ev, 7 * hp + l - 3)
                    for k in range(KKV):
                        src = ckv[:, k, dst:dst + n] if l < 3 else past[:, k, dst - T:dst - T + n]
                        mm = nc.tensor.matmul(ps[:, l % 4, 0:n], wk(k), src, start=(k == 0), stop=(k == KKV - 1))
                    mm.then_inc(kp_mm, 1)
                for e in range(2):
                    for c, (a, n) in enumerate(CH):
                        l = 3 * e + c
                        if l >= 4:
                            pe.wait_ge(qa_ev, 6 * hp + l - 3)
                            pe.wait_ge(qd_ev, 6 * hp + l - 3 + 1)
                        for k in range(KQ):
                            mm = nc.tensor.matmul(ps[:, 4 + l % 4, 0:n], wq(e, k), cq[:, k, a:a + n], start=(k == 0), stop=(k == KQ - 1))
                        mm.then_inc(qp_mm, 1)
                for g, tiles in enumerate(V_GROUPS):
                    if g + 3 < 7:
                        pe.wait_ge(ka_ev, 7 * hp + g + 4)
                        pe.wait_ge(kd_ev, 7 * hp + g + 4)
                    else:
                        pe.wait_ge(v_ev, 7 * hp + g - 3)
                    for x, t in enumerate(tiles):
                        rows = TS if t == 8 else P
                        for k in range(KKV):
                            src = ckv[:, k, P * t:P * t + rows] if t < 9 else past[:, k, P * (t - 9):P * (t - 9) + P]
                            mm = nc.tensor.matmul(ps[0:rows, (7 + g) % 4, P * x:P * x + P], src, wv(k), start=(k == 0), stop=(k == KKV - 1))
                    mm.then_inc(vp_mm, 1)
                pe.wait_ge(v_ev, 7 * hp + 7)
                pe.wait_ge(kd_ev, 7 * hp + 7)
                pe.wait_ge(qa_ev, 6 * hp + 6)
                pe.wait_ge(qd_ev, 6 * hp + 6 + 1)
                scores(0, hp)
                scores(1, hp)
                for jb in range(PJOBS):
                    turn(jb, hp)
                    if jb + 2 < PJOBS:
                        scores(jb + 2, hp)
                    values(jb, hp)
                for jb in range(PJOBS, JOBS):
                    scores(jb, hp)
                    turn(jb, hp)
                    values(jb, hp)

            pe.wait_ge(osplit_lo, 3)
            with pe.Fori(OUT_M, FF_M) as m:
                for u in range(2):
                    project(pe, m, u)
            for name in ("m", "n2"):
                for c in range(3):
                    norm_sum(pe, name, sq2, c)

            def down(g, slot, first=False):
                pe.wait_ge(d_lo, 2 * g + 2)
                pe.wait_ge(act_lo, 6 * g + 6)
                for x in range(24):
                    k, (a, n) = x // 3, CH[x % 3]
                    if not (first and x < 2):
                        pe.wait_ge(d_added, 24 * g + x - 1 + 1)
                    for u in range(2):
                        for w, y in ((dhi, ahi), (dhi, alo), (dlo, ahi)):
                            mm = nc.tensor.matmul(ps[:, 6 + x % 2, 0:n], w[u][:, P * k:P * k + P], y[:, slot + u, a:a + n],
                                                  start=(u == 0 and w is dhi and y is ahi), stop=(u == 1 and w is dlo))
                    mm.then_inc(down_ready, 1)

            pe.wait_ge(lo_ready, 6)

            def group(g, slot):
                for j in range(2):
                    for u in range(2):
                        ff_project(g, j, u)

            def ff_project(g, j, u):
                m = 2 * g + FF_M + j
                pe.wait_ge(w_lo, 2 * m + u + 1)
                for c, (a, n) in enumerate(CH):
                    pe.wait_ge((sil_ready, prod_ready)[u], 6 * g + 3 * j + c - 2)
                    products(m, u, c)

            def products(m, u, c):
                a, n = CH[c]
                for k in range(KD):
                    for w, x in ((whi, hhi), (whi, hlo), (wlo, hhi)):
                        mm = nc.tensor.matmul(ps[:, 3 * u + c, 0:n], w[u][:, k, :], x[:, k, a:a + n],
                                              start=(k == 0 and w is whi and x is hhi), stop=(k == KD - 1 and w is wlo))
                mm.then_inc(out_ready[u], 1)

            for u in range(2):
                pe.wait_ge(bank_free[u], 3 * FF_M)
                pe.wait_ge(w_lo, 2 * FF_M + u + 1)
                for c in range(3):
                    products(FF_M, u, c)
            for u in range(2):
                ff_project(0, 1, u)
            group(1, 2)
            down(0, 0, first=True)
            with pe.Fori(0, (GROUPS - 3) // 2) as it:
                group(2 * it + 2, 0)
                down(2 * it + 1, 2)
                group(2 * it + 3, 2)
                down(2 * it + 2, 0)
            group(GROUPS - 1, 0)
            down(GROUPS - 2, 2)
            down(GROUPS - 1, 0)
            for c in range(3):
                norm_sum(pe, "f", sq3, c)


def shape_table():
    t = np.zeros((P, K_ALL), np.float32)
    t[:, K_IDENT:K_IDENT + P] = np.eye(P)
    t[:, K_ONES:K_ONES + P] = 1.0
    half = np.arange(P) // 64
    t[:, K_BLOCK:K_BLOCK + P] = half[:, None] == half[None, :]
    s, tok = (np.arange(P) % C)[:, None], np.arange(C)[None, :]
    t[:, K_GMASK:K_GMASK + C] = s < tok
    t[:, K_GMASK + C:K_GMASK + 2 * C] = s <= tok
    for l in range(LEVELS):
        m = 2 ** l
        t[:, K_LEVEL + C * l:K_LEVEL + C * l + C] = -1.0 * ((s // (2 * m) == tok // (2 * m)) & (s // m % 2 == 0) & (tok // m % 2 == 1))
    t[:, K_EYE2:K_EYE2 + C] = s == tok
    t[:, K_EPS] = 1e-6
    t[:, K_EPS + 1] = 64e-5
    inv = np.float32(10000.0) ** (-np.arange(0, ROPE, 2, dtype=np.float32) / np.float32(ROPE))
    pos = np.concatenate([np.arange(TP), PAST + np.arange(TS)]).astype(np.float32)
    ang = (inv[:, None] * pos[None, :]).astype(np.float32)
    cos, sin = np.cos(ang), np.sin(ang)
    t[64:96, K_CS:] = np.concatenate([cos, cos])
    t[96:128, K_CS:] = np.concatenate([-sin, sin])
    return t


def kernel(**inputs):
    import concourse.bacc as bacc
    from concourse.bass_utils import run_bass_kernel_spmd

    x = {k: np.asarray(v) for k, v in inputs.items()}

    def columns(v):
        return np.reshape(v, (-1, P)).T

    def tiles(w):
        return np.reshape(w, (KD, P, -1, P)).transpose(2, 1, 0, 3).reshape(-1, P, KD * P)

    def swapped(w):
        return np.concatenate([w[..., ROPE // 2:], w[..., :ROPE // 2]], axis=-1)

    w_in = x["w_in"][0]
    mla = QL + KVL
    kr_cols = w_in[:, mla:mla + ROPE]
    w_lat = np.concatenate([w_in[:, :mla], np.zeros((D, 64), np.float32), kr_cols, swapped(kr_cols)], axis=1)
    w_rw = w_in[:, mla + ROPE:]
    gate, up = tiles(x["w_gate"][0]), tiles(x["w_up"][0])
    gate_up = np.stack([gate, up], axis=1).reshape(-1, P, KD * P)
    w_tiles = np.concatenate([tiles(w_lat), tiles(w_rw), tiles(x["w_out"][0]), gate_up])

    wuq = x["w_uq"][0].reshape(KQ, P, HEADS, DH + ROPE)
    wuq = np.concatenate([wuq, swapped(wuq[..., DH:])], axis=-1).reshape(KQ, P, PAIRS, 2, P).transpose(2, 1, 3, 0, 4).reshape(PAIRS, P, -1)
    by_pair = lambda w: w.reshape(KKV, P, PAIRS, P).transpose(2, 1, 0, 3).reshape(PAIRS, P, -1)
    att_w = np.concatenate([wuq, by_pair(x["w_uk"][0]), by_pair(x["w_uv"][0])], axis=2)

    c2 = np.stack([x["c_prompt"][0].reshape(KD, P), x["c_sample"][0].reshape(KD, P)]).transpose(2, 1, 0).reshape(P, 2 * KD)
    vectors = np.concatenate([columns(x[n][0]) for n in ("norm_g", "q_norm_g", "kv_norm_g", "rw_mu", "rw_w0", "rw_a0", "rw_kk", "rw_ka",
                                                       "rw_rk", "lnx_g", "lnx_b", "ada_b")] + [c2, columns(x["state_shift"][0, 0])], axis=1)
    arrays = {
        "table": shape_table(),
        "vectors": vectors,
        "x_t": np.concatenate([x["x_prompt"][0], x["x_sample"][0]]).T,
        "ada_w": x["ada_w"][0],
        "w_tiles": w_tiles,
        "att_w": att_w,
        "w2a2": np.concatenate([x["rw_w2"][0], x["rw_a2"][0]]),
        "g2": x["rw_g2"][0],
        "w_down": x["w_down"][0],
        "ckv_t": x["cache_ckv"][0, 0].T,
        "krope_t": x["cache_krope"][0, 0].T,
        "state0": x["state_wkv"][0, 0].reshape(PAIRS, 2, DH, DH).transpose(1, 3, 0, 2).reshape(P, PAIRS * DH),
    }
    outs = {"y": (D, T), "ckv_out": (KVL, T), "krope_out": (ROPE, T), "wkv": (2, P, PAIRS * DH), "shift": (P, 2 * RW_TILES)}
    nc = bacc.Bacc("TRN2", target_bir_lowering=False, num_devices=1)
    d, feed = {}, {}
    for name, a in arrays.items():
        feed[f"in_{name}"] = np.ascontiguousarray(a)
        d[name] = nc.dram_tensor(f"in_{name}", a.shape, F32, kind="ExternalInput").ap()
    for name, shape in outs.items():
        d[name] = nc.dram_tensor(f"out_{name}", shape, F32, kind="ExternalOutput").ap()
    d["x_mid"] = nc.dram_tensor("x_mid", (D, T), F32, kind="Internal").ap()
    build(nc, d)
    got = run_bass_kernel_spmd(nc, [feed], core_ids=[0]).results[0]
    y, ckv, krope = (got[f"out_{n}"].T for n in ("y", "ckv_out", "krope_out"))
    wkv = got["out_wkv"].reshape(2, 2, DH, PAIRS, DH).transpose(0, 3, 1, 4, 2).reshape(2, HEADS, DH, DH)
    shift = got["out_shift"].reshape(P, RW_TILES, 2).transpose(2, 1, 0).reshape(2, RW_TILES * P)
    c = np.ascontiguousarray
    return (c(y[None, :TP]), c(y[None, TP:]), c(ckv[None, None, :TP]), c(krope[None, None, :TP]), c(wkv[None, None, 0]), c(shift[None, None, 0]),
            c(ckv[None, None, TP:]), c(krope[None, None, TP:]), c(wkv[None, None, 1]), c(shift[None, None, 1]))
```

```python
from contextlib import ExitStack, contextmanager

import numpy as np

import concourse.bass as bass
from concourse import mybir

F32 = mybir.dt.float32
F32R = mybir.dt.float32r
ALU = mybir.AluOpType
ACT = mybir.ActivationFunctionType
AX_X = mybir.AxisListType.X

P = 128
D = 1024
KD = D // P
TP = 1024
TS = 64
T = TP + TS
PAST = 2048
C = 64
HEADS = 8
PAIRS = HEADS // 2
DH = 64
ROPE = 32
QL, KVL = 384, 256
KQ, KKV = QL // P, KVL // P
RW = 512
KR = RW // P
RW_TILES = 14
MLA_TILES = 6
DFF = 2816
GROUPS = DFF // (2 * P)
TM = T + 1
SAMPLE_COL = TP + 1
KEYS = T + PAST
SCALE = (DH + ROPE) ** -0.5
DECAY = float(np.exp(-0.5))
NEG = -1e30
CH = [(0, 364), (364, 364), (728, 360)]
CM = 363
LEVELS = 6
SF = 6
CHUNKS = TP // C

K_IDENT, K_ONES, K_BLOCK, K_GMASK, K_LEVEL, K_EYE2 = 0, 128, 256, 384, 512, 512 + LEVELS * 64
K_EPS = K_EYE2 + 64
K_CS = K_EPS + 4
K_ALL = K_CS + T
V_NORM, V_QG, V_KVG, V_MU, V_W0, V_A0, V_KK, V_KA, V_RK, V_LG, V_LB = 0, 32, 35, 37, 51, 55, 59, 63, 67, 71, 75
V_ADAB, V_C, V_SHIFT = 79, 127, 143
V_ALL = 157


K_CHUNKS = CH + [(T + 512 * j, 512) for j in range(PAST // 512)]
V_GROUPS = [[0, 1, 2, 3], [4, 5, 6, 7], [8]] + [list(range(9 + 4 * j, 13 + 4 * j)) for j in range(4)]
PJOBS = 2 * (TP // P)
JOBS = PJOBS + 2
QTILES = JOBS // 2
T_PLAN = [[(a, min(a + 4, jb // 2 + 1)) for a in range(0, jb // 2 + 1, 4)] for jb in range(PJOBS)] + 2 * [[(0, 8), (8, 16), (16, 17)]]
T_FIRST = [sum(len(x) for x in T_PLAN[:jb]) for jb in range(JOBS + 1)]
T_GROUPS = T_FIRST[-1]


def job_units():
    units = [("scores", 0, 0), ("scores", 1, 0)]
    for jb in range(JOBS):
        if jb == PJOBS:
            units.append(("scores", jb, 0))
        units += [("turn", jb, g) for g in range(len(T_PLAN[jb]))]
        if jb + 2 < PJOBS:
            units.append(("scores", jb + 2, 0))
        if jb == PJOBS:
            units.append(("scores", jb + 1, 0))
        units.append(("values", jb, 0))
    return units


JOB_UNITS = job_units()
ATT_UNITS = len(K_CHUNKS) + 2 * len(CH) + len(V_GROUPS) + len(JOB_UNITS)
CHUNK_UNITS = 5 + 2 * (LEVELS - 1) + 4
EARLY, SLABS = 4, 12
WB = 6


class Steps:

    def __init__(self, eng, sem):
        self.eng, self.sem, self.base, self.n = eng, sem, 0, 0

    def mark(self, ins):
        ins.then_inc(self.sem, 1)
        self.n += 1

    def wait(self):
        self.eng.wait_ge(self.sem, self.base + self.n)

    def done(self, ins):
        self.mark(ins)
        self.wait()

    @contextmanager
    def loop(self, count, per):
        start = self.base + self.n
        with self.eng.Fori(0, count) as i:
            self.base, self.n = (i * per + start if per else start), 0
            yield i
            assert self.n == per, f"the body makes {self.n} steps, not {per}"
        self.base, self.n = start + count * per, 0


def build(nc, d):
    with ExitStack() as ctx:
        def sem(name):
            return ctx.enter_context(nc.semaphore(name))

        def place(start, *tensors):
            out = []
            for name, shape, *dt in tensors:
                out.append(nc.alloc_sbuf_tensor_at(name, shape, dt[0] if dt else F32, offset=start))
                start += -(-int(np.prod(shape[1:])) * 4 // 32) * 32
            return *out, start

        (con, vec, mod, gains, cs_c, omm, oma, sh_out, sm, rstd, krope, WA) = place(
            17 * 1024,
            ("con", [P, K_ALL]), ("vec", [P, V_ALL]), ("mod", [P, 48, 2]),
            ("gains", [P, 4, 8, 2]),
            ("cs_c", [P, 8, 2]), ("omm", [P, 14]), ("oma", [P, 4]),
            ("sh_out", [P, 14, 2]), ("sm", [P, 3, 2]),
            ("rstd", [P, T]), ("krope", [P, T]))
        tile = [P, KD, P]
        wraw0, wraw1, whi0, whi1, wlo0, wlo1, R1 = place(
            WA, ("wraw0", tile), ("wraw1", tile), ("whi0", tile, F32R), ("whi1", tile, F32R), ("wlo0", tile, F32R), ("wlo1", tile, F32R))
        wraw, whi, wlo = [wraw0, wraw1], [whi0, whi1], [wlo0, wlo1]
        hhi, hlo, R2 = place(R1, ("hhi", [P, KD, T], F32R), ("hlo", [P, KD, T], F32R))
        END = nc.sbuf_usable_end

        sq = [P, 4, 364]
        x1, s0, s1, r0, r1, end = place(R2, ("x1", [P, KD, T]), ("sq1_0", sq), ("sq1_1", sq), ("mrow0", [2, 512]), ("mrow1", [2, 512]))
        sq1, mrow = [s0, s1], [r0, r1]
        assert end <= END
        *slab, end = place(R1, *((f"slab{u}", [P, KD, 512]) for u in range(EARLY)))
        assert end <= R2
        cq, ckv, raw0, raw1, mix, end = place(R2, ("cq", [P, KQ, T]), ("ckv", [P, KKV, T]), ("raw0", [P, TM + 1]), ("raw1", [P, TM + 1]),
                                              ("mix", [P, RW_TILES, TM]))
        raw = [raw0, raw1]
        assert end <= END
        RAW_AT = R2 + (KQ + KKV) * T * 4
        MIX_AT = RAW_AT + 2 * (-(-(TM + 1) * 4 // 32) * 32)
        lw, kk, bb, sqr, rn, w2a2, g2, end = place(R1, ("lw", [P, KR, TM]), ("kk", [P, KR, TM]), ("bb", [P, KR, TM]), ("sqr", [P, TM]),
                                                   ("rn", [P, TM]), ("w2a2", [P, RW]), ("g2", [P, RW]))
        assert end <= R2
        sl0, sl1, end = place(WA, ("sq_lat0", sq), ("sq_lat1", sq))
        sq_lat = [sl0, sl1]
        bn0, bn1, go0, go1, tmp, end = place(WA, ("bn0", [P, TM]), ("bn1", [P, TM]), ("go0", [P, TM]), ("go1", [P, TM]), ("tmp", [P, TM]))
        bonus, gout = [bn0, bn1], [go0, go1]
        assert end <= R1
        cum, pinc, pneg, bk, ar, vv, gm, tt, xt, bktm, uv, st0, st1, rhs, end = place(
            WA, ("cum", [P, PAIRS, C + 1]), ("pinc", [P, PAIRS, C + 1]), ("pneg", [P, PAIRS, C]), ("bk", [P, PAIRS, 2 * C]),
            ("ar", [P, PAIRS, 2 * C]), ("vv", [P, PAIRS, 2, C]), ("gm", [P, 2, PAIRS, 2 * C]),
            ("tt", [P, 2, PAIRS, C]),
            ("xt", [P, PAIRS, C]), ("bktm", [P, PAIRS, P]), ("uv", [P, PAIRS, P]), ("st0", [P, PAIRS, DH]), ("st1", [P, PAIRS, DH]),
            ("rhs", [P, PAIRS, C]))
        state = [st0, st1]
        assert end <= R1
        nlev, end = place(RAW_AT, ("nlev", [P, LEVELS, PAIRS, C]))
        assert end <= MIX_AT
        past, kt0, kt1, qt0, qt1, vt, aw, end = place(
            R1, ("past", [P, KKV, PAST]), ("kt0", [P, KEYS]), ("kt1", [P, KEYS]), ("qt0", [P, T]), ("qt1", [P, T]), ("vt", [P, 25, P]), ("aw", [P, 1280]))
        kt, qt = [kt0, kt1], [qt0, qt1]
        assert end <= R2
        ci0, ci1, yb0, yb1, vz, pr0, pr1, pt0, pt1, rt0, rt1, end = place(
            MIX_AT, ("ci0", [P, SF, PAIRS, C]), ("ci1", [P, SF, PAIRS, C]), ("yb0", [P, PAIRS, C]), ("yb1", [P, PAIRS, C]),
            ("vz", [P, PAIRS, P]),
            ("pr0", [P, TS + PAST]), ("pr1", [P, TS + PAST]), ("pt0", [P, 1088]), ("pt1", [P, 1088]), ("rt0", [P, 364]), ("rt1", [P, 364]))
        cin, ybuf, probs, pt, rtmp = [ci0, ci1], [yb0, yb1], [pr0, pr1], [pt0, pt1], [rt0, rt1]
        OATT_AT = (END - PAIRS * T * 4) // 32 * 32
        assert end <= OATT_AT
        oatt, _ = place(OATT_AT, ("oatt", [P, PAIRS, T]))
        yt, _ = place(R2, ("yt", [P, KR, T]))
        bon, gat, end = place(MIX_AT, ("bon", [P, KR, T]), ("gat", [P, KR, T]))
        assert end <= OATT_AT
        yn, ysq0, ysq1, LATE_AT = place(R1, ("yn", [P, KR, T]), ("ysq0", [P, T]), ("ysq1", [P, T]))
        ysq = [ysq0, ysq1]
        l0, l1, r0, r1, end = place(LATE_AT, ("late0", [P, KD, 512]), ("late1", [P, KD, 512]), ("mrow2", [2, 512]), ("mrow3", [2, 512]))
        late, late_row = [l0, l1], [r0, r1]
        assert end <= R2
        m1, x2, s0, s1, end = place(R2, ("m1", [P, KD, T]), ("x2", [P, KD, T]), ("sq2_0", sq), ("sq2_1", sq))
        sq2 = [s0, s1]
        assert end <= END
        acc, ahi, alo, draw, dhi0, dhi1, dlo0, dlo1, sil0, sil1, sil2, end = place(
            R2, ("acc", [P, KD, T]), ("ahi", [P, 4, T], F32R), ("alo", [P, 4, T], F32R), ("draw", [P, D]),
            ("dhi0", [P, D], F32R), ("dhi1", [P, D], F32R), ("dlo0", [P, D], F32R), ("dlo1", [P, D], F32R),
            ("sil0", [P, 364]), ("sil1", [P, 364]), ("sil2", [P, 364]))
        dhi, dlo, sil = [dhi0, dhi1], [dlo0, dlo1], [sil0, sil1, sil2]
        assert end <= END
        x3, _ = place(R1, ("x3", [P, KD, T]))
        s0, s1, _ = place(R2 + KD * T * 4, ("sq3_0", sq), ("sq3_1", sq))
        sq3 = [s0, s1]

        ps = ctx.enter_context(nc.psum_tensor("ps", [P, 8, 512], F32))

        ident = con[:, K_IDENT:K_IDENT + P]
        ones = con[:, K_ONES:K_ONES + P]
        block64 = con[:, K_BLOCK:K_BLOCK + P]
        gmask = con[:, K_GMASK:K_GMASK + P]
        eye2 = con[:, K_EYE2:K_EYE2 + C]
        eps_rms = con[:, K_EPS:K_EPS + 1]
        eps_ln = con[:, K_EPS + 1:K_EPS + 2]
        zero = con[:, K_EPS + 2:K_EPS + 3]
        cs = con[:, K_CS:K_CS + T]

        const_in, vec_in = sem("const_in"), sem("vec_in")
        x_in = [sem(f"x_in{c}") for c in range(3)]
        slab_in = [sem(f"slab_in{u}") for u in range(EARLY)]
        late_in = [sem(f"late_in{u}") for u in range(2)]
        mrow_ready, turned = sem("mrow_ready"), sem("turned")
        silu_c, waited, pool_waited = sem("silu_c"), sem("waited"), sem("pool_waited")
        slab_mm, mod_done = sem("slab_mm"), sem("mod_done")
        gains_done = sem("gains_done")
        w_in_sem = [sem(f"w_loaded{u}") for u in range(2)]
        w_hi, w_lo = sem("w_hi"), sem("w_lo")
        out_ready = [sem(f"out_ready{u}") for u in range(2)]
        bank_free = [sem(f"bank_free{u}") for u in range(2)]
        sq_ready, sq_used = sem("sq_ready"), sem("sq_used")
        root_ready, rstd_ready = sem("root_ready"), sem("rstd_ready")
        xn_ready, affine_done, hi_ready, lo_ready = sem("xn_ready"), sem("affine_done"), sem("hi_ready"), sem("lo_ready")
        v_step, s_step, g_step = sem("vector_step"), sem("scalar_step"), sem("pool_step")
        raw_zero, raw_ready, mix_done = sem("raw_zero"), sem("raw_ready"), sem("mix_done")
        shift_sent = sem("shift_sent")
        lora_in, lora_act, lora_mm, lora_ev = sem("lora_in"), sem("lora_act"), sem("lora_mm"), sem("lora_evicted")
        kk_raw, kk_sq, kk_mm, kk_root, pre_done = sem("kk_raw"), sem("kk_sq"), sem("kk_mm"), sem("kk_root"), sem("pre_done")
        state_in, state_ready = sem("state_in"), sem("state_ready")
        scan_out, bg_out = sem("scan_out"), sem("bg_out")
        bonus_sent, gate_sent = [sem(f"bonus_sent{u}") for u in range(2)], [sem(f"gate_sent{u}") for u in range(2)]
        bonus_raw, bonus_mm, bonus_done = sem("bonus_raw"), sem("bonus_mm"), sem("bonus_done")
        gate_mm, gate_ev = sem("gate_mm"), sem("gate_evicted")
        cin_in = [sem(f"cin_in{u}") for u in range(2)]
        y_sent = [sem(f"y_sent{u}") for u in range(2)]
        y_back, bg_back = sem("y_back"), sem("bg_back")
        c_cum, c_exp_a, c_exp, c_ab, c_k, c_v = sem("c_cum"), sem("c_exp_a"), sem("c_exp"), sem("c_ab"), sem("c_k"), sem("c_v")
        c_gmm, c_tr, c_gm, c_tm, c_lev = sem("c_gmm"), sem("c_tr"), sem("c_gm"), sem("c_tm"), sem("c_lev")
        c_xmm, c_xev, c_tmm, c_tev = sem("c_xmm"), sem("c_xev"), sem("c_tmm"), sem("c_tev")
        c_rmm, c_rev, c_umm, c_uev, c_ymm, c_yev, c_smm, c_sev = (sem(n) for n in (
            "c_rmm", "c_rev", "c_umm", "c_uev", "c_ymm", "c_yev", "c_smm", "c_sev"))
        c_uvv = sem("c_uvv")
        state_out = sem("state_out")
        mean_mm, yc_done, ysq_done, var_mm, y_root, y_norm, y_affine = (sem(n) for n in (
            "mean_mm", "yc_done", "ysq_done", "var_mm", "y_root", "y_norm", "y_affine"))
        rw_done = sem("rw_done")
        qkv_norm = sem("qkv_norm")
        past_in, aw_in = sem("past_in"), sem("aw_in")
        krope_put = sem("krope_put")
        ka_ev, kd_ev, kp_mm = sem("k_even_evicted"), sem("k_odd_evicted"), sem("k_mm")
        qp_mm, qa_ev, qd_ev = sem("q_mm"), sem("q_nope_evicted"), sem("q_rope_evicted")
        vp_mm, v_ev = sem("v_mm"), sem("v_evicted")
        s_mm, nmax, p_exp, p_norm = sem("scores_ready"), sem("negmax_ready"), sem("exp_ready"), sem("probs_ready")
        t_mm, t_ev, o_mm, o_ev = sem("probs_t_ready"), sem("probs_t_evicted"), sem("out_heads_ready"), sem("out_evicted")
        osplit_hi, osplit_lo = sem("osplit_hi"), sem("osplit_lo")
        x2_in, x2_done, x2_out = sem("x2_in"), sem("x2_done"), sem("x2_out")
        acc_zero = sem("acc_zero")
        d_in, d_hi, d_lo, down_ready = sem("d_loaded"), sem("d_hi"), sem("d_lo"), sem("down_ready")
        d_added = sem("down_added")
        sil_ready, act_hi, act_lo, prod_ready = sem("silu_ready"), sem("act_hi"), sem("act_lo"), sem("product_ready")
        krope_copied = sem("krope_copied")
        x3_in, y_done, stored = sem("x3_in"), sem("y_done"), sem("stored")

        def start_at_one(eng, *sems):
            for x in sems:
                eng.sem_inc(x, 1)

        OUT_M = (MLA_TILES + RW_TILES) // 2
        FF_M = OUT_M + KD // 2
        A_TILES = 2 * FF_M + 4 * GROUPS

        def segments(c):
            a, n = CH[c]
            b = a + n
            return [(a, n, 0)] if b <= TP else [(a, TP - a, 0), (TP, b - TP, 1)]

        def o_parts(h):
            return [(h[:, 0:KR, :], oatt[:, :, :]), (h[:, KR:KD, :], yt[:, :, :])]

        def load_weight(eng, m, u, first=False):
            if not first:
                eng.wait_ge(w_lo, 2 * m + u - 1)
            eng.dma_start(wraw[u][:, :, :].rearrange("p a b -> p (a b)"), d["w_tiles"][2 * m + u, :, :]).then_inc(w_in_sem[u], 16)

        def split_hi(act, m, u, first=False):
            act.wait_ge(w_in_sem[u], 16 * (m + 1))
            if not first:
                act.wait_ge(out_ready[u], 3 * m)
            nc.scalar.copy(whi[u][:, :, :], wraw[u][:, :, :]).then_inc(w_hi, 1)

        def split_lo(dve, m, u):
            dve.wait_ge(w_hi, 2 * m + u + 1)
            nc.vector.tensor_tensor(wlo[u][:, :, :], wraw[u][:, :, :], whi[u][:, :, :].bitcast(F32), ALU.subtract).then_inc(w_lo, 1)

        def project(pe, m, u, first=False, tokens=None):
            pe.wait_ge(w_lo, 2 * m + u + 1)
            for c, (a, n) in enumerate(CH):
                if tokens is not None:
                    pe.wait_ge(lo_ready, tokens + c + 1)
                if not first:
                    pe.wait_ge(bank_free[u], 3 * (m - 1) + c + 1)
                out = ps[:, 3 * u + c, 0:n]
                for k in range(KD):
                    for w, x in ((whi, hhi), (whi, hlo), (wlo, hhi)):
                        mm = nc.tensor.matmul(out, w[u][:, k, :], x[:, k, a:a + n],
                                              start=(k == 0 and w is whi and x is hhi), stop=(k == KD - 1 and w is wlo))
                mm.then_inc(out_ready[u], 1)

        NORMS = {"n1": (KD, D), "q": (KQ, QL), "kv": (KKV, KVL), "m": (KD, D), "n2": (KD, D), "f": (KD, D)}
        pieces, first_piece, chunk_no = 0, {}, {}
        for r, (name, (k, _)) in enumerate(NORMS.items()):
            chunk_no[name] = 3 * r
            first_piece[name] = pieces
            pieces += 3 * (-(-k // 4))

        def norm_squares(act, name, src, sqbuf, c):
            k = NORMS[name][0]
            per = -(-k // 4)
            a, n = CH[c]
            for j in range(per):
                piece = first_piece[name] + c * per + j
                k0, k1 = 4 * j, min(4 * j + 4, k)
                if piece >= 2:
                    act.wait_ge(sq_used, piece - 1)
                nc.scalar.activation(sqbuf[piece % 2][:, 0:k1 - k0, 0:n], src[:, k0:k1, a:a + n], ACT.Square).then_inc(sq_ready, 1)

        def norm_sum(pe, name, sqbuf, c):
            k = NORMS[name][0]
            per = -(-k // 4)
            a, n = CH[c]
            q = chunk_no[name] + c
            if q >= 2:
                pe.wait_ge(root_ready, q - 1)
            for j in range(per):
                piece = first_piece[name] + c * per + j
                pe.wait_ge(sq_ready, piece + 1)
                for i in range(4 * j, min(4 * j + 4, k)):
                    mm = nc.tensor.matmul(ps[:, 6 + q % 2, 0:n], ones, sqbuf[piece % 2][:, i - 4 * j, 0:n], start=(i == 0), stop=(i == k - 1))
                mm.then_inc(sq_used, 1)

        def norm_root(act, name, c):
            k, width = NORMS[name]
            per = -(-k // 4)
            a, n = CH[c]
            q = chunk_no[name] + c
            act.wait_ge(sq_used, first_piece[name] + (c + 1) * per)
            used = {"q": (xn_ready, c + 1), "kv": (qkv_norm, c + 1), "m": (qkv_norm, c + 4), "n2": (x2_done, c + 1), "f": (xn_ready, c + 4)}
            if name in used:
                act.wait_ge(*used[name])
            nc.scalar.activation(rstd[:, a:a + n], ps[:, 6 + q % 2, 0:n], ACT.Sqrt, bias=eps_rms, scale=1.0 / width).then_inc(root_ready, 1)

        def norm_recip(dve, name, c):
            a, n = CH[c]
            q = chunk_no[name] + c
            dve.wait_ge(root_ready, q + 1)
            nc.vector.reciprocal(rstd[:, a:a + n], rstd[:, a:a + n]).then_inc(rstd_ready, 1)
            dve.wait_ge(rstd_ready, q + 1)

        def over_tiles(ap2, k):
            return ap2.unsqueeze(1).broadcast_to([P, k, ap2.shape[1]])

        def interleave(one, steps_one, other, steps_other):
            done = 0
            for k in range(steps_one):
                next(one)
                while done * steps_one < (k + 1) * steps_other:
                    next(other)
                    done += 1
            assert next(one, None) is None and next(other, None) is None

        LAST_CHUNKS = range(CHUNKS - 4, CHUNKS + 1)

        block = ctx.enter_context(nc.Block())

        @block.sync
        def _(sp):
            for u in range(2):
                sp.sem_inc(y_sent[u], 16)
            sp.dma_start(con[:, :], d["table"]).then_inc(const_in, 16)
            sp.dma_start(vec[:, :], d["vectors"]).then_inc(vec_in, 16)
            ada = d["ada_w"].rearrange("(k p) n -> p k n", p=P)
            for c in range(EARLY):
                if c < 3:
                    a, n = CH[c]
                    sp.dma_start(x1[:, :, a:a + n], d["x_t"].rearrange("(k p) t -> p k t", p=P)[:, :, a:a + n]).then_inc(x_in[c], 16)
                sp.dma_start(slab[c][:, :, :], ada[:, :, 512 * c:512 * c + 512]).then_inc(slab_in[c], 16)
            load_weight(sp, 0, 0, first=True)
            load_weight(sp, 0, 1, first=True)
            with sp.Fori(1, OUT_M) as m:
                for u in range(2):
                    load_weight(sp, m, u)
            sp.wait_ge(raw_ready, RW_TILES)
            sp.dma_start(d["shift"], sh_out[:, :, :].rearrange("p a b -> p (a b)")).then_inc(stored, 16)
            for u in range(2):
                sp.wait_ge(out_ready[u], 3 * OUT_M)
            sp.dma_start(w2a2[:, :], d["w2a2"]).then_inc(lora_in, 16)
            sp.dma_start(g2[:, :], d["g2"]).then_inc(lora_in, 16)
            sp.wait_ge(qkv_norm, 6)
            sp.dma_start(d["ckv_out"].rearrange("(k p) t -> p k t", p=P), ckv[:, :, :]).then_inc(stored, 16)
            sp.dma_start(d["krope_out"], krope[64:96, :]).then_inc(stored, 16)

            def spill(field, j, row):
                sp.dma_start(d["scan"][0:CHUNKS, :, field, j, :].rearrange("c p t -> p c t"),
                             row[:, 0:TP].rearrange("p (c t) -> p c t", t=C)).then_inc(scan_out, 16)
                sp.dma_start(d["scan"][CHUNKS, :, field, j, :], row[:, SAMPLE_COL:TM]).then_inc(scan_out, 16)

            def spill_row(name, j, row, signal):
                sp.dma_start(d[name][j, :, 0:TP], row[:, 0:TP]).then_inc(signal, 16)
                sp.dma_start(d[name][j, :, TP:T], row[:, SAMPLE_COL:TM]).then_inc(signal, 16)

            sp.wait_ge(mix_done, RW_TILES)
            for j in range(KR):
                spill(3, j, mix[:, j, :])
                spill(5, j, mix[:, 2 * KR + j, :])
            for j in range(KR):
                sp.wait_ge(gate_ev, 3 * j + 3)
                spill_row("gate_rows", j, gout[j % 2], gate_sent[j % 2])
            for j in range(KR):
                sp.wait_ge(lora_ev, 2 * j + 1)
                spill(0, j, lw[:, j, :])
                sp.wait_ge(pre_done, j + 1)
                spill(1, j, kk[:, j, :])
                spill(2, j, bb[:, j, :])
                spill(4, j, mix[:, KR + j, :])
                sp.wait_ge(bonus_done, j + 1)
                spill_row("bonus_rows", j, bonus[j % 2], bonus_sent[j % 2])
            sp.wait_ge(scan_out, 16 * 2 * SF * KR)
            for u in range(2):
                sp.wait_ge(bonus_sent[u], 64)
                sp.wait_ge(gate_sent[u], 64)

            def load_chunk(i, u):
                sp.dma_start(cin[u][:, :, :, :].rearrange("p a b c -> p (a b c)"),
                             d["scan"][i, :, :, :, :].rearrange("p a b c -> p (a b c)")).then_inc(cin_in[u], 16)

            load_chunk(0, 0)
            load_chunk(1, 1)
            sp.dma_start(aw[:, :], d["att_w"][0, :, :]).then_inc(aw_in, 16)
            sp.dma_start(past[:, :, :], d["ckv_t"].rearrange("(k p) t -> p k t", p=P)).then_inc(past_in, 16)
            for e in range(2):
                sp.dma_start(kt[e][64:96, T:KEYS], d["krope_t"]).then_inc(past_in, 16)
            sp.dma_start(state[1][:, :, :].rearrange("p a b -> p (a b)"), d["state0"]).then_inc(state_in, 16)

            def store_y(i, u):
                sp.wait_ge(c_yev, i + 1 + 1)
                sp.dma_start(d["y_chunks"][i, :, :], ybuf[u][:, :, :].rearrange("p a b -> p (a b)")).then_inc(y_sent[u], 16)

            def pair_loads(hp, last=False):
                for x in range(4):
                    i, u = 4 * hp + x, x % 2
                    if x == 1 and not last:
                        sp.wait_ge(vp_mm, 7 * hp + 7)
                        sp.dma_start(aw[:, :], d["att_w"][hp + 1, :, :]).then_inc(aw_in, 16)
                    if not (last and x == 3):
                        sp.wait_ge(c_ab, i + 1)
                        sp.wait_ge(c_k, 2 * i + 2 + 1)
                        sp.wait_ge(c_v, i + 1)
                        load_chunk(i + 2, u)
                    store_y(i, u)

            with sp.Fori(0, PAIRS - 1) as hp:
                pair_loads(hp)
            pair_loads(PAIRS - 1, last=True)
            sp.wait_ge(c_sev, CHUNKS + 1)
            sp.dma_start(d["wkv"][0, :, :], state[0][:, :, :].rearrange("p a b -> p (a b)")).then_inc(state_out, 16)
            store_y(CHUNKS, 0)
            sp.wait_ge(c_sev, CHUNKS + 1 + 1)
            sp.dma_start(d["wkv"][1, :, :], state[1][:, :, :].rearrange("p a b -> p (a b)")).then_inc(state_out, 16)
            sp.wait_ge(o_ev, QTILES * PAIRS + 1)
            load_slab = lambda n: sp.dma_start(late[n % 2][:, :, :], ada[:, :, 512 * n:512 * n + 512]).then_inc(late_in[n % 2], 16)
            load_slab(EARLY)
            for u in range(2):
                sp.wait_ge(y_sent[u], 16 * (CHUNKS // 2 + 1 - u) + 16)
            for j in range(KR):
                sp.dma_start(yt[:, j, :].rearrange("p (c t) -> p c t", t=C),
                             d["y_chunks"][:, :, C * j:C * j + C].rearrange("c p t -> p c t")).then_inc(y_back, 16)
            load_slab(EARLY + 1)
            sp.dma_start(bon[:, :, :], d["bonus_rows"].rearrange("j p t -> p j t")).then_inc(bg_back, 16)
            sp.dma_start(gat[:, :, :], d["gate_rows"].rearrange("j p t -> p j t")).then_inc(bg_back, 16)
            sp.wait_ge(state_out, 32)
            for u in range(2):
                load_weight(sp, OUT_M, u)
            for n in range(EARLY + 2, SLABS):
                sp.wait_ge(slab_mm, n - 1)
                load_slab(n)
            sp.wait_ge(osplit_lo, 2)
            for c, (a, n) in enumerate(CH):
                sp.dma_start(x2[:, :, a:a + n], d["x_t"].rearrange("(k p) t -> p k t", p=P)[:, :, a:a + n]).then_inc(x2_in, 16)
            with sp.Fori(OUT_M + 1, FF_M) as m:
                for u in range(2):
                    load_weight(sp, m, u)
            for u in range(2):
                load_weight(sp, FF_M, u)
            for c, (a, n) in enumerate(CH):
                sp.wait_ge(x2_done, c + 1)
                sp.dma_start(d["x_mid"].rearrange("(k p) t -> p k t", p=P)[:, :, a:a + n], x2[:, :, a:a + n]).then_inc(x2_out, 16)
            sp.wait_ge(sq_used, first_piece["n2"] + 6)
            def load_down(g, u, first=False):
                if not first:
                    sp.wait_ge(d_lo, 2 * g + u)
                sp.dma_start(draw[:, :], d["w_down"][bass.ds((2 * g + u) * P, P), :]).then_inc(d_in, 16)

            load_weight(sp, FF_M + 1, 0)
            load_weight(sp, FF_M + 1, 1)
            load_down(0, 0, first=True)
            with sp.Fori(1, GROUPS) as g:
                for j in range(2):
                    for u in range(2):
                        load_weight(sp, 2 * g + FF_M + j, u)
                load_down(g - 1, 1)
                load_down(g, 0)
            load_down(GROUPS - 1, 1)
            for u in range(2):
                sp.wait_ge(out_ready[u], 3 * (FF_M + 2 * GROUPS))
            sp.wait_ge(x2_out, 48)
            sp.dma_start(x3[:, :, :], d["x_mid"].rearrange("(k p) t -> p k t", p=P)).then_inc(x3_in, 16)
            for c, (a, n) in enumerate(CH):
                sp.wait_ge(y_done, c + 1)
                sp.dma_start(d["y"].rearrange("(k p) t -> p k t", p=P)[:, :, a:a + n], x3[:, :, a:a + n]).then_inc(stored, 16)
            sp.wait_ge(stored, 16 * 6)
            sp.wait_ge(state_out, 32)

        @block.gpsimd
        def _(pool):
            step = Steps(pool, g_step)
            start_at_one(pool, c_k, c_lev)
            pool.wait_ge(lo_ready, 3)
            for u in range(2):
                nc.gpsimd.memset(raw[u][:, 0:1], 0.0).then_inc(raw_zero, 1)
            pool.wait_ge(scan_out, 16 * 2 * SF * KR)
            for u in range(2):
                pool.wait_ge(bonus_sent[u], 64)
                pool.wait_ge(gate_sent[u], 64)
            nc.gpsimd.memset(state[0][:, :, :], 0.0).then_inc(state_ready, 1)
            nc.gpsimd.memset(vz[:, :, :], 0.0).then_inc(state_ready, 1)
            nc.gpsimd.memset(cum[:, :, 0:1], 0.0).then_inc(state_ready, 1)

            def chunk_pool(i, u):
                pool.wait_ge(cin_in[u], 8 * i + 16 - 8 * u)
                pool.wait_ge(c_exp, i + 1 + 1)
                pool.wait_ge(c_tr, i + 1)
                for e in range(2):
                    r = slice(64 * e, 64 * e + 64)
                    k_half = bk[r, :, C * (1 - e):C * (1 - e) + C]
                    nc.gpsimd.tensor_tensor(k_half, cin[u][r, 4, :, :], pneg[r, :, :], ALU.mult).then_inc(c_k, 1)
                pool.wait_ge(c_gm, 2 * i + 2 + 1)
                pool.wait_ge(c_xmm, LEVELS * i + 1)
                for l in range(LEVELS):
                    for e in range(2):
                        r = slice(64 * e, 64 * e + 64)
                        lv = con[r, K_LEVEL + C * l:K_LEVEL + C * l + C].unsqueeze(1).broadcast_to([64, PAIRS, C])
                        nc.gpsimd.tensor_tensor(nlev[r, l, :, :], gm[r, e, :, 0:C], lv, ALU.mult).then_inc(c_lev, 1)
                pool.wait_ge(c_tm, i + 1 + 1)
                pool.wait_ge(c_ymm, i + 1)
                pool.sem_inc(pool_waited, 1)
                nc.gpsimd.tensor_copy(uv[0:64, :, 64:128], vz[0:64, :, 64:128]).then_inc(c_uvv, 1)
                nc.gpsimd.tensor_copy(uv[64:128, :, 0:64], vz[64:128, :, 0:64]).then_inc(c_uvv, 1)

            with pool.Fori(0, CHUNKS // 2) as i2:
                for u in range(2):
                    chunk_pool(2 * i2 + u, u)
            chunk_pool(CHUNKS, 0)
            pool.wait_ge(hi_ready, 6)
            pool.wait_ge(lo_ready, 6)
            nc.gpsimd.memset(acc[:, :, :], 0.0).then_inc(acc_zero, 1)

        @block.scalar
        def _(act):
            step = Steps(act, s_step)
            start_at_one(act, c_exp, c_tm, c_yev)
            act.wait_ge(vec_in, 16)
            nc.scalar.activation(cs_c[:, :, :].rearrange("p a b -> p (a b)"), vec[:, V_C:V_C + 16], ACT.Silu).then_inc(silu_c, 1)
            act.wait_ge(const_in, 16)

            def put_row(n, row, bank):
                act.wait_ge(slab_mm, n + 1)
                if n % EARLY >= 2:
                    act.wait_ge(turned, n - 1)
                nc.scalar.copy(row[n % 2][:, :], ps[0:2, bank + n % 2, :]).then_inc(mrow_ready, 1)

            def modulation(n, bank):
                act.wait_ge(turned, n + 1)
                for j in range(4):
                    ins = nc.scalar.activation(mod[:, 4 * n + j, :], ps[:, bank, 8 * (n % 4) + 2 * j:8 * (n % 4) + 2 * j + 2], ACT.Identity,
                                               bias=vec[:, V_ADAB + 4 * n + j:V_ADAB + 4 * n + j + 1])
                    if j < 3:
                        step.mark(ins)
                ins.then_inc(mod_done, 1)

            for c in range(3):
                act.wait_ge(x_in[c], 16)
                norm_squares(act, "n1", x1, sq1, c)
                norm_root(act, "n1", c)
                if c:
                    put_row(c - 1, mrow, 0)
            modulation(0, 2)
            for n in range(2, EARLY):
                put_row(n, mrow, 0)
                modulation(n - 1, 2)
            modulation(EARLY - 1, 2)

            def affine_split(src, c, gain, shift, count):
                act.wait_ge(xn_ready, count + 1)
                a, n = CH[c]
                for k in range(KD):
                    for b, w, s in segments(c):
                        step.mark(nc.scalar.activation(src[:, k, b:b + w], src[:, k, b:b + w], ACT.Identity,
                                                       bias=mod[:, shift + k, s:s + 1], scale=gains[:, gain, k, s:s + 1]))
                step.wait()
                nc.scalar.copy(hhi[:, :, a:a + n], src[:, :, a:a + n]).then_inc(hi_ready, 1)

            act.wait_ge(gains_done, 1)
            act.wait_ge(mod_done, EARLY)
            for c in range(3):
                affine_split(x1, c, 0, 0, c)

            def put_chunks(u, m, place):
                for c in range(3):
                    act.wait_ge(out_ready[u], 3 * m + c + 1)
                    parts = place(c)
                    for j, (dst, a, n) in enumerate(parts):
                        ins = nc.scalar.copy(dst, ps[:, 3 * u + c, a:a + n])
                        if j == len(parts) - 1:
                            ins.then_inc(bank_free[u], 1)
                        else:
                            step.mark(ins)

            split_hi(act, 0, 0, first=True)
            split_hi(act, 0, 1, first=True)
            act.wait_ge(lo_ready, 3)
            act.wait_ge(mod_done, EARLY)
            for n in range(MLA_TILES):
                m, u = n // 2, n % 2
                if n < KQ:
                    put_chunks(u, m, lambda c: [(cq[:, n, CH[c][0]:CH[c][0] + CH[c][1]], 0, CH[c][1])])
                elif n < KQ + KKV:
                    put_chunks(u, m, lambda c: [(ckv[:, n - KQ, CH[c][0]:CH[c][0] + CH[c][1]], 0, CH[c][1])])
                else:
                    put_chunks(u, m, lambda c: [(mix[:, 12, CH[c][0]:CH[c][0] + CH[c][1]], 0, CH[c][1])])
                split_hi(act, m + 1, u)

            def raw_place(u):
                def place(c):
                    a, n = CH[c]
                    if c < 2:
                        return [(raw[u][:, 1 + a:1 + a + n], 0, n)]
                    return [(raw[u][:, 1 + a:1 + TP], 0, TP - a), (raw[u][:, TM + 1 - TS:TM + 1], TP - a, TS)]
                return place

            def raw_rows(m, j, u, first=False):
                if not first:
                    act.wait_ge(mix_done, j - 1)
                step.mark(nc.scalar.copy(raw[u][:, TP + 1:TP + 2], vec[:, bass.ds(j + V_SHIFT, 1)]))
                put_chunks(u, m, raw_place(u))
                step.wait()
                act.wait_ge(bank_free[u], 3 * m + 3)
                step.mark(nc.scalar.copy(sh_out[:, bass.ds(j, 1), :].rearrange("p a b -> p (a b)"), raw[u][:, TP:TM + 1:TM - TP]))
                nc.scalar.mul(mix[:, bass.ds(j, 1), :].rearrange("p a b -> p (a b)"), raw[u][:, 0:TM],
                              vec[:, bass.ds(j + V_MU, 1)]).then_inc(raw_ready, 1)

            act.wait_ge(raw_zero, 2)
            RM = MLA_TILES // 2
            for u in range(2):
                raw_rows(RM, u, u, first=True)
                split_hi(act, RM + 1, u)
            with step.loop(RW_TILES // 2 - 2, 6) as i:
                for u in range(2):
                    raw_rows(i + RM + 1, 2 * i + 2 + u, u)
                    split_hi(act, i + RM + 2, u)
            for u in range(2):
                raw_rows(OUT_M - 1, RW_TILES - 2 + u, u)

            for u in range(2):
                act.wait_ge(out_ready[u], 3 * OUT_M)
            for name, src in (("q", cq), ("kv", ckv)):
                for c in range(3):
                    norm_squares(act, name, src, sq_lat, c)
                    norm_root(act, name, c)

            act.wait_ge(mix_done, RW_TILES)
            nc.scalar.activation(mix[0:64, 12, :], mix[0:64, 12, :], ACT.Tanh).then_inc(lora_act, 1)
            nc.scalar.activation(mix[:, 13, :], mix[:, 13, :], ACT.Sigmoid).then_inc(lora_act, 1)
            for j in range(KR):
                for s, (dst, vcol) in enumerate(((lw, V_W0), (bb, V_A0))):
                    act.wait_ge(lora_mm, 2 * j + s + 1)
                    nc.scalar.activation(dst[:, j, :].rearrange("p (c n) -> p c n", c=3), ps[:, 3 * s:3 * s + 3, 0:CM], ACT.Sigmoid,
                                         bias=vec[:, vcol + j:vcol + j + 1]).then_inc(lora_ev, 1)
            for j in range(KR):
                for c in range(3):
                    q = 3 * j + c
                    act.wait_ge(gate_mm, q + 1)
                    if c == 0 and j >= 2:
                        act.wait_ge(gate_sent[j % 2], 32)
                    nc.scalar.copy(gout[j % 2][:, CM * c:CM * c + CM], ps[:, 6 + q % 2, 0:CM]).then_inc(gate_ev, 1)
            for j in range(KR):
                act.wait_ge(kk_raw, j + 1)
                if j:
                    act.wait_ge(kk_mm, j)
                nc.scalar.activation(sqr[:, :], kk[:, j, :], ACT.Square).then_inc(kk_sq, 1)
                act.wait_ge(kk_mm, j + 1)
                if j:
                    act.wait_ge(pre_done, j)
                nc.scalar.activation(rn[:, :].rearrange("p (c n) -> p c n", c=3), ps[:, 0:3, 0:CM], ACT.Sqrt).then_inc(kk_root, 1)

            act.wait_ge(past_in, 48)
            act.wait_ge(krope_put, 1)
            for e in range(2):
                nc.scalar.copy(kt[e][64:96, 0:T], krope[64:96, :]).then_inc(krope_copied, 1)

            def chunk_scalar(i, u):
                act.wait_ge(c_cum, i + 1)
                act.wait_ge(c_k, 2 * i + 1)
                act.wait_ge(c_sev, i + 1)
                nc.scalar.activation(pinc[:, :, :], cum[:, :, :], ACT.Exp, scale=-DECAY).then_inc(c_exp_a, 1)
                nc.scalar.activation(pneg[:, :, :], cum[:, :, 1:C + 1], ACT.Exp, scale=DECAY).then_inc(c_exp, 1)
                yield
                act.wait_ge(c_tr, i + 1)
                nc.scalar.copy(vv[:, :, :, :], cin[u][:, 5, :, :].unsqueeze(2).broadcast_to([P, PAIRS, 2, C])).then_inc(c_v, 1)
                yield
                yield
                act.wait_ge(c_tr, i + 1 + 1)
                act.wait_ge(c_smm, i + 1)
                step.mark(nc.scalar.copy(bktm[:, :, :].rearrange("p a b -> p (a b)"), ps[:, WB, :]))
                v3 = ps[:, WB + 1, :].rearrange("p (a b) -> p a b", a=PAIRS)
                step.mark(nc.scalar.copy(vz[0:64, :, 64:128], v3[0:64, :, 64:128]))
                nc.scalar.copy(vz[64:128, :, 0:64], v3[64:128, :, 0:64]).then_inc(c_tm, 1)
                yield
                yield
                for l in range(LEVELS - 1):
                    act.wait_ge(c_xmm, LEVELS * i + l + 2 + 1)
                    act.wait_ge(c_tmm, (LEVELS - 1) * i + l + 1)
                    nc.scalar.copy(xt[:, :, :].rearrange("p a b -> p (a b)"), ps[:, WB, 0:PAIRS * C]).then_inc(c_xev, 1)
                    yield
                    yield
                act.wait_ge(c_rmm, i + 1)
                nc.scalar.mul(rhs[:, :, :].rearrange("p a b -> p (a b)"), ps[:, WB, 0:PAIRS * C], -1.0).then_inc(c_rev, 1)
                yield
                act.wait_ge(c_umm, i + 1 + 1)
                u3 = ps[:, WB + 1, 0:PAIRS * DH].rearrange("p (a b) -> p a b", a=PAIRS)
                act.wait_ge(c_ymm, i + 1)
                step.mark(nc.scalar.copy(uv[0:64, :, 0:64], u3[0:64, :, :]))
                nc.scalar.copy(uv[64:128, :, 64:128], u3[64:128, :, :]).then_inc(c_uev, 1)
                yield
                yield
                act.wait_ge(c_ymm, i + 1 + 1)
                act.wait_ge(y_sent[u], 8 * i - 8 * u + 16)
                nc.scalar.copy(ybuf[u][:, :, :].rearrange("p a b -> p (a b)"), ps[:, WB + 1, 0:PAIRS * C]).then_inc(c_yev, 1)
                yield

            def attend_scalar(hp):
                for l, (dst, n) in enumerate(K_CHUNKS):
                    act.wait_ge(kp_mm, 7 * hp + l + 1)
                    nc.scalar.copy(kt[0][0:64, dst:dst + n], ps[0:64, l % 4, 0:n]).then_inc(ka_ev, 1)
                    yield
                for e in range(2):
                    for c, (a, n) in enumerate(CH):
                        l = 3 * e + c
                        act.wait_ge(qp_mm, 6 * hp + l + 1)
                        nc.scalar.mul(qt[e][0:64, a:a + n], ps[0:64, 4 + l % 2, 0:n], SCALE).then_inc(qa_ev, 1)
                        yield
                for g, tiles in enumerate(V_GROUPS):
                    act.wait_ge(vp_mm, 7 * hp + g + 1)
                    rows = TS if tiles == [8] else P
                    nc.scalar.copy(vt[0:rows, tiles[0]:tiles[-1] + 1, :],
                                   ps[0:rows, (7 + g) % 4, 0:P * len(tiles)].rearrange("p (a b) -> p a b", b=P)).then_inc(v_ev, 1)
                    yield
                for kind, jb, g in JOB_UNITS:
                    if kind == "scores":
                        exponentials(jb, hp)
                    if kind == "turn":
                        put_probs(jb, g, hp)
                    yield

            def exponentials(jb, hp):
                u = jb % 2
                act.wait_ge(nmax, JOBS * hp + jb + 1)
                act.wait_ge(t_mm, T_GROUPS * hp + (T_FIRST[jb - 1] if jb >= 2 else 0) + 1)
                if jb < PJOBS:
                    n = P * (jb // 2 + 1)
                    dst, src, r = probs[u][:, 0:n], ps[:, 2 * u:2 * u + 2, :].rearrange("p a b -> p (a b)")[:, 0:n], slice(0, P)
                else:
                    dst, src, r = probs[u][0:TS, :].rearrange("p (a b) -> p a b", a=6), ps[0:TS, 0:6, 0:352], slice(0, TS)
                nc.scalar.activation(dst, src, ACT.Exp, bias=sm[r, 0, u:u + 1], accum_out=sm[r, 1, u:u + 1]).then_inc(p_exp, 1)

            def put_probs(jb, g, hp):
                u = jb % 2
                t0, t1 = T_PLAN[jb][g]
                act.wait_ge(o_mm, JOBS * hp + max(jb - 1, 0) + 1)
                act.wait_ge(t_mm, T_GROUPS * hp + T_FIRST[jb] + g + 1 + 1)
                w = P if jb < PJOBS else TS
                if jb >= PJOBS and g == 0:
                    step.mark(nc.scalar.copy(pt[u][0:TS, 0:w], ps[0:TS, 4, 0:w]))
                    nc.scalar.copy(pt[u][:, w:t1 * w], ps[:, 4, w:t1 * w]).then_inc(t_ev, 1)
                else:
                    nc.scalar.copy(pt[u][:, t0 * w:t1 * w], ps[:, 4, 0:(t1 - t0) * w]).then_inc(t_ev, 1)

            with step.loop(PAIRS - 1, 2 + 4 * 3) as hp:
                interleave(attend_scalar(hp), ATT_UNITS, (z for x in range(4) for z in chunk_scalar(4 * hp + x, x % 2)), 4 * CHUNK_UNITS)
            interleave(attend_scalar(PAIRS - 1), ATT_UNITS, (z for i in LAST_CHUNKS for z in chunk_scalar(i, i % 2)), 5 * CHUNK_UNITS)

            def y_squares(j):
                act.wait_ge(yc_done, j + 1)
                if j >= 2:
                    act.wait_ge(var_mm, j - 1)
                nc.scalar.activation(ysq[j % 2][:, :], yt[:, j, :], ACT.Square).then_inc(ysq_done, 1)

            for j in range(KR):
                if j < 2:
                    y_squares(j)
                put_row(EARLY + j, late_row, 4)
                if j:
                    modulation(EARLY + j - 1, 6)
            for j in range(KR):
                act.wait_ge(var_mm, j + 1)
                for c, (a, n) in enumerate(CH):
                    ins = nc.scalar.activation(yn[:, j, a:a + n], ps[:, 3 + c, 0:n], ACT.Sqrt, bias=eps_ln, scale=1.0 / DH)
                    if c < 2:
                        step.mark(ins)
                ins.then_inc(y_root, 1)
                if j + 2 < KR:
                    y_squares(j + 2)
                put_row(EARLY + KR + j, late_row, 0)
                modulation(EARLY + KR + j - 1, 6)
            modulation(SLABS - 1, 6)
            for j in range(KR):
                act.wait_ge(y_norm, j + 1)
                nc.scalar.activation(yt[:, j, :], yt[:, j, :], ACT.Identity, bias=vec[:, V_LB + j:V_LB + j + 1],
                                     scale=vec[:, V_LG + j:V_LG + j + 1]).then_inc(y_affine, 1)

            split_hi(act, OUT_M, 0)
            split_hi(act, OUT_M, 1)

            act.wait_ge(o_ev, QTILES * PAIRS + 1)
            act.wait_ge(rw_done, KR)
            act.wait_ge(mod_done, SLABS)
            for dst, src in o_parts(hhi):
                nc.scalar.copy(dst, src).then_inc(osplit_hi, 1)

            act.wait_ge(osplit_lo, 2)
            for n in range(KD):
                m, u = OUT_M + n // 2, n % 2
                put_chunks(u, m, lambda c: [(m1[:, n, CH[c][0]:CH[c][0] + CH[c][1]], 0, CH[c][1])])
                split_hi(act, m + 1, u)
            for u in range(2):
                act.wait_ge(bank_free[u], 3 * FF_M)
            for c in range(3):
                norm_squares(act, "m", m1, sq2, c)
                norm_root(act, "m", c)
            for c in range(3):
                act.wait_ge(x2_done, c + 1)
                norm_squares(act, "n2", x2, sq2, c)
                norm_root(act, "n2", c)
            for c in range(3):
                affine_split(m1, c, 2, 24, 3 + c)

            def down_hi(g, u):
                act.wait_ge(d_in, 16 * (2 * g + u + 1))
                act.wait_ge(down_ready, 24 * g + 1)
                nc.scalar.copy(dhi[u][:, :], draw[:, :]).then_inc(d_hi, 1)

            def gate(g, slot, j, first=False, last=False):
                m = 2 * g + FF_M + j
                q = 6 * g + 3 * j
                for c, (a, n) in enumerate(CH):
                    act.wait_ge(out_ready[0], 3 * m + c + 1)
                    if not (first and j == 0):
                        act.wait_ge(act_lo, q + c - 2)
                    nc.scalar.activation(sil[c][:, 0:n], ps[:, c, 0:n], ACT.Silu).then_inc(sil_ready, 1)
                if not last:
                    split_hi(act, m + 1, 0)
                if not first:
                    act.wait_ge(down_ready, 24 * (g - 1) + 1)
                for c, (a, n) in enumerate(CH):
                    act.wait_ge(prod_ready, q + c + 1)
                    nc.scalar.copy(ahi[:, slot + j, a:a + n], sil[c][:, 0:n]).then_inc(act_hi, 1)
                if not last:
                    split_hi(act, m + 1, 1)

            act.wait_ge(x2_out, 48)
            gate(0, 0, 0, first=True)
            gate(0, 0, 1, first=True)

            def group(g, slot, last=False):
                gate(g, slot, 0)
                down_hi(g - 1, 0)
                down_hi(g - 1, 1)
                gate(g, slot, 1, last=last)

            with act.Fori(0, (GROUPS - 3) // 2) as it:
                group(2 * it + 1, 2)
                group(2 * it + 2, 0)
            group(GROUPS - 2, 2)
            group(GROUPS - 1, 0, last=True)
            down_hi(GROUPS - 1, 0)
            down_hi(GROUPS - 1, 1)

            act.wait_ge(d_added, 24 * GROUPS + 1)
            for c in range(3):
                norm_squares(act, "f", acc, sq3, c)
                norm_root(act, "f", c)

        @block.vector
        def _(dve):
            step = Steps(dve, v_step)
            start_at_one(dve, c_gm, c_sev, o_ev, qd_ev, d_added)
            dve.wait_ge(vec_in, 16)
            dve.wait_ge(const_in, 16)
            step.mark(nc.vector.tensor_scalar(omm[:, :], vec[:, V_MU:V_MU + 14], -1.0, 1.0, ALU.mult, ALU.add))
            step.mark(nc.vector.tensor_scalar(oma[:, :], vec[:, V_KA:V_KA + 4], -1.0, 1.0, ALU.mult, ALU.add))

            def times_rstd(dst, src, c):
                a, n = CH[c]
                nc.vector.tensor_tensor(dst[:, :, a:a + n], src[:, :, a:a + n], over_tiles(rstd[:, a:a + n], KD), ALU.mult).then_inc(xn_ready, 1)

            def rest(src, c, count):
                a, n = CH[c]
                dve.wait_ge(hi_ready, count + 1)
                nc.vector.tensor_tensor(hlo[:, :, a:a + n], src[:, :, a:a + n], hhi[:, :, a:a + n].bitcast(F32), ALU.subtract).then_inc(lo_ready, 1)

            for c in range(3):
                norm_recip(dve, "n1", c)
                dve.wait_ge(x_in[c], 16)
                times_rstd(x1, x1, c)

            def gain(which, at0, plus, last=False):
                g = vec[:, V_NORM + 8 * which:V_NORM + 8 * which + 8].unsqueeze(2).broadcast_to([P, 8, 2])
                ins = nc.vector.scalar_tensor_tensor(out=gains[:, which, :, :], in0=mod[:, at0:at0 + 8, :], scalar=plus, in1=g,
                                                     op0=ALU.add, op1=ALU.mult)
                ins.then_inc(gains_done, 1)

            dve.wait_ge(mod_done, EARLY)
            gain(0, 8, 1.0)
            split_lo(dve, 0, 0)
            split_lo(dve, 0, 1)
            for c in range(3):
                rest(x1, c, c)

            for n in range(MLA_TILES):
                m, u = n // 2, n % 2
                split_lo(dve, m + 1, u)
                if n == MLA_TILES - 1:
                    dve.wait_ge(bank_free[u], 3 * m + 3)
                    step.mark(nc.vector.tensor_tensor(krope[64:96, :], mix[64:96, 12, 0:T], cs[64:96, :], ALU.mult))
                    step.done(nc.vector.tensor_tensor(mix[64:96, 13, 0:T], mix[96:128, 12, 0:T], cs[96:128, :], ALU.mult))
                    nc.vector.tensor_tensor(krope[64:96, :], krope[64:96, :], mix[64:96, 13, 0:T], ALU.add).then_inc(krope_put, 1)
                    dve.wait_ge(krope_put, 1)

            def shift_mix(j, u):
                dve.wait_ge(raw_ready, j + 1)
                m2 = mix[:, bass.ds(j, 1), :].rearrange("p a b -> p (a b)")
                nc.vector.scalar_tensor_tensor(out=m2, in0=raw[u][:, 1:TM + 1], scalar=omm[:, bass.ds(j, 1)], in1=m2,
                                               op0=ALU.mult, op1=ALU.add).then_inc(mix_done, 1)

            step.wait()
            for u in range(2):
                split_lo(dve, MLA_TILES // 2 + 1, u)
                shift_mix(u, u)
            with dve.Fori(0, RW_TILES // 2 - 2) as i:
                for u in range(2):
                    split_lo(dve, i + MLA_TILES // 2 + 2, u)
                    shift_mix(2 * i + 2 + u, u)
            for u in range(2):
                shift_mix(RW_TILES - 2 + u, u)

            for name, src, k, v0 in (("q", cq, KQ, V_QG), ("kv", ckv, KKV, V_KVG)):
                for c, (a, n) in enumerate(CH):
                    norm_recip(dve, name, c)
                    dve.wait_ge(sq_used, first_piece[name] + c + 1)
                    for t in range(k):
                        ins = nc.vector.scalar_tensor_tensor(out=src[:, t, a:a + n], in0=src[:, t, a:a + n], scalar=vec[:, v0 + t:v0 + t + 1],
                                                             in1=rstd[:, a:a + n], op0=ALU.mult, op1=ALU.mult)
                        if t < k - 1:
                            step.mark(ins)
                        else:
                            ins.then_inc(qkv_norm, 1)

            thirds = lambda ap: ap.rearrange("p (c n) -> p c n", c=3)
            dve.wait_ge(mix_done, RW_TILES)
            for u in range(2):
                dve.wait_ge(out_ready[u], 3 * OUT_M)
            for j in range(KR):
                nc.vector.tensor_scalar(kk[:, j, :], mix[:, KR + j, :], vec[:, V_KK + j:V_KK + j + 1], None, ALU.mult).then_inc(kk_raw, 1)
                dve.wait_ge(lora_ev, 2 * j + 2)
                dve.wait_ge(kk_raw, j + 1)
                step.done(nc.vector.tensor_scalar(tmp[:, :], bb[:, j, :], vec[:, V_KA + j:V_KA + j + 1], oma[:, j:j + 1], ALU.mult, ALU.add))
                step.done(nc.vector.tensor_tensor(mix[:, KR + j, :], mix[:, KR + j, :], tmp[:, :], ALU.mult))
                if j >= 2:
                    dve.wait_ge(bonus_sent[j % 2], 32)
                dve.wait_ge(qkv_norm, 6)
                nc.vector.scalar_tensor_tensor(out=bonus[j % 2][:, :], in0=mix[:, j, :], scalar=vec[:, V_RK + j:V_RK + j + 1], in1=mix[:, KR + j, :],
                                               op0=ALU.mult, op1=ALU.mult).then_inc(bonus_raw, 1)
                dve.wait_ge(kk_root, j + 1)
                step.done(nc.vector.tensor_scalar(rn[:, :], rn[:, :], 1e-12, None, ALU.max))
                step.done(nc.vector.reciprocal(rn[:, :], rn[:, :]))
                dve.wait_ge(kk_sq, j + 1)
                step.done(nc.vector.tensor_tensor(kk[:, j, :], kk[:, j, :], rn[:, :], ALU.mult))
                nc.vector.tensor_tensor(bb[:, j, :], bb[:, j, :], kk[:, j, :], ALU.mult).then_inc(pre_done, 1)
                dve.wait_ge(bonus_mm, j + 1)
                nc.vector.tensor_tensor(thirds(bonus[j % 2][:, :]), ps[:, 3:6, 0:CM], thirds(mix[:, 2 * KR + j, :]), ALU.mult).then_inc(bonus_done, 1)

            def chunk_vector(i, u, s):
                f = cin[u]
                dve.wait_ge(cin_in[u], 8 * i + 16 - 8 * u)
                dve.wait_ge(c_exp, i + 1)
                for p in range(PAIRS):
                    ins = nc.vector.tensor_tensor_scan(cum[:, p, 1:C + 1], ones[:, 0:C], f[:, 0, p, :], 0.0, ALU.mult, ALU.add)
                    if p < PAIRS - 1:
                        step.mark(ins)
                    else:
                        ins.then_inc(c_cum, 1)
                yield
                dve.wait_ge(c_exp, i + 1 + 1)
                dve.wait_ge(c_ymm, i + 1)
                step.mark(nc.vector.tensor_tensor(ar[:, :, 0:C], f[:, 1, :, :], pinc[:, :, 0:C], ALU.mult))
                step.mark(nc.vector.tensor_tensor(ar[:, :, C:2 * C], f[:, 3, :, :], pinc[:, :, 1:C + 1], ALU.mult))
                step.mark(nc.vector.tensor_tensor(bk[0:64, :, 0:C], f[0:64, 2, :, :], pneg[0:64, :, :], ALU.mult))
                nc.vector.tensor_tensor(bk[64:128, :, C:2 * C], f[64:128, 2, :, :], pneg[64:128, :, :], ALU.mult).then_inc(c_ab, 1)
                yield
                dve.wait_ge(c_lev, 2 * LEVELS * i + 1)
                for e in range(2):
                    dve.wait_ge(c_gmm, 2 * i + e + 1)
                    nc.vector.tensor_tensor(gm[:, e, :, :], ps[:, WB + e, :].rearrange("p (a b) -> p a b", a=PAIRS),
                                            gmask.unsqueeze(1).broadcast_to([P, PAIRS, P]), ALU.mult).then_inc(c_gm, 1)
                yield
                yield
                eye4 = eye2.unsqueeze(1).broadcast_to([P, PAIRS, C])
                dve.wait_ge(c_lev, 2 * LEVELS * i + 2 + 1)
                dve.wait_ge(c_umm, i + 1)
                step.mark(nc.vector.tensor_tensor(tt[:, 0, :, :], nlev[:, 0, :, :], eye4, ALU.add))
                dve.wait_ge(c_xmm, LEVELS * i + 1 + 1)
                nc.vector.tensor_tensor(tt[:, 1, :, :], ps[:, WB, 0:PAIRS * C].rearrange("p (a b) -> p a b", a=PAIRS), eye4, ALU.add).then_inc(c_tev, 1)
                step.wait()
                yield
                for l in range(1, LEVELS):
                    yield
                    n = 2 if l < LEVELS - 1 else 1
                    dve.wait_ge(c_tev, LEVELS * i + l)
                    dve.wait_ge(c_tmm, (LEVELS - 1) * i + l + 1)
                    t2 = tt[:, 0:n, :, :].rearrange("p a b c -> p (a b c)")
                    nc.vector.tensor_tensor(t2, t2, ps[:, WB + 1, 0:n * PAIRS * C], ALU.add).then_inc(c_tev, 1)
                    yield
                yield
                yield
                yield
                dve.wait_ge(c_smm, i + 1 + 1)
                dve.wait_ge(c_ymm, i + 1 + 1)
                step.done(nc.vector.tensor_tensor(s[:, :, :], s[:, :, :], ps[:, WB, 0:PAIRS * DH].rearrange("p (a b) -> p a b", a=PAIRS), ALU.add))
                nc.vector.tensor_tensor(s[:, :, :], s[:, :, :], pinc[:, :, C:C + 1].broadcast_to([P, PAIRS, DH]), ALU.mult).then_inc(c_sev, 1)
                yield

            def job_max(jb, hp):
                u = jb % 2
                dve.wait_ge(s_mm, JOBS * hp + jb + 1)
                if jb < PJOBS:
                    n = P * (jb // 2 + 1)
                    scores = ps[:, 2 * u:2 * u + 2, :].rearrange("p a b -> p (a b)")
                    step.done(nc.vector.memset(scores[0:C, n - C:n], NEG))
                    nc.vector.tensor_reduce(sm[:, 0, u:u + 1], scores[:, 0:n], AX_X, ALU.max, negate=True).then_inc(nmax, 1)
                else:
                    nc.vector.tensor_reduce(sm[0:TS, 0, u:u + 1], ps[0:TS, 0:6, 0:352], mybir.AxisListType.XY, ALU.max, negate=True).then_inc(nmax, 1)

            def job_norm(jb, hp):
                u = jb % 2
                r = slice(0, P if jb < PJOBS else TS)
                n = P * (jb // 2 + 1) if jb < PJOBS else TS + PAST
                dve.wait_ge(p_exp, JOBS * hp + jb + 1)
                step.done(nc.vector.reciprocal(sm[r, 2, u:u + 1], sm[r, 1, u:u + 1]))
                nc.vector.tensor_scalar(probs[u][r, 0:n], probs[u][r, 0:n], sm[r, 2, u:u + 1], None, ALU.mult).then_inc(p_norm, 1)

            def put_out(i, hp):
                a, w = (P * i, P) if i < QTILES - 1 else (TP, TS)
                dve.wait_ge(o_mm, JOBS * hp + 2 * i + 2 + 1)
                nc.vector.tensor_copy(oatt[:, bass.ds(hp, 1), a:a + w].rearrange("p a b -> p (a b)"), ps[:, 5, 0:w]).then_inc(o_ev, 1)

            def attend_vector(hp):
                for l, (dst, n) in enumerate(K_CHUNKS):
                    dve.wait_ge(kp_mm, 7 * hp + l + 1)
                    nc.vector.tensor_copy(kt[1][0:64, dst:dst + n], ps[64:128, l % 4, 0:n]).then_inc(kd_ev, 1)
                    yield
                for e in range(2):
                    for c, (a, n) in enumerate(CH):
                        l = 3 * e + c
                        dve.wait_ge(qp_mm, 6 * hp + l + 1)
                        dve.wait_ge(qd_ev, 6 * hp + l + 1)
                        step.mark(nc.vector.scalar_tensor_tensor(out=rtmp[0][64:96, 0:n], in0=ps[64:96, 4 + l % 2, 0:n], scalar=SCALE,
                                                                 in1=cs[64:96, a:a + n], op0=ALU.mult, op1=ALU.mult))
                        step.done(nc.vector.scalar_tensor_tensor(out=rtmp[1][64:96, 0:n], in0=ps[96:128, 4 + l % 2, 0:n], scalar=SCALE,
                                                                 in1=cs[96:128, a:a + n], op0=ALU.mult, op1=ALU.mult))
                        nc.vector.tensor_tensor(qt[e][64:96, a:a + n], rtmp[0][64:96, 0:n], rtmp[1][64:96, 0:n], ALU.add).then_inc(qd_ev, 1)
                        yield
                for g in V_GROUPS:
                    yield
                pending = []
                for kind, jb, g in JOB_UNITS:
                    if kind == "scores":
                        for x in pending:
                            job_norm(x, hp)
                        pending = [jb]
                        job_max(jb, hp)
                    else:
                        for x in pending:
                            job_norm(x, hp)
                        pending = []
                    if kind == "values" and jb % 2:
                        put_out(jb // 2, hp)
                    yield

            dve.wait_ge(state_ready, 3)
            with step.loop(PAIRS - 1, 12 + PJOBS + JOBS + 4 * 8) as hp:
                interleave(attend_vector(hp), ATT_UNITS, (z for x in range(4) for z in chunk_vector(4 * hp + x, x % 2, state[0])), 4 * CHUNK_UNITS)
            dve.wait_ge(state_in, 16)
            interleave(attend_vector(PAIRS - 1), ATT_UNITS, (z for i in LAST_CHUNKS for z in chunk_vector(i, i % 2, state[i // CHUNKS])), 5 * CHUNK_UNITS)

            dve.wait_ge(y_back, 16 * KR)
            for j in range(KR):
                for c, (a, n) in enumerate(CH):
                    dve.wait_ge(mean_mm, 3 * j + c + 1)
                    ins = nc.vector.scalar_tensor_tensor(out=yt[:, j, a:a + n], in0=ps[:, c, 0:n], scalar=-1.0 / DH, in1=yt[:, j, a:a + n],
                                                         op0=ALU.mult, op1=ALU.add)
                    if c < 2:
                        step.mark(ins)
                ins.then_inc(yc_done, 1)
            step.wait()
            dve.wait_ge(yc_done, KR)
            for j in range(KR):
                dve.wait_ge(y_root, j + 1)
                step.done(nc.vector.reciprocal(yn[:, j, :], yn[:, j, :]))
                dve.wait_ge(ysq_done, j + 1)
                nc.vector.tensor_tensor(yt[:, j, :], yt[:, j, :], yn[:, j, :], ALU.mult).then_inc(y_norm, 1)
            dve.wait_ge(bg_back, 32)
            for j in range(KR):
                dve.wait_ge(y_affine, j + 1)
                step.done(nc.vector.tensor_tensor(yt[:, j, :], yt[:, j, :], bon[:, j, :], ALU.add))
                nc.vector.tensor_tensor(yt[:, j, :], yt[:, j, :], gat[:, j, :], ALU.mult).then_inc(rw_done, 1)

            dve.wait_ge(mod_done, SLABS)
            gain(1, 16, 0.0)
            gain(2, 32, 1.0)
            gain(3, 40, 0.0)
            dve.wait_ge(o_ev, QTILES * PAIRS + 1)
            dve.wait_ge(rw_done, KR)
            for i, (dst, src) in enumerate(o_parts(hlo)):
                dve.wait_ge(osplit_hi, i + 1)
                hi = o_parts(hhi)[i][0].bitcast(F32)
                nc.vector.tensor_tensor(dst, src, hi, ALU.subtract).then_inc(osplit_lo, 1)

            split_lo(dve, OUT_M, 0)
            split_lo(dve, OUT_M, 1)
            for n in range(KD):
                split_lo(dve, OUT_M + 1 + n // 2, n % 2)

            def residual(dst, src, which, c, signal):
                parts = [(k, b, w, s) for k in range(KD) for b, w, s in segments(c)]
                for i, (k, b, w, s) in enumerate(parts):
                    ins = nc.vector.scalar_tensor_tensor(out=dst[:, k, b:b + w], in0=src[:, k, b:b + w], scalar=gains[:, which, k, s:s + 1],
                                                         in1=dst[:, k, b:b + w], op0=ALU.mult, op1=ALU.add)
                    if i < len(parts) - 1:
                        step.mark(ins)
                    else:
                        ins.then_inc(signal, 1)

            dve.wait_ge(x2_in, 48)
            for c, (a, n) in enumerate(CH):
                norm_recip(dve, "m", c)
                step.done(nc.vector.tensor_tensor(m1[:, :, a:a + n], m1[:, :, a:a + n], over_tiles(rstd[:, a:a + n], KD), ALU.mult))
                residual(x2, m1, 1, c, x2_done)
            step.wait()
            dve.wait_ge(x2_done, 3)
            for c in range(3):
                norm_recip(dve, "n2", c)
                times_rstd(m1, x2, c)
            for c in range(3):
                rest(m1, c, 3 + c)

            def down_lo(g, u):
                dve.wait_ge(d_hi, 2 * g + u + 1)
                nc.vector.tensor_tensor(dlo[u][:, :], draw[:, :], dhi[u][:, :].bitcast(F32), ALU.subtract).then_inc(d_lo, 1)

            def product(g, slot, j, last=False):
                m = 2 * g + FF_M + j
                q = 6 * g + 3 * j
                if not last:
                    split_lo(dve, m + 1, 0)
                for c, (a, n) in enumerate(CH):
                    dve.wait_ge(sil_ready, q + c + 1)
                    dve.wait_ge(out_ready[1], 3 * m + c + 1)
                    nc.vector.tensor_tensor(sil[c][:, 0:n], sil[c][:, 0:n], ps[:, 3 + c, 0:n], ALU.mult).then_inc(prod_ready, 1)
                for c, (a, n) in enumerate(CH):
                    dve.wait_ge(act_hi, q + c + 1)
                    nc.vector.tensor_tensor(alo[:, slot + j, a:a + n], sil[c][:, 0:n], ahi[:, slot + j, a:a + n].bitcast(F32),
                                            ALU.subtract).then_inc(act_lo, 1)
                if not last:
                    split_lo(dve, m + 1, 1)

            def add_down(g):
                for x in range(24):
                    k, (a, n) = x // 3, CH[x % 3]
                    dve.wait_ge(down_ready, 24 * g + x + 1 + 1)
                    nc.vector.tensor_tensor(acc[:, k, a:a + n], acc[:, k, a:a + n], ps[:, 6 + x % 2, 0:n], ALU.add).then_inc(d_added, 1)

            def group(g, slot, last=False):
                product(g, slot, 0)
                down_lo(g - 1, 0)
                down_lo(g - 1, 1)
                product(g, slot, 1, last=last)
                dve.wait_ge(d_added, 24 * (g - 1) + 1)
                add_down(g - 1)

            dve.wait_ge(acc_zero, 1)
            product(0, 0, 0)
            product(0, 0, 1)
            with dve.Fori(0, (GROUPS - 3) // 2) as it:
                group(2 * it + 1, 2)
                group(2 * it + 2, 0)
            group(GROUPS - 2, 2)
            group(GROUPS - 1, 0, last=True)
            down_lo(GROUPS - 1, 0)
            down_lo(GROUPS - 1, 1)
            dve.wait_ge(d_added, 24 * (GROUPS - 1) + 1)
            add_down(GROUPS - 1)

            dve.wait_ge(d_added, 24 * GROUPS + 1)
            dve.wait_ge(x3_in, 16)
            for c, (a, n) in enumerate(CH):
                norm_recip(dve, "f", c)
                dve.wait_ge(sq_used, first_piece["f"] + 2 * c + 2)
                step.done(nc.vector.tensor_tensor(acc[:, :, a:a + n], acc[:, :, a:a + n], over_tiles(rstd[:, a:a + n], KD), ALU.mult))
                residual(x3, acc, 3, c, y_done)

        @block.tensor
        def _(pe):
            def before_small():
                pe.sem_inc(waited, 1)

            start_at_one(pe, c_tr, c_xmm, c_ymm, c_smm, c_tmm, c_umm, t_mm, o_mm, down_ready)
            pe.wait_ge(const_in, 16)

            def ada(n, source, filled, bank):
                pe.wait_ge(filled, 16 * ((n - EARLY) // 2 + 1 if n >= EARLY else 1))
                if n % EARLY >= 2:
                    pe.wait_ge(mrow_ready, n - 1)
                for k in range(KD):
                    mm = nc.tensor.matmul(ps[0:2, bank + n % 2, :], cs_c[:, k, :], source[:, k, :], start=(k == 0), stop=(k == KD - 1))
                mm.then_inc(slab_mm, 1)

            def turn_row(n, row, bank):
                pe.wait_ge(mrow_ready, n + 1)
                if n:
                    pe.wait_ge(mod_done, n)
                for j in range(4):
                    mm = nc.tensor.matmul(ps[:, bank, 8 * (n % 4) + 2 * j:8 * (n % 4) + 2 * j + 2], row[n % 2][:, P * j:P * j + P], con[0:2, 0:2],
                                          start=True, stop=True)
                mm.then_inc(turned, 1)

            pe.wait_ge(silu_c, 1)
            for n in range(EARLY):
                if n < 3:
                    norm_sum(pe, "n1", sq1, n)
                ada(n, slab[n], slab_in[n], 0)
                if n:
                    turn_row(n - 1, mrow, 2)
            turn_row(EARLY - 1, mrow, 2)

            pe.wait_ge(mod_done, EARLY)
            project(pe, 0, 0, first=True, tokens=0)
            project(pe, 0, 1, first=True)
            with pe.Fori(1, OUT_M) as m:
                for u in range(2):
                    project(pe, m, u)
            for u in range(2):
                pe.wait_ge(bank_free[u], 3 * OUT_M)

            for name in ("q", "kv"):
                for c in range(3):
                    norm_sum(pe, name, sq_lat, c)

            pe.wait_ge(lora_act, 2)
            pe.wait_ge(mix_done, RW_TILES)
            pe.wait_ge(lora_in, 32)
            for j in range(KR):
                for s in range(2):
                    if j:
                        pe.wait_ge(lora_ev, 2 * j + s - 1)
                    for c in range(3):
                        mm = nc.tensor.matmul(ps[:, 3 * s + c, 0:CM], w2a2[64 * s:64 * s + 64, P * j:P * j + P],
                                              mix[64 * s:64 * s + 64, 12, CM * c:CM * c + CM], start=True, stop=True)
                    mm.then_inc(lora_mm, 1)
            pe.wait_ge(root_ready, chunk_no["kv"] + 3)
            for q in range(3 * KR):
                j, c = q // 3, q % 3
                if q >= 2:
                    pe.wait_ge(gate_ev, q - 1)
                nc.tensor.matmul(ps[:, 6 + q % 2, 0:CM], g2[:, P * j:P * j + P], mix[:, 13, CM * c:CM * c + CM], start=True, stop=True).then_inc(gate_mm, 1)

            def block_sum(src, b, signal):
                for c in range(3):
                    mm = nc.tensor.matmul(ps[:, b + c, 0:CM], block64, src[:, CM * c:CM * c + CM], start=True, stop=True)
                mm.then_inc(signal, 1)

            pe.wait_ge(lora_ev, 2 * KR)
            for j in range(KR):
                pe.wait_ge(kk_sq, j + 1)
                if j:
                    pe.wait_ge(kk_root, j)
                block_sum(sqr, 0, kk_mm)
                pe.wait_ge(bonus_raw, j + 1)
                if j:
                    pe.wait_ge(bonus_done, j)
                block_sum(bonus[j % 2], 3, bonus_mm)
            pe.wait_ge(kk_root, KR)
            pe.wait_ge(bonus_done, KR)
            pe.wait_ge(state_ready, 3)

            def per_head():
                return [(p, e, slice(64 * e, 64 * e + 64)) for p in range(PAIRS) for e in range(2)]

            def chunk_tensor(i, s):
                yield
                yield
                pe.wait_ge(c_ab, i + 1)
                pe.wait_ge(c_k, 2 * i + 2 + 1)
                pe.wait_ge(c_sev, i + 1)
                pe.wait_ge(c_yev, i + 1)
                before_small()
                for e in range(2):
                    r = slice(64 * e, 64 * e + 64)
                    for p in range(PAIRS):
                        mm = nc.tensor.matmul(ps[:, WB + e, P * p:P * p + P], bk[r, p, :], ar[r, p, :], start=True, stop=True)
                    mm.then_inc(c_gmm, 1)
                yield
                pe.wait_ge(c_v, i + 1)
                pe.wait_ge(c_gm, 2 * i + 2 + 1)
                for p in range(PAIRS):
                    nc.tensor.transpose(ps[:, WB, P * p:P * p + P], bk[:, p, :], ident)
                for p in range(PAIRS):
                    mm = nc.tensor.transpose(ps[:, WB + 1, P * p:P * p + P], vv[:, p, :, :].rearrange("p a b -> p (a b)"), ident)
                mm.then_inc(c_tr, 1)
                yield
                pe.wait_ge(c_tm, i + 1 + 1)
                for l in range(LEVELS):
                    pe.wait_ge(c_lev, 2 * LEVELS * i + 2 * l + 2 + 1)
                    if l:
                        pe.wait_ge(c_tev, LEVELS * i + l)
                    before_small()
                    for p, e, r in per_head():
                        x = tt[r, 1, p, :] if l else con[r, K_EYE2:K_EYE2 + C]
                        mm = nc.tensor.matmul(ps[r, WB, C * p:C * p + C], nlev[r, l, p, :], x, start=True, stop=True)
                    mm.then_inc(c_xmm, 1)
                    yield
                    if l:
                        pe.wait_ge(c_xev, (LEVELS - 1) * i + l)
                        before_small()
                        for p, e, r in per_head():
                            mm = nc.tensor.matmul(ps[r, WB + 1, C * p:C * p + C], xt[r, p, :], tt[r, 0, p, :], start=True, stop=True)
                        if l < LEVELS - 1:
                            for p, e, r in per_head():
                                mm = nc.tensor.matmul(ps[r, WB + 1, C * (PAIRS + p):C * (PAIRS + p) + C], tt[r, 0, p, :], xt[r, p, :], start=True, stop=True)
                        mm.then_inc(c_tmm, 1)
                        yield
                before_small()
                for p, e, r in per_head():
                    nc.tensor.matmul(ps[r, WB, C * p:C * p + C], ar[r, p, 0:C], s[r, p, :], start=(p == 0), stop=False, skip_group_check=True)
                for p, e, r in per_head():
                    mm = nc.tensor.matmul(ps[r, WB, C * p:C * p + C], gm[:, e, p, 0:C], vz[:, p, C * e:C * e + C], start=False, stop=True, skip_group_check=True)
                mm.then_inc(c_rmm, 1)
                yield
                pe.wait_ge(c_rev, i + 1)
                pe.wait_ge(c_tev, LEVELS * (i + 1))
                before_small()
                for p, e, r in per_head():
                    mm = nc.tensor.matmul(ps[r, WB + 1, C * p:C * p + C], tt[r, 0, p, :], rhs[r, p, :], start=True, stop=True)
                mm.then_inc(c_umm, 1)
                yield
                pe.wait_ge(c_uev, i + 1)
                pe.wait_ge(c_uvv, 2 * i + 2)
                before_small()
                for p, e, r in per_head():
                    mm = nc.tensor.matmul(ps[r, WB, C * p:C * p + C], bktm[:, p, C * e:C * e + C], uv[:, p, C * e:C * e + C], start=True, stop=True)
                mm.then_inc(c_smm, 1)
                yield
                for p, e, r in per_head():
                    nc.tensor.matmul(ps[r, WB + 1, C * p:C * p + C], s[r, p, :], ar[r, p, C:2 * C], start=(p == 0), stop=False, skip_group_check=True)
                for p, e, r in per_head():
                    mm = nc.tensor.matmul(ps[r, WB + 1, C * p:C * p + C], uv[:, p, C * e:C * e + C], gm[:, e, p, C:2 * C], start=False, stop=True, skip_group_check=True)
                mm.then_inc(c_ymm, 1)
                yield

            pe.wait_ge(qkv_norm, 6)
            pe.wait_ge(past_in, 48)
            pe.wait_ge(krope_copied, 2)

            def scores(jb, hp):
                e, u, i = jb % 2, jb % 2, jb // 2
                if jb >= PJOBS:
                    pe.wait_ge(p_exp, JOBS * hp + jb)
                    pe.wait_ge(t_ev, T_GROUPS * hp + T_FIRST[jb])
                    pe.wait_ge(o_ev, QTILES * hp + QTILES - 1 + 1)
                    for b in range(6):
                        mm = nc.tensor.matmul(ps[0:TS, b, 0:352], qt[e][0:96, TP:T], kt[e][0:96, TP + 352 * b:TP + 352 * b + 352], start=True, stop=True)
                else:
                    if jb >= 2:
                        pe.wait_ge(p_exp, JOBS * hp + jb - 1)
                    n = P * (i + 1)
                    for b, n0 in enumerate(range(0, n, 512)):
                        w = min(512, n - n0)
                        mm = nc.tensor.matmul(ps[:, 2 * u + b, 0:w], qt[e][0:96, P * i:P * i + P], kt[e][0:96, n0:n0 + w], start=True, stop=True)
                mm.then_inc(s_mm, 1)

            def turn(jb, g, hp):
                u = jb % 2
                pe.wait_ge(p_norm, JOBS * hp + jb + 1)
                t0, t1 = T_PLAN[jb][g]
                tg = T_FIRST[jb] + g
                if tg >= 1:
                    pe.wait_ge(t_ev, T_GROUPS * hp + tg)
                if jb >= PJOBS:
                    before_small()
                for t in range(t0, t1):
                    if jb < PJOBS:
                        mm = nc.tensor.transpose(ps[:, 4, P * (t - t0):P * (t - t0) + P], probs[u][:, P * t:P * t + P], ident)
                    else:
                        k0, rows = (0, TS) if t == 0 else (TS + P * (t - 1), P)
                        mm = nc.tensor.transpose(ps[0:rows, 4, TS * (t - t0):TS * (t - t0) + TS], probs[u][0:TS, k0:k0 + rows], con[0:TS, 0:TS])
                mm.then_inc(t_mm, 1)

            def values(jb, hp):
                e, u, i = jb % 2, jb % 2, jb // 2
                pe.wait_ge(t_ev, T_GROUPS * hp + T_FIRST[jb + 1])
                if i >= 1:
                    pe.wait_ge(o_ev, QTILES * hp + i + 1)
                r = slice(64 * e, 64 * e + 64)
                if jb == PJOBS:
                    pe.wait_ge(p_exp, JOBS * hp + JOBS)
                if jb >= PJOBS:
                    before_small()
                    for t in range(17):
                        rows = slice(0, TS if t == 0 else P)
                        mm = nc.tensor.matmul(ps[r, 5, 0:TS], vt[rows, 8 + t, r], pt[u][rows, TS * t:TS * t + TS], start=(t == 0), stop=(t == 16))
                else:
                    for t in range(i + 1):
                        mm = nc.tensor.matmul(ps[r, 5, 0:P], vt[:, t, r], pt[u][:, P * t:P * t + P], start=(t == 0), stop=(t == i))
                mm.then_inc(o_mm, 1)

            def attend_tensor(hp):
                pe.wait_ge(aw_in, 16 * hp + 16)
                pe.wait_ge(o_ev, QTILES * hp + 1)
                wq = lambda e, k: aw[:, 384 * e + P * k:384 * e + P * k + P]
                wk = lambda k: aw[:, 768 + P * k:768 + P * k + P]
                wv = lambda k: aw[:, 1024 + P * k:1024 + P * k + P]
                for l, (dst, n) in enumerate(K_CHUNKS):
                    if l >= 4:
                        pe.wait_ge(ka_ev, 7 * hp + l - 3)
                        pe.wait_ge(kd_ev, 7 * hp + l - 3)
                    for k in range(KKV):
                        src = ckv[:, k, dst:dst + n] if l < 3 else past[:, k, dst - T:dst - T + n]
                        mm = nc.tensor.matmul(ps[:, l % 4, 0:n], wk(k), src, start=(k == 0), stop=(k == KKV - 1))
                    mm.then_inc(kp_mm, 1)
                    yield
                for e in range(2):
                    for c, (a, n) in enumerate(CH):
                        l = 3 * e + c
                        if l >= 2:
                            pe.wait_ge(qa_ev, 6 * hp + l - 1)
                            pe.wait_ge(qd_ev, 6 * hp + l - 1 + 1)
                        for k in range(KQ):
                            mm = nc.tensor.matmul(ps[:, 4 + l % 2, 0:n], wq(e, k), cq[:, k, a:a + n], start=(k == 0), stop=(k == KQ - 1))
                        mm.then_inc(qp_mm, 1)
                        yield
                for g, tiles in enumerate(V_GROUPS):
                    if g + 3 < 7:
                        pe.wait_ge(ka_ev, 7 * hp + g + 4)
                        pe.wait_ge(kd_ev, 7 * hp + g + 4)
                    else:
                        pe.wait_ge(v_ev, 7 * hp + g - 3)
                    for x, t in enumerate(tiles):
                        rows = TS if t == 8 else P
                        for k in range(KKV):
                            src = ckv[:, k, P * t:P * t + rows] if t < 9 else past[:, k, P * (t - 9):P * (t - 9) + P]
                            mm = nc.tensor.matmul(ps[0:rows, (7 + g) % 4, P * x:P * x + P], src, wv(k), start=(k == 0), stop=(k == KKV - 1))
                    mm.then_inc(vp_mm, 1)
                    yield
                pe.wait_ge(v_ev, 7 * hp + 7)
                pe.wait_ge(kd_ev, 7 * hp + 7)
                pe.wait_ge(qa_ev, 6 * hp + 6)
                pe.wait_ge(qd_ev, 6 * hp + 6 + 1)
                for kind, jb, g in JOB_UNITS:
                    if kind == "scores":
                        scores(jb, hp)
                    elif kind == "turn":
                        turn(jb, g, hp)
                    else:
                        values(jb, hp)
                    yield

            with pe.Fori(0, PAIRS - 1) as hp:
                interleave(attend_tensor(hp), ATT_UNITS, (z for x in range(4) for z in chunk_tensor(4 * hp + x, state[0])), 4 * CHUNK_UNITS)
            pe.wait_ge(state_in, 16)
            interleave(attend_tensor(PAIRS - 1), ATT_UNITS, (z for i in LAST_CHUNKS for z in chunk_tensor(i, state[i // CHUNKS])), 5 * CHUNK_UNITS)

            pe.wait_ge(y_back, 16 * KR)
            pe.wait_ge(o_ev, QTILES * PAIRS + 1)
            pe.wait_ge(c_yev, CHUNKS + 1 + 1)
            for j in range(KR):
                for c, (a, n) in enumerate(CH):
                    if j:
                        pe.wait_ge(yc_done, j)
                    nc.tensor.matmul(ps[:, c, 0:n], block64, yt[:, j, a:a + n], start=True, stop=True).then_inc(mean_mm, 1)
                n = EARLY + j
                ada(n, late[n % 2], late_in[n % 2], 4)
                if j:
                    turn_row(n - 1, late_row, 6)
            pe.wait_ge(mrow_ready, EARLY + KR)
            pe.wait_ge(yc_done, KR)
            for j in range(KR):
                pe.wait_ge(ysq_done, j + 1)
                if j:
                    pe.wait_ge(y_root, j)
                for c, (a, n) in enumerate(CH):
                    mm = nc.tensor.matmul(ps[:, 3 + c, 0:n], block64, ysq[j % 2][:, a:a + n], start=True, stop=True)
                mm.then_inc(var_mm, 1)
                n = EARLY + KR + j
                ada(n, late[n % 2], late_in[n % 2], 0)
                turn_row(n - 1, late_row, 6)
            turn_row(SLABS - 1, late_row, 6)

            pe.wait_ge(osplit_lo, 2)
            with pe.Fori(OUT_M, FF_M) as m:
                for u in range(2):
                    project(pe, m, u)
            for name in ("m", "n2"):
                for c in range(3):
                    norm_sum(pe, name, sq2, c)

            def down(g, slot, first=False):
                pe.wait_ge(d_lo, 2 * g + 2)
                pe.wait_ge(act_lo, 6 * g + 6)
                for x in range(24):
                    k, (a, n) = x // 3, CH[x % 3]
                    if not (first and x < 2):
                        pe.wait_ge(d_added, 24 * g + x - 1 + 1)
                    for u in range(2):
                        for w, y in ((dhi, ahi), (dhi, alo), (dlo, ahi)):
                            mm = nc.tensor.matmul(ps[:, 6 + x % 2, 0:n], w[u][:, P * k:P * k + P], y[:, slot + u, a:a + n],
                                                  start=(u == 0 and w is dhi and y is ahi), stop=(u == 1 and w is dlo))
                    mm.then_inc(down_ready, 1)

            pe.wait_ge(lo_ready, 6)

            def group(g, slot):
                for j in range(2):
                    for u in range(2):
                        ff_project(g, j, u)

            def ff_project(g, j, u):
                m = 2 * g + FF_M + j
                pe.wait_ge(w_lo, 2 * m + u + 1)
                for c, (a, n) in enumerate(CH):
                    pe.wait_ge((sil_ready, prod_ready)[u], 6 * g + 3 * j + c - 2)
                    products(m, u, c)

            def products(m, u, c):
                a, n = CH[c]
                for k in range(KD):
                    for w, x in ((whi, hhi), (whi, hlo), (wlo, hhi)):
                        mm = nc.tensor.matmul(ps[:, 3 * u + c, 0:n], w[u][:, k, :], x[:, k, a:a + n],
                                              start=(k == 0 and w is whi and x is hhi), stop=(k == KD - 1 and w is wlo))
                mm.then_inc(out_ready[u], 1)

            for u in range(2):
                pe.wait_ge(bank_free[u], 3 * FF_M)
                pe.wait_ge(w_lo, 2 * FF_M + u + 1)
                for c in range(3):
                    products(FF_M, u, c)
            for u in range(2):
                ff_project(0, 1, u)
            group(1, 2)
            down(0, 0, first=True)
            with pe.Fori(0, (GROUPS - 3) // 2) as it:
                group(2 * it + 2, 0)
                down(2 * it + 1, 2)
                group(2 * it + 3, 2)
                down(2 * it + 2, 0)
            group(GROUPS - 1, 0)
            down(GROUPS - 2, 2)
            down(GROUPS - 1, 0)
            for c in range(3):
                norm_sum(pe, "f", sq3, c)


def shape_table():
    t = np.zeros((P, K_ALL), np.float32)
    t[:, K_IDENT:K_IDENT + P] = np.eye(P)
    t[:, K_ONES:K_ONES + P] = 1.0
    half = np.arange(P) // 64
    t[:, K_BLOCK:K_BLOCK + P] = half[:, None] == half[None, :]
    s, tok = (np.arange(P) % C)[:, None], np.arange(C)[None, :]
    t[:, K_GMASK:K_GMASK + C] = s < tok
    t[:, K_GMASK + C:K_GMASK + 2 * C] = s <= tok
    for l in range(LEVELS):
        m = 2 ** l
        t[:, K_LEVEL + C * l:K_LEVEL + C * l + C] = -1.0 * ((s // (2 * m) == tok // (2 * m)) & (s // m % 2 == 0) & (tok // m % 2 == 1))
    t[:, K_EYE2:K_EYE2 + C] = s == tok
    t[:, K_EPS] = 1e-6
    t[:, K_EPS + 1] = 64e-5
    inv = np.float32(10000.0) ** (-np.arange(0, ROPE, 2, dtype=np.float32) / np.float32(ROPE))
    pos = np.concatenate([np.arange(TP), PAST + np.arange(TS)]).astype(np.float32)
    ang = (inv[:, None] * pos[None, :]).astype(np.float32)
    cos, sin = np.cos(ang), np.sin(ang)
    t[64:96, K_CS:] = np.concatenate([cos, cos])
    t[96:128, K_CS:] = np.concatenate([-sin, sin])
    return t


def kernel(**inputs):
    import concourse.bacc as bacc
    from concourse.bass_utils import run_bass_kernel_spmd

    x = {k: np.asarray(v) for k, v in inputs.items()}

    def columns(v):
        return np.reshape(v, (-1, P)).T

    def tiles(w):
        return np.reshape(w, (KD, P, -1, P)).transpose(2, 1, 0, 3).reshape(-1, P, KD * P)

    def swapped(w):
        return np.concatenate([w[..., ROPE // 2:], w[..., :ROPE // 2]], axis=-1)

    w_in = x["w_in"][0]
    mla = QL + KVL
    kr_cols = w_in[:, mla:mla + ROPE]
    w_lat = np.concatenate([w_in[:, :mla], np.zeros((D, 64), np.float32), kr_cols, swapped(kr_cols)], axis=1)
    w_rw = w_in[:, mla + ROPE:]
    gate, up = tiles(x["w_gate"][0]), tiles(x["w_up"][0])
    gate_up = np.stack([gate, up], axis=1).reshape(-1, P, KD * P)
    w_tiles = np.concatenate([tiles(w_lat), tiles(w_rw), tiles(x["w_out"][0]), gate_up])

    wuq = x["w_uq"][0].reshape(KQ, P, HEADS, DH + ROPE)
    wuq = np.concatenate([wuq, swapped(wuq[..., DH:])], axis=-1).reshape(KQ, P, PAIRS, 2, P).transpose(2, 1, 3, 0, 4).reshape(PAIRS, P, -1)
    by_pair = lambda w: w.reshape(KKV, P, PAIRS, P).transpose(2, 1, 0, 3).reshape(PAIRS, P, -1)
    att_w = np.concatenate([wuq, by_pair(x["w_uk"][0]), by_pair(x["w_uv"][0])], axis=2)

    c2 = np.stack([x["c_prompt"][0].reshape(KD, P), x["c_sample"][0].reshape(KD, P)]).transpose(2, 1, 0).reshape(P, 2 * KD)
    vectors = np.concatenate([columns(x[n][0]) for n in ("norm_g", "q_norm_g", "kv_norm_g", "rw_mu", "rw_w0", "rw_a0", "rw_kk", "rw_ka",
                                                       "rw_rk", "lnx_g", "lnx_b", "ada_b")] + [c2, columns(x["state_shift"][0, 0])], axis=1)
    arrays = {
        "table": shape_table(),
        "vectors": vectors,
        "x_t": np.concatenate([x["x_prompt"][0], x["x_sample"][0]]).T,
        "ada_w": x["ada_w"][0],
        "w_tiles": w_tiles,
        "att_w": att_w,
        "w2a2": np.concatenate([x["rw_w2"][0], x["rw_a2"][0]]),
        "g2": x["rw_g2"][0],
        "w_down": x["w_down"][0],
        "ckv_t": x["cache_ckv"][0, 0].T,
        "krope_t": x["cache_krope"][0, 0].T,
        "state0": x["state_wkv"][0, 0].reshape(PAIRS, 2, DH, DH).transpose(1, 3, 0, 2).reshape(P, PAIRS * DH),
    }
    outs = {"y": (D, T), "ckv_out": (KVL, T), "krope_out": (ROPE, T), "wkv": (2, P, PAIRS * DH), "shift": (P, 2 * RW_TILES)}
    nc = bacc.Bacc("TRN2", target_bir_lowering=False, num_devices=1)
    d, feed = {}, {}
    for name, a in arrays.items():
        feed[f"in_{name}"] = np.ascontiguousarray(a)
        d[name] = nc.dram_tensor(f"in_{name}", a.shape, F32, kind="ExternalInput").ap()
    for name, shape in outs.items():
        d[name] = nc.dram_tensor(f"out_{name}", shape, F32, kind="ExternalOutput").ap()
    for name, shape in {"scan": (CHUNKS + 1, P, SF, PAIRS, C), "y_chunks": (CHUNKS + 1, P, PAIRS * C),
                        "bonus_rows": (KR, P, T), "gate_rows": (KR, P, T)}.items():
        d[name] = nc.dram_tensor(name, shape, F32, kind="Internal").ap()
    d["x_mid"] = nc.dram_tensor("x_mid", (D, T), F32, kind="Internal").ap()
    build(nc, d)
    got = run_bass_kernel_spmd(nc, [feed], core_ids=[0]).results[0]
    y, ckv, krope = (got[f"out_{n}"].T for n in ("y", "ckv_out", "krope_out"))
    wkv = got["out_wkv"].reshape(2, 2, DH, PAIRS, DH).transpose(0, 3, 1, 4, 2).reshape(2, HEADS, DH, DH)
    shift = got["out_shift"].reshape(P, RW_TILES, 2).transpose(2, 1, 0).reshape(2, RW_TILES * P)
    c = np.ascontiguousarray
    return (c(y[None, :TP]), c(y[None, TP:]), c(ckv[None, None, :TP]), c(krope[None, None, :TP]), c(wkv[None, None, 0]), c(shift[None, None, 0]),
            c(ckv[None, None, TP:]), c(krope[None, None, TP:]), c(wkv[None, None, 1]), c(shift[None, None, 1]))
```

```python
from contextlib import ExitStack, contextmanager

import numpy as np

import concourse.bass as bass
from concourse import mybir

F32 = mybir.dt.float32
F32R = mybir.dt.float32r
ALU = mybir.AluOpType
ACT = mybir.ActivationFunctionType
AX_X = mybir.AxisListType.X

P = 128
D = 1024
KD = D // P
TP = 1024
TS = 64
T = TP + TS
PAST = 2048
C = 64
HEADS = 8
PAIRS = HEADS // 2
DH = 64
ROPE = 32
QL, KVL = 384, 256
KQ, KKV = QL // P, KVL // P
RW = 512
KR = RW // P
RW_TILES = 14
MLA_TILES = 6
DFF = 2816
GROUPS = DFF // (2 * P)
TM = T + 1
SAMPLE_COL = TP + 1
KEYS = T + PAST
SCALE = (DH + ROPE) ** -0.5
DECAY = float(np.exp(-0.5))
NEG = -1e30
CH = [(0, 364), (364, 364), (728, 360)]
CM = 363
LEVELS = 6
SF = 6
CHUNKS = TP // C

K_IDENT, K_ONES, K_BLOCK, K_GMASK, K_LEVEL, K_EYE2 = 0, 128, 256, 384, 512, 512 + LEVELS * 64
K_EPS = K_EYE2 + 64
K_CS = K_EPS + 4
K_ALL = K_CS + T
V_NORM, V_QG, V_KVG, V_MU, V_W0, V_A0, V_KK, V_KA, V_RK, V_LG, V_LB = 0, 32, 35, 37, 51, 55, 59, 63, 67, 71, 75
V_ADAB, V_C, V_SHIFT = 79, 127, 143
V_ALL = 157


K_CHUNKS = CH + [(T + 512 * j, 512) for j in range(PAST // 512)]
V_GROUPS = [[0, 1, 2, 3], [4, 5, 6, 7], [8]] + [list(range(9 + 4 * j, 13 + 4 * j)) for j in range(4)]
PJOBS = 2 * (TP // P)
JOBS = PJOBS + 2
QTILES = JOBS // 2
T_PLAN = [[(a, min(a + 4, jb // 2 + 1)) for a in range(0, jb // 2 + 1, 4)] for jb in range(PJOBS)] + 2 * [[(0, 8), (8, 16), (16, 17)]]
T_FIRST = [sum(len(x) for x in T_PLAN[:jb]) for jb in range(JOBS + 1)]
T_GROUPS = T_FIRST[-1]


def job_units():
    units = [("scores", 0, 0), ("scores", 1, 0)]
    for jb in range(JOBS):
        if jb == PJOBS:
            units.append(("scores", jb, 0))
        units += [("turn", jb, g) for g in range(len(T_PLAN[jb]))]
        if jb + 2 < PJOBS:
            units.append(("scores", jb + 2, 0))
        if jb == PJOBS:
            units.append(("scores", jb + 1, 0))
        units.append(("values", jb, 0))
    return units


JOB_UNITS = job_units()


def unit_cost(kind, jb, g):
    tiles = jb // 2 + 1 if jb < PJOBS else 17
    t0, t1 = T_PLAN[jb][g]
    return {"scores": P * tiles, "turn": P * (t1 - t0) // 2, "values": P * tiles if jb < PJOBS else TS * tiles}[kind]



ATT_COSTS = ([KKV * n for _, n in K_CHUNKS] + 2 * [KQ * n for _, n in CH]
             + [KKV * P * len(t) for t in V_GROUPS] + [unit_cost(*u) for u in JOB_UNITS])
SLOTS = TP // C + 2
SLOT_UNITS, LAST_SLOT_UNITS = 2 + 1 + 2 * (LEVELS - 1), 4
EARLY, SLABS = 4, 12
WB = 6


class Steps:

    def __init__(self, eng, sem):
        self.eng, self.sem, self.base, self.n = eng, sem, 0, 0

    def mark(self, ins):
        ins.then_inc(self.sem, 1)
        self.n += 1

    def wait(self):
        self.eng.wait_ge(self.sem, self.base + self.n)

    def done(self, ins):
        self.mark(ins)
        self.wait()

    @contextmanager
    def loop(self, count, per):
        start = self.base + self.n
        count = count if isinstance(count, range) else range(count)
        with self.eng.Fori(count[0], count[-1] + 1) as i:
            self.base, self.n = (i * per + (start - count[0] * per) if per else start), 0
            yield i
            assert self.n == per, f"the body makes {self.n} steps, not {per}"
        self.base, self.n = start + len(count) * per, 0


def build(nc, d):
    with ExitStack() as ctx:
        def sem(name):
            return ctx.enter_context(nc.semaphore(name))

        def place(start, *tensors):
            out = []
            for name, shape, *dt in tensors:
                out.append(nc.alloc_sbuf_tensor_at(name, shape, dt[0] if dt else F32, offset=start))
                start += -(-int(np.prod(shape[1:])) * 4 // 32) * 32
            return *out, start

        (con, vec, mod, gains, cs_c, omm, oma, sh_out, sm, krope, rstd, WA) = place(
            17 * 1024,
            ("con", [P, K_ALL]), ("vec", [P, V_ALL]), ("mod", [P, 48, 2]),
            ("gains", [P, 4, 8, 2]),
            ("cs_c", [P, 8, 2]), ("omm", [P, 14]), ("oma", [P, 4]),
            ("sh_out", [P, 14, 2]), ("sm", [P, 3, 2]),
            ("krope", [P, T]), ("rstd", [P, T]))
        tile = [P, KD, P]
        wraw0, wraw1, whi0, whi1, wlo0, wlo1, R1 = place(
            WA, ("wraw0", tile), ("wraw1", tile), ("whi0", tile, F32R), ("whi1", tile, F32R), ("wlo0", tile, F32R), ("wlo1", tile, F32R))
        wraw, whi, wlo = [wraw0, wraw1], [whi0, whi1], [wlo0, wlo1]
        hhi, hlo, R2 = place(R1, ("hhi", [P, KD, T], F32R), ("hlo", [P, KD, T], F32R))
        END = nc.sbuf_usable_end

        sq = [P, 4, 364]
        x1, s0, s1, r0, r1, end = place(R2, ("x1", [P, KD, T]), ("sq1_0", sq), ("sq1_1", sq), ("mrow0", [2, 512]), ("mrow1", [2, 512]))
        sq1, mrow = [s0, s1], [r0, r1]
        assert end <= END
        *slab, end = place(R1, *((f"slab{u}", [P, KD, 512]) for u in range(EARLY)))
        assert end <= R2
        cq, ckv, raw0, raw1, mix, end = place(R2, ("cq", [P, KQ, T]), ("ckv", [P, KKV, T]), ("raw0", [P, TM + 1]), ("raw1", [P, TM + 1]),
                                              ("mix", [P, RW_TILES, TM]))
        raw = [raw0, raw1]
        assert end <= END
        RAW_AT = R2 + (KQ + KKV) * T * 4
        MIX_AT = RAW_AT + 2 * (-(-(TM + 1) * 4 // 32) * 32)
        lw, kk, bb, sqr, rn, w2a2, g2, end = place(R1, ("lw", [P, KR, TM]), ("kk", [P, KR, TM]), ("bb", [P, KR, TM]), ("sqr", [P, TM]),
                                                   ("rn", [P, TM]), ("w2a2", [P, RW]), ("g2", [P, RW]))
        assert end <= R2
        sl0, sl1, end = place(WA, ("sq_lat0", sq), ("sq_lat1", sq))
        sq_lat = [sl0, sl1]
        bn0, bn1, go0, go1, tmp, end = place(WA, ("bn0", [P, TM]), ("bn1", [P, TM]), ("go0", [P, TM]), ("go1", [P, TM]), ("tmp", [P, TM]))
        bonus, gout = [bn0, bn1], [go0, go1]
        assert end <= R1
        cum, pinc0, pneg, bk, ar0, vv, gm0, tt0, xt, bktm0, uv, st0, st1, rhs, end = place(
            WA, ("cum", [P, PAIRS, C + 1]), ("pinc0", [P, PAIRS, C + 1]), ("pneg", [P, PAIRS, C]), ("bk", [P, PAIRS, 2 * C]),
            ("ar0", [P, PAIRS, 2 * C]), ("vv", [P, PAIRS, 2, C]), ("gm0", [P, 2, PAIRS, 2 * C]),
            ("tt0", [P, 2, PAIRS, C]),
            ("xt", [P, PAIRS, C]), ("bktm0", [P, PAIRS, P]), ("uv", [P, PAIRS, P]), ("st0", [P, PAIRS, DH]), ("st1", [P, PAIRS, DH]),
            ("rhs", [P, PAIRS, C]))
        state = [st0, st1]
        assert end <= R1
        gm1, end = place(WA - T * 4, ("gm1", [P, 2, PAIRS, 2 * C]))
        assert end <= WA
        nlev, tt1, end = place(RAW_AT, ("nlev", [P, LEVELS, PAIRS, C]), ("tt1", [P, 2, PAIRS, C]))
        assert end <= MIX_AT
        past, kt0, kt1, qt0, qt1, vt, aw, pinc1, end = place(
            R1, ("past", [P, KKV, PAST]), ("kt0", [P, KEYS]), ("kt1", [P, KEYS]), ("qt0", [P, T]), ("qt1", [P, T]), ("vt", [P, 25, P]), ("aw", [P, 1280]),
            ("pinc1", [P, PAIRS, C + 1]))
        kt, qt = [kt0, kt1], [qt0, qt1]
        assert end <= R2
        ci0, ci1, yb0, yb1, vz0, vz1, ar1, bktm1, pr0, pr1, pt0, pt1, rt0, rt1, end = place(
            MIX_AT, ("ci0", [P, SF, PAIRS, C]), ("ci1", [P, SF, PAIRS, C]), ("yb0", [P, PAIRS, C]), ("yb1", [P, PAIRS, C]),
            ("vz0", [P, PAIRS, P]), ("vz1", [P, PAIRS, P]), ("ar1", [P, PAIRS, 2 * C]), ("bktm1", [P, PAIRS, P]),
            ("pr0", [P, TS + PAST]), ("pr1", [P, TS + PAST]), ("pt0", [P, 1088]), ("pt1", [P, 1088]), ("rt0", [P, 364]), ("rt1", [P, 364]))
        pinc, ar, gm, tt, bktm, vz = [pinc0, pinc1], [ar0, ar1], [gm0, gm1], [tt0, tt1], [bktm0, bktm1], [vz0, vz1]
        cin, ybuf, probs, pt, rtmp = [ci0, ci1], [yb0, yb1], [pr0, pr1], [pt0, pt1], [rt0, rt1]
        OATT_AT = (END - PAIRS * T * 4) // 32 * 32
        assert end <= OATT_AT
        oatt, _ = place(OATT_AT, ("oatt", [P, PAIRS, T]))
        yt, _ = place(R2, ("yt", [P, KR, T]))
        bon, gat, end = place(MIX_AT, ("bon", [P, KR, T]), ("gat", [P, KR, T]))
        assert end <= OATT_AT
        yn, ysq0, ysq1, LATE_AT = place(R1, ("yn", [P, KR, T]), ("ysq0", [P, T]), ("ysq1", [P, T]))
        ysq = [ysq0, ysq1]
        l0, l1, r0, r1, end = place(LATE_AT, ("late0", [P, KD, 512]), ("late1", [P, KD, 512]), ("mrow2", [2, 512]), ("mrow3", [2, 512]))
        late, late_row = [l0, l1], [r0, r1]
        assert end <= R2
        m1, x2, s0, s1, end = place(R2, ("m1", [P, KD, T]), ("x2", [P, KD, T]), ("sq2_0", sq), ("sq2_1", sq))
        sq2 = [s0, s1]
        assert end <= END
        acc, ahi, alo, draw, dhi0, dhi1, dlo0, dlo1, sil0, sil1, sil2, end = place(
            R2, ("acc", [P, KD, T]), ("ahi", [P, 4, T], F32R), ("alo", [P, 4, T], F32R), ("draw", [P, D]),
            ("dhi0", [P, D], F32R), ("dhi1", [P, D], F32R), ("dlo0", [P, D], F32R), ("dlo1", [P, D], F32R),
            ("sil0", [P, 364]), ("sil1", [P, 364]), ("sil2", [P, 364]))
        dhi, dlo, sil = [dhi0, dhi1], [dlo0, dlo1], [sil0, sil1, sil2]
        assert end <= END
        x3, _ = place(R1, ("x3", [P, KD, T]))
        s0, s1, _ = place(R2 + KD * T * 4, ("sq3_0", sq), ("sq3_1", sq))
        sq3 = [s0, s1]

        ps = ctx.enter_context(nc.psum_tensor("ps", [P, 8, 512], F32))

        ident = con[:, K_IDENT:K_IDENT + P]
        ones = con[:, K_ONES:K_ONES + P]
        block64 = con[:, K_BLOCK:K_BLOCK + P]
        gmask = con[:, K_GMASK:K_GMASK + P]
        eye2 = con[:, K_EYE2:K_EYE2 + C]
        eps_rms = con[:, K_EPS:K_EPS + 1]
        eps_ln = con[:, K_EPS + 1:K_EPS + 2]
        zero = con[:, K_EPS + 2:K_EPS + 3]
        cs = con[:, K_CS:K_CS + T]

        const_in, vec_in = sem("const_in"), sem("vec_in")
        x_in = [sem(f"x_in{c}") for c in range(3)]
        slab_in = [sem(f"slab_in{u}") for u in range(EARLY)]
        late_in = [sem(f"late_in{u}") for u in range(2)]
        mrow_ready, turned = sem("mrow_ready"), sem("turned")
        silu_c, waited, pool_waited = sem("silu_c"), sem("waited"), sem("pool_waited")
        slab_mm, mod_done = sem("slab_mm"), sem("mod_done")
        gains_done = sem("gains_done")
        w_in_sem = [sem(f"w_loaded{u}") for u in range(2)]
        w_hi, w_lo = sem("w_hi"), sem("w_lo")
        out_ready = [sem(f"out_ready{u}") for u in range(2)]
        bank_free = [sem(f"bank_free{u}") for u in range(2)]
        sq_ready, sq_used = sem("sq_ready"), sem("sq_used")
        root_ready, rstd_ready = sem("root_ready"), sem("rstd_ready")
        xn_ready, affine_done, hi_ready, lo_ready = sem("xn_ready"), sem("affine_done"), sem("hi_ready"), sem("lo_ready")
        v_step, s_step, g_step = sem("vector_step"), sem("scalar_step"), sem("pool_step")
        raw_zero, raw_ready, mix_done = sem("raw_zero"), sem("raw_ready"), sem("mix_done")
        shift_sent = sem("shift_sent")
        lora_in, lora_act, lora_mm, lora_ev = sem("lora_in"), sem("lora_act"), sem("lora_mm"), sem("lora_evicted")
        kk_raw, kk_sq, kk_mm, kk_root, pre_done = sem("kk_raw"), sem("kk_sq"), sem("kk_mm"), sem("kk_root"), sem("pre_done")
        state_in, state_ready = sem("state_in"), sem("state_ready")
        scan_out, bg_out = sem("scan_out"), sem("bg_out")
        bonus_sent, gate_sent = [sem(f"bonus_sent{u}") for u in range(2)], [sem(f"gate_sent{u}") for u in range(2)]
        bonus_raw, bonus_mm, bonus_done = sem("bonus_raw"), sem("bonus_mm"), sem("bonus_done")
        gate_mm, gate_ev = sem("gate_mm"), sem("gate_evicted")
        cin_in = [sem(f"cin_in{u}") for u in range(2)]
        y_sent = [sem(f"y_sent{u}") for u in range(2)]
        y_back, bg_back = sem("y_back"), sem("bg_back")
        c_cum, c_exp_a, c_exp, c_ab, c_k, c_v = sem("c_cum"), sem("c_exp_a"), sem("c_exp"), sem("c_ab"), sem("c_k"), sem("c_v")
        c_gmm, c_tr, c_gm, c_tm, c_lev = sem("c_gmm"), sem("c_tr"), sem("c_gm"), sem("c_tm"), sem("c_lev")
        c_xmm, c_xev, c_tmm, c_tev = sem("c_xmm"), sem("c_xev"), sem("c_tmm"), sem("c_tev")
        c_rmm, c_rev, c_umm, c_uev, c_ymm, c_yev, c_smm, c_sev = (sem(n) for n in (
            "c_rmm", "c_rev", "c_umm", "c_uev", "c_ymm", "c_yev", "c_smm", "c_sev"))
        c_uvv = sem("c_uvv")
        state_out = sem("state_out")
        mean_mm, yc_done, ysq_done, var_mm, y_root, y_norm, y_affine = (sem(n) for n in (
            "mean_mm", "yc_done", "ysq_done", "var_mm", "y_root", "y_norm", "y_affine"))
        rw_done = sem("rw_done")
        qkv_norm = sem("qkv_norm")
        past_in, aw_in = sem("past_in"), sem("aw_in")
        krope_put = sem("krope_put")
        ka_ev, kd_ev, kp_mm = sem("k_even_evicted"), sem("k_odd_evicted"), sem("k_mm")
        qp_mm, qa_ev, qd_ev = sem("q_mm"), sem("q_nope_evicted"), sem("q_rope_evicted")
        vp_mm, v_ev = sem("v_mm"), sem("v_evicted")
        s_mm, nmax, p_exp, p_norm = sem("scores_ready"), sem("negmax_ready"), sem("exp_ready"), sem("probs_ready")
        t_mm, t_ev, o_mm, o_ev = sem("probs_t_ready"), sem("probs_t_evicted"), sem("out_heads_ready"), sem("out_evicted")
        osplit_hi, osplit_lo = sem("osplit_hi"), sem("osplit_lo")
        x2_in, x2_done, x2_out = sem("x2_in"), sem("x2_done"), sem("x2_out")
        acc_zero = sem("acc_zero")
        d_in, d_hi, d_lo, down_ready = sem("d_loaded"), sem("d_hi"), sem("d_lo"), sem("down_ready")
        d_added = sem("down_added")
        sil_ready, act_hi, act_lo, prod_ready = sem("silu_ready"), sem("act_hi"), sem("act_lo"), sem("product_ready")
        krope_copied = sem("krope_copied")
        x3_in, y_done, stored = sem("x3_in"), sem("y_done"), sem("stored")

        def start_at_one(eng, *sems):
            for x in sems:
                eng.sem_inc(x, 1)

        OUT_M = (MLA_TILES + RW_TILES) // 2
        FF_M = OUT_M + KD // 2
        A_TILES = 2 * FF_M + 4 * GROUPS

        def segments(c):
            a, n = CH[c]
            b = a + n
            return [(a, n, 0)] if b <= TP else [(a, TP - a, 0), (TP, b - TP, 1)]

        def o_parts(h):
            return [(h[:, 0:KR, :], oatt[:, :, :]), (h[:, KR:KD, :], yt[:, :, :])]

        def load_weight(eng, m, u, first=False):
            if not first:
                eng.wait_ge(w_lo, 2 * m + u - 1)
            eng.dma_start(wraw[u][:, :, :].rearrange("p a b -> p (a b)"), d["w_tiles"][2 * m + u, :, :]).then_inc(w_in_sem[u], 16)

        def split_hi(act, m, u, first=False):
            act.wait_ge(w_in_sem[u], 16 * (m + 1))
            if not first:
                act.wait_ge(out_ready[u], 3 * m)
            nc.scalar.copy(whi[u][:, :, :], wraw[u][:, :, :]).then_inc(w_hi, 1)

        def split_lo(dve, m, u):
            dve.wait_ge(w_hi, 2 * m + u + 1)
            nc.vector.tensor_tensor(wlo[u][:, :, :], wraw[u][:, :, :], whi[u][:, :, :].bitcast(F32), ALU.subtract).then_inc(w_lo, 1)

        def project(pe, m, u, first=False, tokens=None):
            pe.wait_ge(w_lo, 2 * m + u + 1)
            for c, (a, n) in enumerate(CH):
                if tokens is not None:
                    pe.wait_ge(lo_ready, tokens + c + 1)
                if not first:
                    pe.wait_ge(bank_free[u], 3 * (m - 1) + c + 1)
                out = ps[:, 3 * u + c, 0:n]
                for k in range(KD):
                    for w, x in ((whi, hhi), (whi, hlo), (wlo, hhi)):
                        mm = nc.tensor.matmul(out, w[u][:, k, :], x[:, k, a:a + n],
                                              start=(k == 0 and w is whi and x is hhi), stop=(k == KD - 1 and w is wlo))
                mm.then_inc(out_ready[u], 1)

        NORMS = {"n1": (KD, D), "q": (KQ, QL), "kv": (KKV, KVL), "m": (KD, D), "n2": (KD, D), "f": (KD, D)}
        pieces, first_piece, chunk_no = 0, {}, {}
        for r, (name, (k, _)) in enumerate(NORMS.items()):
            chunk_no[name] = 3 * r
            first_piece[name] = pieces
            pieces += 3 * (-(-k // 4))

        def norm_squares(act, name, src, sqbuf, c):
            k = NORMS[name][0]
            per = -(-k // 4)
            a, n = CH[c]
            for j in range(per):
                piece = first_piece[name] + c * per + j
                k0, k1 = 4 * j, min(4 * j + 4, k)
                if piece >= 2:
                    act.wait_ge(sq_used, piece - 1)
                nc.scalar.activation(sqbuf[piece % 2][:, 0:k1 - k0, 0:n], src[:, k0:k1, a:a + n], ACT.Square).then_inc(sq_ready, 1)

        def norm_sum(pe, name, sqbuf, c):
            k = NORMS[name][0]
            per = -(-k // 4)
            a, n = CH[c]
            q = chunk_no[name] + c
            if q >= 2:
                pe.wait_ge(root_ready, q - 1)
            for j in range(per):
                piece = first_piece[name] + c * per + j
                pe.wait_ge(sq_ready, piece + 1)
                for i in range(4 * j, min(4 * j + 4, k)):
                    mm = nc.tensor.matmul(ps[:, 6 + q % 2, 0:n], ones, sqbuf[piece % 2][:, i - 4 * j, 0:n], start=(i == 0), stop=(i == k - 1))
                mm.then_inc(sq_used, 1)

        def norm_root(act, name, c):
            k, width = NORMS[name]
            per = -(-k // 4)
            a, n = CH[c]
            q = chunk_no[name] + c
            act.wait_ge(sq_used, first_piece[name] + (c + 1) * per)
            used = {"q": (xn_ready, c + 1), "kv": (qkv_norm, c + 1), "m": (qkv_norm, c + 4), "n2": (x2_done, c + 1), "f": (xn_ready, c + 4)}
            if name in used:
                act.wait_ge(*used[name])
            nc.scalar.activation(rstd[:, a:a + n], ps[:, 6 + q % 2, 0:n], ACT.Sqrt, bias=eps_rms, scale=1.0 / width).then_inc(root_ready, 1)

        def norm_recip(dve, name, c):
            a, n = CH[c]
            q = chunk_no[name] + c
            dve.wait_ge(root_ready, q + 1)
            nc.vector.reciprocal(rstd[:, a:a + n], rstd[:, a:a + n]).then_inc(rstd_ready, 1)
            dve.wait_ge(rstd_ready, q + 1)

        def at_least(eng, signal, value):
            if not isinstance(value, int) or value > 0:
                eng.wait_ge(signal, value)

        def slots(emit, numbers, first=0):
            return (unit for x in numbers for unit in emit(first + x, x % 2))

        def slot_units(numbers):
            return sum(SLOT_UNITS if x < SLOTS - 1 else LAST_SLOT_UNITS for x in numbers)

        def over_tiles(ap2, k):
            return ap2.unsqueeze(1).broadcast_to([P, k, ap2.shape[1]])

        def interleave(one, costs, other, steps_other):
            done, work = 0, 0
            for cost in costs:
                next(one)
                work += cost
                while done * sum(costs) < work * steps_other:
                    next(other)
                    done += 1
            assert next(one, None) is None and next(other, None) is None

        FIRST_SLOTS, MID_SLOTS, LAST_SLOTS = range(0, 5), range(1, 5), range(SLOTS - 5, SLOTS)

        block = ctx.enter_context(nc.Block())

        @block.sync
        def _(sp):
            for u in range(2):
                sp.sem_inc(y_sent[u], 16)
            sp.dma_start(con[:, :], d["table"]).then_inc(const_in, 16)
            sp.dma_start(vec[:, :], d["vectors"]).then_inc(vec_in, 16)
            ada = d["ada_w"].rearrange("(k p) n -> p k n", p=P)
            for c in range(EARLY):
                if c < 3:
                    a, n = CH[c]
                    sp.dma_start(x1[:, :, a:a + n], d["x_t"].rearrange("(k p) t -> p k t", p=P)[:, :, a:a + n]).then_inc(x_in[c], 16)
                sp.dma_start(slab[c][:, :, :], ada[:, :, 512 * c:512 * c + 512]).then_inc(slab_in[c], 16)
            load_weight(sp, 0, 0, first=True)
            load_weight(sp, 0, 1, first=True)
            with sp.Fori(1, OUT_M) as m:
                for u in range(2):
                    load_weight(sp, m, u)
            sp.wait_ge(raw_ready, RW_TILES)
            sp.dma_start(d["shift"], sh_out[:, :, :].rearrange("p a b -> p (a b)")).then_inc(stored, 16)
            for u in range(2):
                sp.wait_ge(out_ready[u], 3 * OUT_M)
            sp.dma_start(w2a2[:, :], d["w2a2"]).then_inc(lora_in, 16)
            sp.dma_start(g2[:, :], d["g2"]).then_inc(lora_in, 16)
            sp.wait_ge(qkv_norm, 6)
            sp.dma_start(d["ckv_out"].rearrange("(k p) t -> p k t", p=P), ckv[:, :, :]).then_inc(stored, 16)
            sp.dma_start(d["krope_out"], krope[64:96, :]).then_inc(stored, 16)

            def spill(field, j, row):
                sp.dma_start(d["scan"][0:CHUNKS, :, field, j, :].rearrange("c p t -> p c t"),
                             row[:, 0:TP].rearrange("p (c t) -> p c t", t=C)).then_inc(scan_out, 16)
                sp.dma_start(d["scan"][CHUNKS, :, field, j, :], row[:, SAMPLE_COL:TM]).then_inc(scan_out, 16)

            def spill_row(name, j, row, signal):
                sp.dma_start(d[name][j, :, 0:TP], row[:, 0:TP]).then_inc(signal, 16)
                sp.dma_start(d[name][j, :, TP:T], row[:, SAMPLE_COL:TM]).then_inc(signal, 16)

            sp.wait_ge(mix_done, RW_TILES)
            for j in range(KR):
                spill(3, j, mix[:, j, :])
                spill(5, j, mix[:, 2 * KR + j, :])
            for j in range(KR):
                sp.wait_ge(gate_ev, 3 * j + 3)
                spill_row("gate_rows", j, gout[j % 2], gate_sent[j % 2])
            for j in range(KR):
                sp.wait_ge(lora_ev, 2 * j + 1)
                spill(0, j, lw[:, j, :])
                sp.wait_ge(pre_done, j + 1)
                spill(1, j, kk[:, j, :])
                spill(2, j, bb[:, j, :])
                spill(4, j, mix[:, KR + j, :])
                sp.wait_ge(bonus_done, j + 1)
                spill_row("bonus_rows", j, bonus[j % 2], bonus_sent[j % 2])
            sp.wait_ge(scan_out, 16 * 2 * SF * KR)
            for u in range(2):
                sp.wait_ge(bonus_sent[u], 64)
                sp.wait_ge(gate_sent[u], 64)

            def load_chunk(i, u):
                sp.dma_start(cin[u][:, :, :, :].rearrange("p a b c -> p (a b c)"),
                             d["scan"][i, :, :, :, :].rearrange("p a b c -> p (a b c)")).then_inc(cin_in[u], 16)

            load_chunk(0, 0)
            load_chunk(1, 1)

            def next_load(f, u):
                sp.wait_ge(c_ab, f + 1)
                sp.wait_ge(c_k, 2 * f + 2 + 1)
                sp.wait_ge(c_v, f + 1)
                load_chunk(f + 2, u)

            sp.dma_start(aw[:, :], d["att_w"][0, :, :]).then_inc(aw_in, 16)
            sp.dma_start(past[:, :, :], d["ckv_t"].rearrange("(k p) t -> p k t", p=P)).then_inc(past_in, 16)
            for e in range(2):
                sp.dma_start(kt[e][64:96, T:KEYS], d["krope_t"]).then_inc(past_in, 16)
            sp.dma_start(state[1][:, :, :].rearrange("p a b -> p (a b)"), d["state0"]).then_inc(state_in, 16)

            def store_y(i, u):
                sp.wait_ge(c_yev, i + 1 + 1)
                sp.dma_start(d["y_chunks"][i, :, :], ybuf[u][:, :, :].rearrange("p a b -> p (a b)")).then_inc(y_sent[u], 16)

            def slot_moves(s, x, hp, aw_at):
                if x == aw_at:
                    sp.wait_ge(vp_mm, 7 * hp + 7)
                    sp.dma_start(aw[:, :], d["att_w"][hp + 1, :, :]).then_inc(aw_in, 16)
                if not isinstance(s, int) or s + 3 <= CHUNKS:
                    next_load(s + 1, (x + 1) % 2)
                if not isinstance(s, int) or s >= 1:
                    store_y(s - 1, (x - 1) % 2)

            next_load(0, 0)
            for x in FIRST_SLOTS:
                slot_moves(x, x, 0, 1)
            with sp.Fori(1, PAIRS - 1) as hp:
                for x in MID_SLOTS:
                    slot_moves(4 * hp + x, x, hp, 2)
            for x in LAST_SLOTS[:-1]:
                slot_moves(x, x, PAIRS - 1, None)
            sp.wait_ge(c_sev, CHUNKS + 1)
            sp.dma_start(d["wkv"][0, :, :], state[0][:, :, :].rearrange("p a b -> p (a b)")).then_inc(state_out, 16)
            store_y(CHUNKS, 0)
            sp.wait_ge(c_sev, CHUNKS + 1 + 1)
            sp.dma_start(d["wkv"][1, :, :], state[1][:, :, :].rearrange("p a b -> p (a b)")).then_inc(state_out, 16)
            sp.wait_ge(o_ev, QTILES * PAIRS + 1)
            load_slab = lambda n: sp.dma_start(late[n % 2][:, :, :], ada[:, :, 512 * n:512 * n + 512]).then_inc(late_in[n % 2], 16)
            load_slab(EARLY)
            for u in range(2):
                sp.wait_ge(y_sent[u], 16 * (CHUNKS // 2 + 1 - u) + 16)
            for j in range(KR):
                sp.dma_start(yt[:, j, :].rearrange("p (c t) -> p c t", t=C),
                             d["y_chunks"][:, :, C * j:C * j + C].rearrange("c p t -> p c t")).then_inc(y_back, 16)
            load_slab(EARLY + 1)
            sp.dma_start(bon[:, :, :], d["bonus_rows"].rearrange("j p t -> p j t")).then_inc(bg_back, 16)
            sp.dma_start(gat[:, :, :], d["gate_rows"].rearrange("j p t -> p j t")).then_inc(bg_back, 16)
            sp.wait_ge(state_out, 32)
            for u in range(2):
                load_weight(sp, OUT_M, u)
            for n in range(EARLY + 2, SLABS):
                sp.wait_ge(slab_mm, n - 1)
                load_slab(n)
            sp.wait_ge(osplit_lo, 2)
            for c, (a, n) in enumerate(CH):
                sp.dma_start(x2[:, :, a:a + n], d["x_t"].rearrange("(k p) t -> p k t", p=P)[:, :, a:a + n]).then_inc(x2_in, 16)
            with sp.Fori(OUT_M + 1, FF_M) as m:
                for u in range(2):
                    load_weight(sp, m, u)
            for u in range(2):
                load_weight(sp, FF_M, u)
            for c, (a, n) in enumerate(CH):
                sp.wait_ge(x2_done, c + 1)
                sp.dma_start(d["x_mid"].rearrange("(k p) t -> p k t", p=P)[:, :, a:a + n], x2[:, :, a:a + n]).then_inc(x2_out, 16)
            sp.wait_ge(sq_used, first_piece["n2"] + 6)
            def load_down(g, u, first=False):
                if not first:
                    sp.wait_ge(d_lo, 2 * g + u)
                sp.dma_start(draw[:, :], d["w_down"][bass.ds((2 * g + u) * P, P), :]).then_inc(d_in, 16)

            load_weight(sp, FF_M + 1, 0)
            load_weight(sp, FF_M + 1, 1)
            load_down(0, 0, first=True)
            with sp.Fori(1, GROUPS) as g:
                for j in range(2):
                    for u in range(2):
                        load_weight(sp, 2 * g + FF_M + j, u)
                load_down(g - 1, 1)
                load_down(g, 0)
            load_down(GROUPS - 1, 1)
            for u in range(2):
                sp.wait_ge(out_ready[u], 3 * (FF_M + 2 * GROUPS))
            sp.wait_ge(x2_out, 48)
            sp.dma_start(x3[:, :, :], d["x_mid"].rearrange("(k p) t -> p k t", p=P)).then_inc(x3_in, 16)
            for c, (a, n) in enumerate(CH):
                sp.wait_ge(y_done, c + 1)
                sp.dma_start(d["y"].rearrange("(k p) t -> p k t", p=P)[:, :, a:a + n], x3[:, :, a:a + n]).then_inc(stored, 16)
            sp.wait_ge(stored, 16 * 6)
            sp.wait_ge(state_out, 32)

        @block.gpsimd
        def _(pool):
            step = Steps(pool, g_step)
            start_at_one(pool, c_k, c_lev)
            pool.wait_ge(lo_ready, 3)
            for u in range(2):
                nc.gpsimd.memset(raw[u][:, 0:1], 0.0).then_inc(raw_zero, 1)
            pool.wait_ge(scan_out, 16 * 2 * SF * KR)
            for u in range(2):
                pool.wait_ge(bonus_sent[u], 64)
                pool.wait_ge(gate_sent[u], 64)
            nc.gpsimd.memset(state[0][:, :, :], 0.0).then_inc(state_ready, 1)
            for u in range(2):
                nc.gpsimd.memset(vz[u][:, :, :], 0.0).then_inc(state_ready, 1)
            nc.gpsimd.memset(cum[:, :, 0:1], 0.0).then_inc(state_ready, 1)

            def prepare(f, u):
                pool.wait_ge(cin_in[u], 8 * f + 16 - 8 * u)
                pool.wait_ge(c_exp, f + 1 + 1)
                pool.wait_ge(c_tr, f + 1)
                for e in range(2):
                    r = slice(64 * e, 64 * e + 64)
                    k_half = bk[r, :, C * (1 - e):C * (1 - e) + C]
                    nc.gpsimd.tensor_tensor(k_half, cin[u][r, 4, :, :], pneg[r, :, :], ALU.mult).then_inc(c_k, 1)

            def slot_pool(s, u):
                if not isinstance(s, int) or s <= CHUNKS:
                    pool.wait_ge(c_gm, 2 * s + 2 + 1)
                    pool.wait_ge(c_xmm, LEVELS * s + 1)
                    for l in range(LEVELS):
                        for e in range(2):
                            r = slice(64 * e, 64 * e + 64)
                            lv = con[r, K_LEVEL + C * l:K_LEVEL + C * l + C].unsqueeze(1).broadcast_to([64, PAIRS, C])
                            nc.gpsimd.tensor_tensor(nlev[r, l, :, :], gm[u][r, e, :, 0:C], lv, ALU.mult).then_inc(c_lev, 1)
                if not isinstance(s, int) or s >= 1:
                    pool.wait_ge(c_tm, s + 1)
                    pool.wait_ge(c_ymm, s)
                    pool.sem_inc(pool_waited, 1)
                    nc.gpsimd.tensor_copy(uv[0:64, :, 64:128], vz[1 - u][0:64, :, 64:128]).then_inc(c_uvv, 1)
                    nc.gpsimd.tensor_copy(uv[64:128, :, 0:64], vz[1 - u][64:128, :, 0:64]).then_inc(c_uvv, 1)
                if not isinstance(s, int) or s < CHUNKS:
                    prepare(s + 1, 1 - u)

            prepare(0, 0)
            slot_pool(0, 0)
            with pool.Fori(0, CHUNKS // 2 - 1) as s2:
                for x in (1, 2):
                    slot_pool(2 * s2 + x, x % 2)
            for x in range(CHUNKS - 1, SLOTS):
                slot_pool(x, x % 2)
            pool.wait_ge(hi_ready, 6)
            pool.wait_ge(lo_ready, 6)
            nc.gpsimd.memset(acc[:, :, :], 0.0).then_inc(acc_zero, 1)

        @block.scalar
        def _(act):
            step = Steps(act, s_step)
            start_at_one(act, c_exp, c_tm, c_yev)
            act.wait_ge(vec_in, 16)
            nc.scalar.activation(cs_c[:, :, :].rearrange("p a b -> p (a b)"), vec[:, V_C:V_C + 16], ACT.Silu).then_inc(silu_c, 1)
            act.wait_ge(const_in, 16)

            def put_row(n, row, bank):
                act.wait_ge(slab_mm, n + 1)
                if n % EARLY >= 2:
                    act.wait_ge(turned, n - 1)
                nc.scalar.copy(row[n % 2][:, :], ps[0:2, bank + n % 2, :]).then_inc(mrow_ready, 1)

            def modulation(n, bank):
                act.wait_ge(turned, n + 1)
                for j in range(4):
                    ins = nc.scalar.activation(mod[:, 4 * n + j, :], ps[:, bank, 8 * (n % 4) + 2 * j:8 * (n % 4) + 2 * j + 2], ACT.Identity,
                                               bias=vec[:, V_ADAB + 4 * n + j:V_ADAB + 4 * n + j + 1])
                    if j < 3:
                        step.mark(ins)
                ins.then_inc(mod_done, 1)

            for c in range(3):
                act.wait_ge(x_in[c], 16)
                norm_squares(act, "n1", x1, sq1, c)
                norm_root(act, "n1", c)
                if c:
                    put_row(c - 1, mrow, 0)
            modulation(0, 2)
            for n in range(2, EARLY):
                put_row(n, mrow, 0)
                modulation(n - 1, 2)
            modulation(EARLY - 1, 2)

            def affine_split(src, c, gain, shift, count):
                act.wait_ge(xn_ready, count + 1)
                a, n = CH[c]
                for k in range(KD):
                    for b, w, s in segments(c):
                        step.mark(nc.scalar.activation(src[:, k, b:b + w], src[:, k, b:b + w], ACT.Identity,
                                                       bias=mod[:, shift + k, s:s + 1], scale=gains[:, gain, k, s:s + 1]))
                step.wait()
                nc.scalar.copy(hhi[:, :, a:a + n], src[:, :, a:a + n]).then_inc(hi_ready, 1)

            act.wait_ge(gains_done, 1)
            act.wait_ge(mod_done, EARLY)
            for c in range(3):
                affine_split(x1, c, 0, 0, c)

            def put_chunks(u, m, place):
                for c in range(3):
                    act.wait_ge(out_ready[u], 3 * m + c + 1)
                    parts = place(c)
                    for j, (dst, a, n) in enumerate(parts):
                        ins = nc.scalar.copy(dst, ps[:, 3 * u + c, a:a + n])
                        if j == len(parts) - 1:
                            ins.then_inc(bank_free[u], 1)
                        else:
                            step.mark(ins)

            split_hi(act, 0, 0, first=True)
            split_hi(act, 0, 1, first=True)
            act.wait_ge(lo_ready, 3)
            act.wait_ge(mod_done, EARLY)
            for n in range(MLA_TILES):
                m, u = n // 2, n % 2
                if n < KQ:
                    put_chunks(u, m, lambda c: [(cq[:, n, CH[c][0]:CH[c][0] + CH[c][1]], 0, CH[c][1])])
                elif n < KQ + KKV:
                    put_chunks(u, m, lambda c: [(ckv[:, n - KQ, CH[c][0]:CH[c][0] + CH[c][1]], 0, CH[c][1])])
                else:
                    put_chunks(u, m, lambda c: [(mix[:, 12, CH[c][0]:CH[c][0] + CH[c][1]], 0, CH[c][1])])
                split_hi(act, m + 1, u)

            def raw_place(u):
                def place(c):
                    a, n = CH[c]
                    if c < 2:
                        return [(raw[u][:, 1 + a:1 + a + n], 0, n)]
                    return [(raw[u][:, 1 + a:1 + TP], 0, TP - a), (raw[u][:, TM + 1 - TS:TM + 1], TP - a, TS)]
                return place

            def raw_rows(m, j, u, first=False):
                if not first:
                    act.wait_ge(mix_done, j - 1)
                step.mark(nc.scalar.copy(raw[u][:, TP + 1:TP + 2], vec[:, bass.ds(j + V_SHIFT, 1)]))
                put_chunks(u, m, raw_place(u))
                step.wait()
                act.wait_ge(bank_free[u], 3 * m + 3)
                step.mark(nc.scalar.copy(sh_out[:, bass.ds(j, 1), :].rearrange("p a b -> p (a b)"), raw[u][:, TP:TM + 1:TM - TP]))
                nc.scalar.mul(mix[:, bass.ds(j, 1), :].rearrange("p a b -> p (a b)"), raw[u][:, 0:TM],
                              vec[:, bass.ds(j + V_MU, 1)]).then_inc(raw_ready, 1)

            act.wait_ge(raw_zero, 2)
            RM = MLA_TILES // 2
            for u in range(2):
                raw_rows(RM, u, u, first=True)
                split_hi(act, RM + 1, u)
            with step.loop(RW_TILES // 2 - 2, 6) as i:
                for u in range(2):
                    raw_rows(i + RM + 1, 2 * i + 2 + u, u)
                    split_hi(act, i + RM + 2, u)
            for u in range(2):
                raw_rows(OUT_M - 1, RW_TILES - 2 + u, u)

            for u in range(2):
                act.wait_ge(out_ready[u], 3 * OUT_M)
            for name, src in (("q", cq), ("kv", ckv)):
                for c in range(3):
                    norm_squares(act, name, src, sq_lat, c)
                    norm_root(act, name, c)

            act.wait_ge(mix_done, RW_TILES)
            nc.scalar.activation(mix[0:64, 12, :], mix[0:64, 12, :], ACT.Tanh).then_inc(lora_act, 1)
            nc.scalar.activation(mix[:, 13, :], mix[:, 13, :], ACT.Sigmoid).then_inc(lora_act, 1)
            for j in range(KR):
                for s, (dst, vcol) in enumerate(((lw, V_W0), (bb, V_A0))):
                    act.wait_ge(lora_mm, 2 * j + s + 1)
                    nc.scalar.activation(dst[:, j, :].rearrange("p (c n) -> p c n", c=3), ps[:, 3 * s:3 * s + 3, 0:CM], ACT.Sigmoid,
                                         bias=vec[:, vcol + j:vcol + j + 1]).then_inc(lora_ev, 1)
            for j in range(KR):
                for c in range(3):
                    q = 3 * j + c
                    act.wait_ge(gate_mm, q + 1)
                    if c == 0 and j >= 2:
                        act.wait_ge(gate_sent[j % 2], 32)
                    nc.scalar.copy(gout[j % 2][:, CM * c:CM * c + CM], ps[:, 6 + q % 2, 0:CM]).then_inc(gate_ev, 1)
            for j in range(KR):
                act.wait_ge(kk_raw, j + 1)
                if j:
                    act.wait_ge(kk_mm, j)
                nc.scalar.activation(sqr[:, :], kk[:, j, :], ACT.Square).then_inc(kk_sq, 1)
                act.wait_ge(kk_mm, j + 1)
                if j:
                    act.wait_ge(pre_done, j)
                nc.scalar.activation(rn[:, :].rearrange("p (c n) -> p c n", c=3), ps[:, 0:3, 0:CM], ACT.Sqrt).then_inc(kk_root, 1)

            act.wait_ge(past_in, 48)
            act.wait_ge(krope_put, 1)
            for e in range(2):
                nc.scalar.copy(kt[e][64:96, 0:T], krope[64:96, :]).then_inc(krope_copied, 1)

            def prepare_scalar(f, u):
                act.wait_ge(c_cum, f + 1)
                act.wait_ge(c_k, 2 * f + 1)
                at_least(act, c_ab, f)
                at_least(act, c_sev, f)
                nc.scalar.activation(pinc[u][:, :, :], cum[:, :, :], ACT.Exp, scale=-DECAY).then_inc(c_exp_a, 1)
                nc.scalar.activation(pneg[:, :, :], cum[:, :, 1:C + 1], ACT.Exp, scale=DECAY).then_inc(c_exp, 1)
                act.wait_ge(c_tr, f + 1)
                nc.scalar.copy(vv[:, :, :, :], cin[u][:, 5, :, :].unsqueeze(2).broadcast_to([P, PAIRS, 2, C])).then_inc(c_v, 1)

            def level_copy(j, l):
                act.wait_ge(c_xmm, LEVELS * j + l + 1 + 1)
                act.wait_ge(c_tmm, (LEVELS - 1) * j + l)
                nc.scalar.copy(xt[:, :, :].rearrange("p a b -> p (a b)"), ps[:, WB, 0:PAIRS * C]).then_inc(c_xev, 1)

            def right_side(i):
                act.wait_ge(c_rmm, i + 1)
                nc.scalar.mul(rhs[:, :, :].rearrange("p a b -> p (a b)"), ps[:, WB + 1, 0:PAIRS * C], -1.0).then_inc(c_rev, 1)

            def put_u(i):
                act.wait_ge(c_umm, i + 1 + 1)
                u3 = ps[:, WB + 1, 0:PAIRS * DH].rearrange("p (a b) -> p a b", a=PAIRS)
                act.wait_ge(c_ymm, i + 1)
                step.mark(nc.scalar.copy(uv[0:64, :, 0:64], u3[0:64, :, :]))
                nc.scalar.copy(uv[64:128, :, 64:128], u3[64:128, :, :]).then_inc(c_uev, 1)

            def put_y(i, u):
                act.wait_ge(c_ymm, i + 1 + 1)
                act.wait_ge(c_sev, i + 1 + 1)
                act.wait_ge(y_sent[u], 8 * i - 8 * u + 16)
                nc.scalar.copy(ybuf[u][:, :, :].rearrange("p a b -> p (a b)"), ps[:, WB + 1, PAIRS * C:2 * PAIRS * C]).then_inc(c_yev, 1)

            def slot_scalar(s, u):
                later = not isinstance(s, int) or s >= 1
                if isinstance(s, int) and s > CHUNKS:
                    right_side(s - 1)
                    yield
                    put_u(s - 1)
                    yield
                    yield
                    put_y(s - 1, 1 - u)
                    yield
                    return
                yield
                act.wait_ge(c_tr, s + 1 + 1)
                at_least(act, c_smm, s)
                step.mark(nc.scalar.copy(bktm[u][:, :, :].rearrange("p a b -> p (a b)"), ps[:, WB, :]))
                v3 = ps[:, WB + 1, :].rearrange("p (a b) -> p a b", a=PAIRS)
                step.mark(nc.scalar.copy(vz[u][0:64, :, 64:128], v3[0:64, :, 64:128]))
                nc.scalar.copy(vz[u][64:128, :, 0:64], v3[64:128, :, 0:64]).then_inc(c_tm, 1)
                yield
                if later:
                    right_side(s - 1)
                yield
                level_copy(s, 1)
                yield
                if later:
                    put_u(s - 1)
                yield
                level_copy(s, 2)
                yield
                yield
                level_copy(s, 3)
                if later:
                    put_y(s - 1, 1 - u)
                yield
                if not isinstance(s, int) or s < CHUNKS:
                    prepare_scalar(s + 1, 1 - u)
                yield
                for l in range(4, LEVELS):
                    level_copy(s, l)
                    yield
                    yield

            def attend_scalar(hp):
                for l, (dst, n) in enumerate(K_CHUNKS):
                    act.wait_ge(kp_mm, 7 * hp + l + 1)
                    nc.scalar.copy(kt[0][0:64, dst:dst + n], ps[0:64, l % 4, 0:n]).then_inc(ka_ev, 1)
                    yield
                for e in range(2):
                    for c, (a, n) in enumerate(CH):
                        l = 3 * e + c
                        act.wait_ge(qp_mm, 6 * hp + l + 1)
                        nc.scalar.mul(qt[e][0:64, a:a + n], ps[0:64, 4 + l % 2, 0:n], SCALE).then_inc(qa_ev, 1)
                        yield
                for g, tiles in enumerate(V_GROUPS):
                    act.wait_ge(vp_mm, 7 * hp + g + 1)
                    rows = TS if tiles == [8] else P
                    nc.scalar.copy(vt[0:rows, tiles[0]:tiles[-1] + 1, :],
                                   ps[0:rows, (7 + g) % 4, 0:P * len(tiles)].rearrange("p (a b) -> p a b", b=P)).then_inc(v_ev, 1)
                    yield
                for kind, jb, g in JOB_UNITS:
                    if kind == "scores":
                        exponentials(jb, hp)
                    if kind == "turn":
                        put_probs(jb, g, hp)
                    yield

            def exponentials(jb, hp):
                u = jb % 2
                act.wait_ge(nmax, JOBS * hp + jb + 1)
                act.wait_ge(t_mm, T_GROUPS * hp + (T_FIRST[jb - 1] if jb >= 2 else 0) + 1)
                if jb < PJOBS:
                    n = P * (jb // 2 + 1)
                    dst, src, r = probs[u][:, 0:n], ps[:, 2 * u:2 * u + 2, :].rearrange("p a b -> p (a b)")[:, 0:n], slice(0, P)
                else:
                    dst, src, r = probs[u][0:TS, :].rearrange("p (a b) -> p a b", a=6), ps[0:TS, 0:6, 0:352], slice(0, TS)
                nc.scalar.activation(dst, src, ACT.Exp, bias=sm[r, 0, u:u + 1], accum_out=sm[r, 1, u:u + 1]).then_inc(p_exp, 1)

            def put_probs(jb, g, hp):
                u = jb % 2
                t0, t1 = T_PLAN[jb][g]
                act.wait_ge(o_mm, JOBS * hp + max(jb - 1, 0) + 1)
                act.wait_ge(t_mm, T_GROUPS * hp + T_FIRST[jb] + g + 1 + 1)
                w = P if jb < PJOBS else TS
                if jb >= PJOBS and g == 0:
                    step.mark(nc.scalar.copy(pt[u][0:TS, 0:w], ps[0:TS, 4, 0:w]))
                    nc.scalar.copy(pt[u][:, w:t1 * w], ps[:, 4, w:t1 * w]).then_inc(t_ev, 1)
                else:
                    nc.scalar.copy(pt[u][:, t0 * w:t1 * w], ps[:, 4, 0:(t1 - t0) * w]).then_inc(t_ev, 1)

            prepare_scalar(0, 0)
            interleave(attend_scalar(0), ATT_COSTS, slots(slot_scalar, FIRST_SLOTS), slot_units(FIRST_SLOTS))
            with step.loop(range(1, PAIRS - 1), 2 + 4 * 3) as hp:
                interleave(attend_scalar(hp), ATT_COSTS, slots(slot_scalar, MID_SLOTS, 4 * hp), slot_units(MID_SLOTS))
            interleave(attend_scalar(PAIRS - 1), ATT_COSTS, slots(slot_scalar, LAST_SLOTS), slot_units(LAST_SLOTS))

            def y_squares(j):
                act.wait_ge(yc_done, j + 1)
                if j >= 2:
                    act.wait_ge(var_mm, j - 1)
                nc.scalar.activation(ysq[j % 2][:, :], yt[:, j, :], ACT.Square).then_inc(ysq_done, 1)

            for j in range(KR):
                if j < 2:
                    y_squares(j)
                put_row(EARLY + j, late_row, 4)
                if j:
                    modulation(EARLY + j - 1, 6)
            for j in range(KR):
                act.wait_ge(var_mm, j + 1)
                for c, (a, n) in enumerate(CH):
                    ins = nc.scalar.activation(yn[:, j, a:a + n], ps[:, 3 + c, 0:n], ACT.Sqrt, bias=eps_ln, scale=1.0 / DH)
                    if c < 2:
                        step.mark(ins)
                ins.then_inc(y_root, 1)
                if j + 2 < KR:
                    y_squares(j + 2)
                put_row(EARLY + KR + j, late_row, 0)
                modulation(EARLY + KR + j - 1, 6)
            modulation(SLABS - 1, 6)
            for j in range(KR):
                act.wait_ge(y_norm, j + 1)
                nc.scalar.activation(yt[:, j, :], yt[:, j, :], ACT.Identity, bias=vec[:, V_LB + j:V_LB + j + 1],
                                     scale=vec[:, V_LG + j:V_LG + j + 1]).then_inc(y_affine, 1)

            split_hi(act, OUT_M, 0)
            split_hi(act, OUT_M, 1)

            act.wait_ge(o_ev, QTILES * PAIRS + 1)
            act.wait_ge(rw_done, KR)
            act.wait_ge(mod_done, SLABS)
            for dst, src in o_parts(hhi):
                nc.scalar.copy(dst, src).then_inc(osplit_hi, 1)

            act.wait_ge(osplit_lo, 2)
            for n in range(KD):
                m, u = OUT_M + n // 2, n % 2
                put_chunks(u, m, lambda c: [(m1[:, n, CH[c][0]:CH[c][0] + CH[c][1]], 0, CH[c][1])])
                split_hi(act, m + 1, u)
            for u in range(2):
                act.wait_ge(bank_free[u], 3 * FF_M)
            for c in range(3):
                norm_squares(act, "m", m1, sq2, c)
                norm_root(act, "m", c)
            for c in range(3):
                act.wait_ge(x2_done, c + 1)
                norm_squares(act, "n2", x2, sq2, c)
                norm_root(act, "n2", c)
            for c in range(3):
                affine_split(m1, c, 2, 24, 3 + c)

            def down_hi(g, u):
                act.wait_ge(d_in, 16 * (2 * g + u + 1))
                act.wait_ge(down_ready, 24 * g + 1)
                nc.scalar.copy(dhi[u][:, :], draw[:, :]).then_inc(d_hi, 1)

            def gate(g, slot, j, first=False, last=False):
                m = 2 * g + FF_M + j
                q = 6 * g + 3 * j
                for c, (a, n) in enumerate(CH):
                    act.wait_ge(out_ready[0], 3 * m + c + 1)
                    if not (first and j == 0):
                        act.wait_ge(act_lo, q + c - 2)
                    nc.scalar.activation(sil[c][:, 0:n], ps[:, c, 0:n], ACT.Silu).then_inc(sil_ready, 1)
                if not last:
                    split_hi(act, m + 1, 0)
                if not first:
                    act.wait_ge(down_ready, 24 * (g - 1) + 1)
                for c, (a, n) in enumerate(CH):
                    act.wait_ge(prod_ready, q + c + 1)
                    nc.scalar.copy(ahi[:, slot + j, a:a + n], sil[c][:, 0:n]).then_inc(act_hi, 1)
                if not last:
                    split_hi(act, m + 1, 1)

            act.wait_ge(x2_out, 48)
            gate(0, 0, 0, first=True)
            gate(0, 0, 1, first=True)

            def group(g, slot, last=False):
                gate(g, slot, 0)
                down_hi(g - 1, 0)
                down_hi(g - 1, 1)
                gate(g, slot, 1, last=last)

            with act.Fori(0, (GROUPS - 3) // 2) as it:
                group(2 * it + 1, 2)
                group(2 * it + 2, 0)
            group(GROUPS - 2, 2)
            group(GROUPS - 1, 0, last=True)
            down_hi(GROUPS - 1, 0)
            down_hi(GROUPS - 1, 1)

            act.wait_ge(d_added, 24 * GROUPS + 1)
            for c in range(3):
                norm_squares(act, "f", acc, sq3, c)
                norm_root(act, "f", c)

        @block.vector
        def _(dve):
            step = Steps(dve, v_step)
            start_at_one(dve, c_gm, c_sev, o_ev, qd_ev, d_added)
            dve.wait_ge(vec_in, 16)
            dve.wait_ge(const_in, 16)
            step.mark(nc.vector.tensor_scalar(omm[:, :], vec[:, V_MU:V_MU + 14], -1.0, 1.0, ALU.mult, ALU.add))
            step.mark(nc.vector.tensor_scalar(oma[:, :], vec[:, V_KA:V_KA + 4], -1.0, 1.0, ALU.mult, ALU.add))

            def times_rstd(dst, src, c):
                a, n = CH[c]
                nc.vector.tensor_tensor(dst[:, :, a:a + n], src[:, :, a:a + n], over_tiles(rstd[:, a:a + n], KD), ALU.mult).then_inc(xn_ready, 1)

            def rest(src, c, count):
                a, n = CH[c]
                dve.wait_ge(hi_ready, count + 1)
                nc.vector.tensor_tensor(hlo[:, :, a:a + n], src[:, :, a:a + n], hhi[:, :, a:a + n].bitcast(F32), ALU.subtract).then_inc(lo_ready, 1)

            for c in range(3):
                norm_recip(dve, "n1", c)
                dve.wait_ge(x_in[c], 16)
                times_rstd(x1, x1, c)

            def gain(which, at0, plus, last=False):
                g = vec[:, V_NORM + 8 * which:V_NORM + 8 * which + 8].unsqueeze(2).broadcast_to([P, 8, 2])
                ins = nc.vector.scalar_tensor_tensor(out=gains[:, which, :, :], in0=mod[:, at0:at0 + 8, :], scalar=plus, in1=g,
                                                     op0=ALU.add, op1=ALU.mult)
                ins.then_inc(gains_done, 1)

            dve.wait_ge(mod_done, EARLY)
            gain(0, 8, 1.0)
            split_lo(dve, 0, 0)
            split_lo(dve, 0, 1)
            for c in range(3):
                rest(x1, c, c)

            for n in range(MLA_TILES):
                m, u = n // 2, n % 2
                split_lo(dve, m + 1, u)
                if n == MLA_TILES - 1:
                    dve.wait_ge(bank_free[u], 3 * m + 3)
                    step.mark(nc.vector.tensor_tensor(krope[64:96, :], mix[64:96, 12, 0:T], cs[64:96, :], ALU.mult))
                    step.done(nc.vector.tensor_tensor(mix[64:96, 13, 0:T], mix[96:128, 12, 0:T], cs[96:128, :], ALU.mult))
                    nc.vector.tensor_tensor(krope[64:96, :], krope[64:96, :], mix[64:96, 13, 0:T], ALU.add).then_inc(krope_put, 1)
                    dve.wait_ge(krope_put, 1)

            def shift_mix(j, u):
                dve.wait_ge(raw_ready, j + 1)
                m2 = mix[:, bass.ds(j, 1), :].rearrange("p a b -> p (a b)")
                nc.vector.scalar_tensor_tensor(out=m2, in0=raw[u][:, 1:TM + 1], scalar=omm[:, bass.ds(j, 1)], in1=m2,
                                               op0=ALU.mult, op1=ALU.add).then_inc(mix_done, 1)

            step.wait()
            for u in range(2):
                split_lo(dve, MLA_TILES // 2 + 1, u)
                shift_mix(u, u)
            with dve.Fori(0, RW_TILES // 2 - 2) as i:
                for u in range(2):
                    split_lo(dve, i + MLA_TILES // 2 + 2, u)
                    shift_mix(2 * i + 2 + u, u)
            for u in range(2):
                shift_mix(RW_TILES - 2 + u, u)

            for name, src, k, v0 in (("q", cq, KQ, V_QG), ("kv", ckv, KKV, V_KVG)):
                for c, (a, n) in enumerate(CH):
                    norm_recip(dve, name, c)
                    dve.wait_ge(sq_used, first_piece[name] + c + 1)
                    for t in range(k):
                        ins = nc.vector.scalar_tensor_tensor(out=src[:, t, a:a + n], in0=src[:, t, a:a + n], scalar=vec[:, v0 + t:v0 + t + 1],
                                                             in1=rstd[:, a:a + n], op0=ALU.mult, op1=ALU.mult)
                        if t < k - 1:
                            step.mark(ins)
                        else:
                            ins.then_inc(qkv_norm, 1)

            thirds = lambda ap: ap.rearrange("p (c n) -> p c n", c=3)
            dve.wait_ge(mix_done, RW_TILES)
            for u in range(2):
                dve.wait_ge(out_ready[u], 3 * OUT_M)
            for j in range(KR):
                nc.vector.tensor_scalar(kk[:, j, :], mix[:, KR + j, :], vec[:, V_KK + j:V_KK + j + 1], None, ALU.mult).then_inc(kk_raw, 1)
                dve.wait_ge(lora_ev, 2 * j + 2)
                dve.wait_ge(kk_raw, j + 1)
                step.done(nc.vector.tensor_scalar(tmp[:, :], bb[:, j, :], vec[:, V_KA + j:V_KA + j + 1], oma[:, j:j + 1], ALU.mult, ALU.add))
                step.done(nc.vector.tensor_tensor(mix[:, KR + j, :], mix[:, KR + j, :], tmp[:, :], ALU.mult))
                if j >= 2:
                    dve.wait_ge(bonus_sent[j % 2], 32)
                dve.wait_ge(qkv_norm, 6)
                nc.vector.scalar_tensor_tensor(out=bonus[j % 2][:, :], in0=mix[:, j, :], scalar=vec[:, V_RK + j:V_RK + j + 1], in1=mix[:, KR + j, :],
                                               op0=ALU.mult, op1=ALU.mult).then_inc(bonus_raw, 1)
                dve.wait_ge(kk_root, j + 1)
                step.done(nc.vector.tensor_scalar(rn[:, :], rn[:, :], 1e-12, None, ALU.max))
                step.done(nc.vector.reciprocal(rn[:, :], rn[:, :]))
                dve.wait_ge(kk_sq, j + 1)
                step.done(nc.vector.tensor_tensor(kk[:, j, :], kk[:, j, :], rn[:, :], ALU.mult))
                nc.vector.tensor_tensor(bb[:, j, :], bb[:, j, :], kk[:, j, :], ALU.mult).then_inc(pre_done, 1)
                dve.wait_ge(bonus_mm, j + 1)
                nc.vector.tensor_tensor(thirds(bonus[j % 2][:, :]), ps[:, 3:6, 0:CM], thirds(mix[:, 2 * KR + j, :]), ALU.mult).then_inc(bonus_done, 1)

            def prepare_sums(f, u):
                dve.wait_ge(cin_in[u], 8 * f + 16 - 8 * u)
                dve.wait_ge(c_exp, f + 1)
                for p in range(PAIRS):
                    ins = nc.vector.tensor_tensor_scan(cum[:, p, 1:C + 1], ones[:, 0:C], cin[u][:, 0, p, :], 0.0, ALU.mult, ALU.add)
                    if p < PAIRS - 1:
                        step.mark(ins)
                    else:
                        ins.then_inc(c_cum, 1)

            def prepare_rows(f, u):
                x, a = cin[u], ar[u]
                dve.wait_ge(c_exp, f + 1 + 1)
                dve.wait_ge(c_tr, f + 1)
                at_least(dve, c_ymm, f)
                step.mark(nc.vector.tensor_tensor(a[:, :, 0:C], x[:, 1, :, :], pinc[u][:, :, 0:C], ALU.mult))
                step.mark(nc.vector.tensor_tensor(a[:, :, C:2 * C], x[:, 3, :, :], pinc[u][:, :, 1:C + 1], ALU.mult))
                step.mark(nc.vector.tensor_tensor(bk[0:64, :, 0:C], x[0:64, 2, :, :], pneg[0:64, :, :], ALU.mult))
                nc.vector.tensor_tensor(bk[64:128, :, C:2 * C], x[64:128, 2, :, :], pneg[64:128, :, :], ALU.mult).then_inc(c_ab, 1)

            def causal(j, u):
                dve.wait_ge(c_lev, 2 * LEVELS * j + 1)
                at_least(dve, c_ymm, j)
                for e in range(2):
                    dve.wait_ge(c_gmm, 2 * j + e + 1)
                    nc.vector.tensor_tensor(gm[u][:, e, :, :], ps[:, WB + e, :].rearrange("p (a b) -> p a b", a=PAIRS),
                                            gmask.unsqueeze(1).broadcast_to([P, PAIRS, P]), ALU.mult).then_inc(c_gm, 1)

            def invert_first(j, u):
                eye4 = eye2.unsqueeze(1).broadcast_to([P, PAIRS, C])
                dve.wait_ge(c_lev, 2 * LEVELS * j + 2 + 1)
                at_least(dve, c_umm, j)
                step.mark(nc.vector.tensor_tensor(tt[u][:, 0, :, :], nlev[:, 0, :, :], eye4, ALU.add))
                dve.wait_ge(c_xmm, LEVELS * j + 1 + 1)
                nc.vector.tensor_tensor(tt[u][:, 1, :, :], ps[:, WB, 0:PAIRS * C].rearrange("p (a b) -> p a b", a=PAIRS), eye4, ALU.add).then_inc(c_tev, 1)
                step.wait()

            def invert_level(j, u, l):
                n = 2 if l < LEVELS - 1 else 1
                dve.wait_ge(c_tev, LEVELS * j + l)
                dve.wait_ge(c_tmm, (LEVELS - 1) * j + l + 1)
                t2 = tt[u][:, 0:n, :, :].rearrange("p a b c -> p (a b c)")
                nc.vector.tensor_tensor(t2, t2, ps[:, WB, 0:n * PAIRS * C], ALU.add).then_inc(c_tev, 1)

            def next_state(i, u, last):
                st = state[1 if last else 0]
                dve.wait_ge(c_smm, i + 1 + 1)
                dve.wait_ge(c_ymm, i + 1 + 1)
                step.done(nc.vector.tensor_tensor(st[:, :, :], st[:, :, :], ps[:, WB + 1, 0:PAIRS * DH].rearrange("p (a b) -> p a b", a=PAIRS), ALU.add))
                nc.vector.tensor_tensor(st[:, :, :], st[:, :, :], pinc[u][:, :, C:C + 1].broadcast_to([P, PAIRS, DH]), ALU.mult).then_inc(c_sev, 1)

            def slot_vector(s, u):
                later = not isinstance(s, int) or s >= 1
                if isinstance(s, int) and s > CHUNKS:
                    yield
                    yield
                    next_state(s - 1, 1 - u, True)
                    yield
                    yield
                    return
                causal(s, u)
                yield
                yield
                invert_first(s, u)
                yield
                yield
                invert_level(s, u, 1)
                yield
                yield
                invert_level(s, u, 2)
                if later:
                    next_state(s - 1, 1 - u, False)
                yield
                more = not isinstance(s, int) or s < CHUNKS
                if more:
                    prepare_sums(s + 1, 1 - u)
                yield
                invert_level(s, u, 3)
                yield
                if more:
                    prepare_rows(s + 1, 1 - u)
                yield
                for l in range(4, LEVELS):
                    invert_level(s, u, l)
                    yield
                    if l < LEVELS - 1:
                        yield

            def job_max(jb, hp):
                u = jb % 2
                dve.wait_ge(s_mm, JOBS * hp + jb + 1)
                if jb < PJOBS:
                    n = P * (jb // 2 + 1)
                    scores = ps[:, 2 * u:2 * u + 2, :].rearrange("p a b -> p (a b)")
                    step.done(nc.vector.memset(scores[0:C, n - C:n], NEG))
                    nc.vector.tensor_reduce(sm[:, 0, u:u + 1], scores[:, 0:n], AX_X, ALU.max, negate=True).then_inc(nmax, 1)
                else:
                    nc.vector.tensor_reduce(sm[0:TS, 0, u:u + 1], ps[0:TS, 0:6, 0:352], mybir.AxisListType.XY, ALU.max, negate=True).then_inc(nmax, 1)

            def job_norm(jb, hp):
                u = jb % 2
                r = slice(0, P if jb < PJOBS else TS)
                n = P * (jb // 2 + 1) if jb < PJOBS else TS + PAST
                dve.wait_ge(p_exp, JOBS * hp + jb + 1)
                step.done(nc.vector.reciprocal(sm[r, 2, u:u + 1], sm[r, 1, u:u + 1]))
                nc.vector.tensor_scalar(probs[u][r, 0:n], probs[u][r, 0:n], sm[r, 2, u:u + 1], None, ALU.mult).then_inc(p_norm, 1)

            def put_out(i, hp):
                a, w = (P * i, P) if i < QTILES - 1 else (TP, TS)
                dve.wait_ge(o_mm, JOBS * hp + 2 * i + 2 + 1)
                nc.vector.tensor_copy(oatt[:, bass.ds(hp, 1), a:a + w].rearrange("p a b -> p (a b)"), ps[:, 5, 0:w]).then_inc(o_ev, 1)

            def attend_vector(hp):
                for l, (dst, n) in enumerate(K_CHUNKS):
                    dve.wait_ge(kp_mm, 7 * hp + l + 1)
                    nc.vector.tensor_copy(kt[1][0:64, dst:dst + n], ps[64:128, l % 4, 0:n]).then_inc(kd_ev, 1)
                    yield
                for e in range(2):
                    for c, (a, n) in enumerate(CH):
                        l = 3 * e + c
                        dve.wait_ge(qp_mm, 6 * hp + l + 1)
                        dve.wait_ge(qd_ev, 6 * hp + l + 1)
                        step.mark(nc.vector.scalar_tensor_tensor(out=rtmp[0][64:96, 0:n], in0=ps[64:96, 4 + l % 2, 0:n], scalar=SCALE,
                                                                 in1=cs[64:96, a:a + n], op0=ALU.mult, op1=ALU.mult))
                        step.done(nc.vector.scalar_tensor_tensor(out=rtmp[1][64:96, 0:n], in0=ps[96:128, 4 + l % 2, 0:n], scalar=SCALE,
                                                                 in1=cs[96:128, a:a + n], op0=ALU.mult, op1=ALU.mult))
                        nc.vector.tensor_tensor(qt[e][64:96, a:a + n], rtmp[0][64:96, 0:n], rtmp[1][64:96, 0:n], ALU.add).then_inc(qd_ev, 1)
                        yield
                for g in V_GROUPS:
                    yield
                pending = []
                for kind, jb, g in JOB_UNITS:
                    if kind == "scores":
                        for x in pending:
                            job_norm(x, hp)
                        pending = [jb]
                        job_max(jb, hp)
                    else:
                        for x in pending:
                            job_norm(x, hp)
                        pending = []
                    if kind == "values" and jb % 2:
                        put_out(jb // 2, hp)
                    yield

            dve.wait_ge(state_ready, 4)
            prepare_sums(0, 0)
            prepare_rows(0, 0)
            interleave(attend_vector(0), ATT_COSTS, slots(slot_vector, FIRST_SLOTS), slot_units(FIRST_SLOTS))
            with step.loop(range(1, PAIRS - 1), 12 + PJOBS + JOBS + 4 * 8) as hp:
                interleave(attend_vector(hp), ATT_COSTS, slots(slot_vector, MID_SLOTS, 4 * hp), slot_units(MID_SLOTS))
            dve.wait_ge(state_in, 16)
            interleave(attend_vector(PAIRS - 1), ATT_COSTS, slots(slot_vector, LAST_SLOTS), slot_units(LAST_SLOTS))

            dve.wait_ge(y_back, 16 * KR)
            for j in range(KR):
                for c, (a, n) in enumerate(CH):
                    dve.wait_ge(mean_mm, 3 * j + c + 1)
                    ins = nc.vector.scalar_tensor_tensor(out=yt[:, j, a:a + n], in0=ps[:, c, 0:n], scalar=-1.0 / DH, in1=yt[:, j, a:a + n],
                                                         op0=ALU.mult, op1=ALU.add)
                    if c < 2:
                        step.mark(ins)
                ins.then_inc(yc_done, 1)
            step.wait()
            dve.wait_ge(yc_done, KR)
            for j in range(KR):
                dve.wait_ge(y_root, j + 1)
                step.done(nc.vector.reciprocal(yn[:, j, :], yn[:, j, :]))
                dve.wait_ge(ysq_done, j + 1)
                nc.vector.tensor_tensor(yt[:, j, :], yt[:, j, :], yn[:, j, :], ALU.mult).then_inc(y_norm, 1)
            dve.wait_ge(bg_back, 32)
            for j in range(KR):
                dve.wait_ge(y_affine, j + 1)
                step.done(nc.vector.tensor_tensor(yt[:, j, :], yt[:, j, :], bon[:, j, :], ALU.add))
                nc.vector.tensor_tensor(yt[:, j, :], yt[:, j, :], gat[:, j, :], ALU.mult).then_inc(rw_done, 1)

            dve.wait_ge(mod_done, SLABS)
            gain(1, 16, 0.0)
            gain(2, 32, 1.0)
            gain(3, 40, 0.0)
            dve.wait_ge(o_ev, QTILES * PAIRS + 1)
            dve.wait_ge(rw_done, KR)
            for i, (dst, src) in enumerate(o_parts(hlo)):
                dve.wait_ge(osplit_hi, i + 1)
                hi = o_parts(hhi)[i][0].bitcast(F32)
                nc.vector.tensor_tensor(dst, src, hi, ALU.subtract).then_inc(osplit_lo, 1)

            split_lo(dve, OUT_M, 0)
            split_lo(dve, OUT_M, 1)
            for n in range(KD):
                split_lo(dve, OUT_M + 1 + n // 2, n % 2)

            def residual(dst, src, which, c, signal):
                parts = [(k, b, w, s) for k in range(KD) for b, w, s in segments(c)]
                for i, (k, b, w, s) in enumerate(parts):
                    ins = nc.vector.scalar_tensor_tensor(out=dst[:, k, b:b + w], in0=src[:, k, b:b + w], scalar=gains[:, which, k, s:s + 1],
                                                         in1=dst[:, k, b:b + w], op0=ALU.mult, op1=ALU.add)
                    if i < len(parts) - 1:
                        step.mark(ins)
                    else:
                        ins.then_inc(signal, 1)

            dve.wait_ge(x2_in, 48)
            for c, (a, n) in enumerate(CH):
                norm_recip(dve, "m", c)
                step.done(nc.vector.tensor_tensor(m1[:, :, a:a + n], m1[:, :, a:a + n], over_tiles(rstd[:, a:a + n], KD), ALU.mult))
                residual(x2, m1, 1, c, x2_done)
            step.wait()
            dve.wait_ge(x2_done, 3)
            for c in range(3):
                norm_recip(dve, "n2", c)
                times_rstd(m1, x2, c)
            for c in range(3):
                rest(m1, c, 3 + c)

            def down_lo(g, u):
                dve.wait_ge(d_hi, 2 * g + u + 1)
                nc.vector.tensor_tensor(dlo[u][:, :], draw[:, :], dhi[u][:, :].bitcast(F32), ALU.subtract).then_inc(d_lo, 1)

            def product(g, slot, j, last=False):
                m = 2 * g + FF_M + j
                q = 6 * g + 3 * j
                if not last:
                    split_lo(dve, m + 1, 0)
                for c, (a, n) in enumerate(CH):
                    dve.wait_ge(sil_ready, q + c + 1)
                    dve.wait_ge(out_ready[1], 3 * m + c + 1)
                    nc.vector.tensor_tensor(sil[c][:, 0:n], sil[c][:, 0:n], ps[:, 3 + c, 0:n], ALU.mult).then_inc(prod_ready, 1)
                for c, (a, n) in enumerate(CH):
                    dve.wait_ge(act_hi, q + c + 1)
                    nc.vector.tensor_tensor(alo[:, slot + j, a:a + n], sil[c][:, 0:n], ahi[:, slot + j, a:a + n].bitcast(F32),
                                            ALU.subtract).then_inc(act_lo, 1)
                if not last:
                    split_lo(dve, m + 1, 1)

            def add_down(g):
                for x in range(24):
                    k, (a, n) = x // 3, CH[x % 3]
                    dve.wait_ge(down_ready, 24 * g + x + 1 + 1)
                    nc.vector.tensor_tensor(acc[:, k, a:a + n], acc[:, k, a:a + n], ps[:, 6 + x % 2, 0:n], ALU.add).then_inc(d_added, 1)

            def group(g, slot, last=False):
                product(g, slot, 0)
                down_lo(g - 1, 0)
                down_lo(g - 1, 1)
                product(g, slot, 1, last=last)
                dve.wait_ge(d_added, 24 * (g - 1) + 1)
                add_down(g - 1)

            dve.wait_ge(acc_zero, 1)
            product(0, 0, 0)
            product(0, 0, 1)
            with dve.Fori(0, (GROUPS - 3) // 2) as it:
                group(2 * it + 1, 2)
                group(2 * it + 2, 0)
            group(GROUPS - 2, 2)
            group(GROUPS - 1, 0, last=True)
            down_lo(GROUPS - 1, 0)
            down_lo(GROUPS - 1, 1)
            dve.wait_ge(d_added, 24 * (GROUPS - 1) + 1)
            add_down(GROUPS - 1)

            dve.wait_ge(d_added, 24 * GROUPS + 1)
            dve.wait_ge(x3_in, 16)
            for c, (a, n) in enumerate(CH):
                norm_recip(dve, "f", c)
                dve.wait_ge(sq_used, first_piece["f"] + 2 * c + 2)
                step.done(nc.vector.tensor_tensor(acc[:, :, a:a + n], acc[:, :, a:a + n], over_tiles(rstd[:, a:a + n], KD), ALU.mult))
                residual(x3, acc, 3, c, y_done)

        @block.tensor
        def _(pe):
            def before_small():
                pe.sem_inc(waited, 1)

            start_at_one(pe, c_tr, c_xmm, c_ymm, c_smm, c_tmm, c_umm, t_mm, o_mm, down_ready)
            pe.wait_ge(const_in, 16)

            def ada(n, source, filled, bank):
                pe.wait_ge(filled, 16 * ((n - EARLY) // 2 + 1 if n >= EARLY else 1))
                if n % EARLY >= 2:
                    pe.wait_ge(mrow_ready, n - 1)
                for k in range(KD):
                    mm = nc.tensor.matmul(ps[0:2, bank + n % 2, :], cs_c[:, k, :], source[:, k, :], start=(k == 0), stop=(k == KD - 1))
                mm.then_inc(slab_mm, 1)

            def turn_row(n, row, bank):
                pe.wait_ge(mrow_ready, n + 1)
                if n:
                    pe.wait_ge(mod_done, n)
                for j in range(4):
                    mm = nc.tensor.matmul(ps[:, bank, 8 * (n % 4) + 2 * j:8 * (n % 4) + 2 * j + 2], row[n % 2][:, P * j:P * j + P], con[0:2, 0:2],
                                          start=True, stop=True)
                mm.then_inc(turned, 1)

            pe.wait_ge(silu_c, 1)
            for n in range(EARLY):
                if n < 3:
                    norm_sum(pe, "n1", sq1, n)
                ada(n, slab[n], slab_in[n], 0)
                if n:
                    turn_row(n - 1, mrow, 2)
            turn_row(EARLY - 1, mrow, 2)

            pe.wait_ge(mod_done, EARLY)
            project(pe, 0, 0, first=True, tokens=0)
            project(pe, 0, 1, first=True)
            with pe.Fori(1, OUT_M) as m:
                for u in range(2):
                    project(pe, m, u)
            for u in range(2):
                pe.wait_ge(bank_free[u], 3 * OUT_M)

            for name in ("q", "kv"):
                for c in range(3):
                    norm_sum(pe, name, sq_lat, c)

            pe.wait_ge(lora_act, 2)
            pe.wait_ge(mix_done, RW_TILES)
            pe.wait_ge(lora_in, 32)
            for j in range(KR):
                for s in range(2):
                    if j:
                        pe.wait_ge(lora_ev, 2 * j + s - 1)
                    for c in range(3):
                        mm = nc.tensor.matmul(ps[:, 3 * s + c, 0:CM], w2a2[64 * s:64 * s + 64, P * j:P * j + P],
                                              mix[64 * s:64 * s + 64, 12, CM * c:CM * c + CM], start=True, stop=True)
                    mm.then_inc(lora_mm, 1)
            pe.wait_ge(root_ready, chunk_no["kv"] + 3)
            for q in range(3 * KR):
                j, c = q // 3, q % 3
                if q >= 2:
                    pe.wait_ge(gate_ev, q - 1)
                nc.tensor.matmul(ps[:, 6 + q % 2, 0:CM], g2[:, P * j:P * j + P], mix[:, 13, CM * c:CM * c + CM], start=True, stop=True).then_inc(gate_mm, 1)

            def block_sum(src, b, signal):
                for c in range(3):
                    mm = nc.tensor.matmul(ps[:, b + c, 0:CM], block64, src[:, CM * c:CM * c + CM], start=True, stop=True)
                mm.then_inc(signal, 1)

            pe.wait_ge(lora_ev, 2 * KR)
            for j in range(KR):
                pe.wait_ge(kk_sq, j + 1)
                if j:
                    pe.wait_ge(kk_root, j)
                block_sum(sqr, 0, kk_mm)
                pe.wait_ge(bonus_raw, j + 1)
                if j:
                    pe.wait_ge(bonus_done, j)
                block_sum(bonus[j % 2], 3, bonus_mm)
            pe.wait_ge(kk_root, KR)
            pe.wait_ge(bonus_done, KR)
            pe.wait_ge(state_ready, 3)

            def per_head():
                return [(p, e, slice(64 * e, 64 * e + 64)) for p in range(PAIRS) for e in range(2)]

            def products(j, u):
                pe.wait_ge(c_ab, j + 1)
                pe.wait_ge(c_k, 2 * j + 2 + 1)
                at_least(pe, c_tev, LEVELS * j)
                at_least(pe, c_sev, j)
                at_least(pe, c_yev, j)
                before_small()
                for e in range(2):
                    r = slice(64 * e, 64 * e + 64)
                    for p in range(PAIRS):
                        mm = nc.tensor.matmul(ps[:, WB + e, P * p:P * p + P], bk[r, p, :], ar[u][r, p, :], start=True, stop=True)
                    mm.then_inc(c_gmm, 1)

            def turns(j, u):
                pe.wait_ge(c_v, j + 1)
                pe.wait_ge(c_gm, 2 * j + 2 + 1)
                for p in range(PAIRS):
                    nc.tensor.transpose(ps[:, WB, P * p:P * p + P], bk[:, p, :], ident)
                for p in range(PAIRS):
                    mm = nc.tensor.transpose(ps[:, WB + 1, P * p:P * p + P], vv[:, p, :, :].rearrange("p a b -> p (a b)"), ident)
                mm.then_inc(c_tr, 1)

            def level_x(j, u, l):
                if l == 0:
                    pe.wait_ge(c_tm, j + 1 + 1)
                pe.wait_ge(c_lev, 2 * LEVELS * j + 2 * l + 2 + 1)
                if l:
                    pe.wait_ge(c_tev, LEVELS * j + l)
                before_small()
                for p, e, r in per_head():
                    x = tt[u][r, 1, p, :] if l else con[r, K_EYE2:K_EYE2 + C]
                    mm = nc.tensor.matmul(ps[r, WB, C * p:C * p + C], nlev[r, l, p, :], x, start=True, stop=True)
                mm.then_inc(c_xmm, 1)

            def level_t(j, u, l):
                pe.wait_ge(c_xev, (LEVELS - 1) * j + l)
                before_small()
                for p, e, r in per_head():
                    mm = nc.tensor.matmul(ps[r, WB, C * p:C * p + C], xt[r, p, :], tt[u][r, 0, p, :], start=True, stop=True)
                if l < LEVELS - 1:
                    for p, e, r in per_head():
                        mm = nc.tensor.matmul(ps[r, WB, C * (PAIRS + p):C * (PAIRS + p) + C], tt[u][r, 0, p, :], xt[r, p, :], start=True, stop=True)
                mm.then_inc(c_tmm, 1)

            def right_side(i, u, st):
                pe.wait_ge(c_sev, i + 1)
                pe.wait_ge(c_yev, i + 1)
                before_small()
                for p, e, r in per_head():
                    nc.tensor.matmul(ps[r, WB + 1, C * p:C * p + C], ar[u][r, p, 0:C], st[r, p, :], start=(p == 0), stop=False, skip_group_check=True)
                for p, e, r in per_head():
                    mm = nc.tensor.matmul(ps[r, WB + 1, C * p:C * p + C], gm[u][:, e, p, 0:C], vz[u][:, p, C * e:C * e + C], start=False, stop=True,
                                          skip_group_check=True)
                mm.then_inc(c_rmm, 1)

            def solve(i, u):
                pe.wait_ge(c_rev, i + 1)
                pe.wait_ge(c_tev, LEVELS * (i + 1))
                before_small()
                for p, e, r in per_head():
                    mm = nc.tensor.matmul(ps[r, WB + 1, C * p:C * p + C], tt[u][r, 0, p, :], rhs[r, p, :], start=True, stop=True)
                mm.then_inc(c_umm, 1)

            def state_and_y(i, u, st):
                pe.wait_ge(c_uev, i + 1)
                pe.wait_ge(c_uvv, 2 * i + 2)
                before_small()
                for p, e, r in per_head():
                    mm = nc.tensor.matmul(ps[r, WB + 1, C * p:C * p + C], bktm[u][:, p, C * e:C * e + C], uv[:, p, C * e:C * e + C], start=True, stop=True)
                mm.then_inc(c_smm, 1)
                y_at = lambda r, p: ps[r, WB + 1, C * (PAIRS + p):C * (PAIRS + p) + C]
                for p, e, r in per_head():
                    nc.tensor.matmul(y_at(r, p), st[r, p, :], ar[u][r, p, C:2 * C], start=(p == 0), stop=False, skip_group_check=True)
                for p, e, r in per_head():
                    mm = nc.tensor.matmul(y_at(r, p), uv[:, p, C * e:C * e + C], gm[u][:, e, p, C:2 * C], start=False, stop=True, skip_group_check=True)
                mm.then_inc(c_ymm, 1)

            def slot_tensor(s, u):
                later = not isinstance(s, int) or s >= 1
                if isinstance(s, int) and s > CHUNKS:
                    right_side(s - 1, 1 - u, state[1])
                    yield
                    solve(s - 1, 1 - u)
                    yield
                    state_and_y(s - 1, 1 - u, state[1])
                    yield
                    yield
                    return
                products(s, u)
                yield
                turns(s, u)
                yield
                level_x(s, u, 0)
                if later:
                    right_side(s - 1, 1 - u, state[0])
                yield
                for l in range(1, LEVELS):
                    level_x(s, u, l)
                    yield
                    level_t(s, u, l)
                    if later and l == 1:
                        solve(s - 1, 1 - u)
                    if later and l == 2:
                        state_and_y(s - 1, 1 - u, state[0])
                    yield

            pe.wait_ge(qkv_norm, 6)
            pe.wait_ge(past_in, 48)
            pe.wait_ge(krope_copied, 2)

            def scores(jb, hp):
                e, u, i = jb % 2, jb % 2, jb // 2
                if jb >= PJOBS:
                    pe.wait_ge(p_exp, JOBS * hp + jb)
                    pe.wait_ge(t_ev, T_GROUPS * hp + T_FIRST[jb])
                    pe.wait_ge(o_ev, QTILES * hp + QTILES - 1 + 1)
                    for b in range(6):
                        mm = nc.tensor.matmul(ps[0:TS, b, 0:352], qt[e][0:96, TP:T], kt[e][0:96, TP + 352 * b:TP + 352 * b + 352], start=True, stop=True)
                else:
                    if jb >= 2:
                        pe.wait_ge(p_exp, JOBS * hp + jb - 1)
                    n = P * (i + 1)
                    for b, n0 in enumerate(range(0, n, 512)):
                        w = min(512, n - n0)
                        mm = nc.tensor.matmul(ps[:, 2 * u + b, 0:w], qt[e][0:96, P * i:P * i + P], kt[e][0:96, n0:n0 + w], start=True, stop=True)
                mm.then_inc(s_mm, 1)

            def turn(jb, g, hp):
                u = jb % 2
                pe.wait_ge(p_norm, JOBS * hp + jb + 1)
                t0, t1 = T_PLAN[jb][g]
                tg = T_FIRST[jb] + g
                if tg >= 1:
                    pe.wait_ge(t_ev, T_GROUPS * hp + tg)
                if jb >= PJOBS:
                    before_small()
                for t in range(t0, t1):
                    if jb < PJOBS:
                        mm = nc.tensor.transpose(ps[:, 4, P * (t - t0):P * (t - t0) + P], probs[u][:, P * t:P * t + P], ident)
                    else:
                        k0, rows = (0, TS) if t == 0 else (TS + P * (t - 1), P)
                        mm = nc.tensor.transpose(ps[0:rows, 4, TS * (t - t0):TS * (t - t0) + TS], probs[u][0:TS, k0:k0 + rows], con[0:TS, 0:TS])
                mm.then_inc(t_mm, 1)

            def values(jb, hp):
                e, u, i = jb % 2, jb % 2, jb // 2
                pe.wait_ge(t_ev, T_GROUPS * hp + T_FIRST[jb + 1])
                if i >= 1:
                    pe.wait_ge(o_ev, QTILES * hp + i + 1)
                r = slice(64 * e, 64 * e + 64)
                if jb == PJOBS:
                    pe.wait_ge(p_exp, JOBS * hp + JOBS)
                if jb >= PJOBS:
                    before_small()
                    for t in range(17):
                        rows = slice(0, TS if t == 0 else P)
                        mm = nc.tensor.matmul(ps[r, 5, 0:TS], vt[rows, 8 + t, r], pt[u][rows, TS * t:TS * t + TS], start=(t == 0), stop=(t == 16))
                else:
                    for t in range(i + 1):
                        mm = nc.tensor.matmul(ps[r, 5, 0:P], vt[:, t, r], pt[u][:, P * t:P * t + P], start=(t == 0), stop=(t == i))
                mm.then_inc(o_mm, 1)

            def attend_tensor(hp):
                pe.wait_ge(aw_in, 16 * hp + 16)
                pe.wait_ge(o_ev, QTILES * hp + 1)
                wq = lambda e, k: aw[:, 384 * e + P * k:384 * e + P * k + P]
                wk = lambda k: aw[:, 768 + P * k:768 + P * k + P]
                wv = lambda k: aw[:, 1024 + P * k:1024 + P * k + P]
                for l, (dst, n) in enumerate(K_CHUNKS):
                    if l >= 4:
                        pe.wait_ge(ka_ev, 7 * hp + l - 3)
                        pe.wait_ge(kd_ev, 7 * hp + l - 3)
                    for k in range(KKV):
                        src = ckv[:, k, dst:dst + n] if l < 3 else past[:, k, dst - T:dst - T + n]
                        mm = nc.tensor.matmul(ps[:, l % 4, 0:n], wk(k), src, start=(k == 0), stop=(k == KKV - 1))
                    mm.then_inc(kp_mm, 1)
                    yield
                for e in range(2):
                    for c, (a, n) in enumerate(CH):
                        l = 3 * e + c
                        if l >= 2:
                            pe.wait_ge(qa_ev, 6 * hp + l - 1)
                            pe.wait_ge(qd_ev, 6 * hp + l - 1 + 1)
                        for k in range(KQ):
                            mm = nc.tensor.matmul(ps[:, 4 + l % 2, 0:n], wq(e, k), cq[:, k, a:a + n], start=(k == 0), stop=(k == KQ - 1))
                        mm.then_inc(qp_mm, 1)
                        yield
                for g, tiles in enumerate(V_GROUPS):
                    if g + 3 < 7:
                        pe.wait_ge(ka_ev, 7 * hp + g + 4)
                        pe.wait_ge(kd_ev, 7 * hp + g + 4)
                    else:
                        pe.wait_ge(v_ev, 7 * hp + g - 3)
                    for x, t in enumerate(tiles):
                        rows = TS if t == 8 else P
                        for k in range(KKV):
                            src = ckv[:, k, P * t:P * t + rows] if t < 9 else past[:, k, P * (t - 9):P * (t - 9) + P]
                            mm = nc.tensor.matmul(ps[0:rows, (7 + g) % 4, P * x:P * x + P], src, wv(k), start=(k == 0), stop=(k == KKV - 1))
                    mm.then_inc(vp_mm, 1)
                    yield
                pe.wait_ge(v_ev, 7 * hp + 7)
                pe.wait_ge(kd_ev, 7 * hp + 7)
                pe.wait_ge(qa_ev, 6 * hp + 6)
                pe.wait_ge(qd_ev, 6 * hp + 6 + 1)
                for kind, jb, g in JOB_UNITS:
                    if kind == "scores":
                        scores(jb, hp)
                    elif kind == "turn":
                        turn(jb, g, hp)
                    else:
                        values(jb, hp)
                    yield

            pe.wait_ge(state_ready, 4)
            interleave(attend_tensor(0), ATT_COSTS, slots(slot_tensor, FIRST_SLOTS), slot_units(FIRST_SLOTS))
            with pe.Fori(1, PAIRS - 1) as hp:
                interleave(attend_tensor(hp), ATT_COSTS, slots(slot_tensor, MID_SLOTS, 4 * hp), slot_units(MID_SLOTS))
            pe.wait_ge(state_in, 16)
            interleave(attend_tensor(PAIRS - 1), ATT_COSTS, slots(slot_tensor, LAST_SLOTS), slot_units(LAST_SLOTS))

            pe.wait_ge(y_back, 16 * KR)
            pe.wait_ge(o_ev, QTILES * PAIRS + 1)
            pe.wait_ge(c_yev, CHUNKS + 1 + 1)
            for j in range(KR):
                for c, (a, n) in enumerate(CH):
                    if j:
                        pe.wait_ge(yc_done, j)
                    nc.tensor.matmul(ps[:, c, 0:n], block64, yt[:, j, a:a + n], start=True, stop=True).then_inc(mean_mm, 1)
                n = EARLY + j
                ada(n, late[n % 2], late_in[n % 2], 4)
                if j:
                    turn_row(n - 1, late_row, 6)
            pe.wait_ge(mrow_ready, EARLY + KR)
            pe.wait_ge(yc_done, KR)
            for j in range(KR):
                pe.wait_ge(ysq_done, j + 1)
                if j:
                    pe.wait_ge(y_root, j)
                for c, (a, n) in enumerate(CH):
                    mm = nc.tensor.matmul(ps[:, 3 + c, 0:n], block64, ysq[j % 2][:, a:a + n], start=True, stop=True)
                mm.then_inc(var_mm, 1)
                n = EARLY + KR + j
                ada(n, late[n % 2], late_in[n % 2], 0)
                turn_row(n - 1, late_row, 6)
            turn_row(SLABS - 1, late_row, 6)

            pe.wait_ge(osplit_lo, 2)
            with pe.Fori(OUT_M, FF_M) as m:
                for u in range(2):
                    project(pe, m, u)
            for name in ("m", "n2"):
                for c in range(3):
                    norm_sum(pe, name, sq2, c)

            def down(g, slot, first=False):
                pe.wait_ge(d_lo, 2 * g + 2)
                pe.wait_ge(act_lo, 6 * g + 6)
                for x in range(24):
                    k, (a, n) = x // 3, CH[x % 3]
                    if not (first and x < 2):
                        pe.wait_ge(d_added, 24 * g + x - 1 + 1)
                    for u in range(2):
                        for w, y in ((dhi, ahi), (dhi, alo), (dlo, ahi)):
                            mm = nc.tensor.matmul(ps[:, 6 + x % 2, 0:n], w[u][:, P * k:P * k + P], y[:, slot + u, a:a + n],
                                                  start=(u == 0 and w is dhi and y is ahi), stop=(u == 1 and w is dlo))
                    mm.then_inc(down_ready, 1)

            pe.wait_ge(lo_ready, 6)

            def group(g, slot):
                for j in range(2):
                    for u in range(2):
                        ff_project(g, j, u)

            def ff_project(g, j, u):
                m = 2 * g + FF_M + j
                pe.wait_ge(w_lo, 2 * m + u + 1)
                for c, (a, n) in enumerate(CH):
                    pe.wait_ge((sil_ready, prod_ready)[u], 6 * g + 3 * j + c - 2)
                    products(m, u, c)

            def products(m, u, c):
                a, n = CH[c]
                for k in range(KD):
                    for w, x in ((whi, hhi), (whi, hlo), (wlo, hhi)):
                        mm = nc.tensor.matmul(ps[:, 3 * u + c, 0:n], w[u][:, k, :], x[:, k, a:a + n],
                                              start=(k == 0 and w is whi and x is hhi), stop=(k == KD - 1 and w is wlo))
                mm.then_inc(out_ready[u], 1)

            for u in range(2):
                pe.wait_ge(bank_free[u], 3 * FF_M)
                pe.wait_ge(w_lo, 2 * FF_M + u + 1)
                for c in range(3):
                    products(FF_M, u, c)
            for u in range(2):
                ff_project(0, 1, u)
            group(1, 2)
            down(0, 0, first=True)
            with pe.Fori(0, (GROUPS - 3) // 2) as it:
                group(2 * it + 2, 0)
                down(2 * it + 1, 2)
                group(2 * it + 3, 2)
                down(2 * it + 2, 0)
            group(GROUPS - 1, 0)
            down(GROUPS - 2, 2)
            down(GROUPS - 1, 0)
            for c in range(3):
                norm_sum(pe, "f", sq3, c)


def shape_table():
    t = np.zeros((P, K_ALL), np.float32)
    t[:, K_IDENT:K_IDENT + P] = np.eye(P)
    t[:, K_ONES:K_ONES + P] = 1.0
    half = np.arange(P) // 64
    t[:, K_BLOCK:K_BLOCK + P] = half[:, None] == half[None, :]
    s, tok = (np.arange(P) % C)[:, None], np.arange(C)[None, :]
    t[:, K_GMASK:K_GMASK + C] = s < tok
    t[:, K_GMASK + C:K_GMASK + 2 * C] = s <= tok
    for l in range(LEVELS):
        m = 2 ** l
        t[:, K_LEVEL + C * l:K_LEVEL + C * l + C] = -1.0 * ((s // (2 * m) == tok // (2 * m)) & (s // m % 2 == 0) & (tok // m % 2 == 1))
    t[:, K_EYE2:K_EYE2 + C] = s == tok
    t[:, K_EPS] = 1e-6
    t[:, K_EPS + 1] = 64e-5
    inv = np.float32(10000.0) ** (-np.arange(0, ROPE, 2, dtype=np.float32) / np.float32(ROPE))
    pos = np.concatenate([np.arange(TP), PAST + np.arange(TS)]).astype(np.float32)
    ang = (inv[:, None] * pos[None, :]).astype(np.float32)
    cos, sin = np.cos(ang), np.sin(ang)
    t[64:96, K_CS:] = np.concatenate([cos, cos])
    t[96:128, K_CS:] = np.concatenate([-sin, sin])
    return t


def kernel(**inputs):
    import concourse.bacc as bacc
    from concourse.bass_utils import run_bass_kernel_spmd

    x = {k: np.asarray(v) for k, v in inputs.items()}

    def columns(v):
        return np.reshape(v, (-1, P)).T

    def tiles(w):
        return np.reshape(w, (KD, P, -1, P)).transpose(2, 1, 0, 3).reshape(-1, P, KD * P)

    def swapped(w):
        return np.concatenate([w[..., ROPE // 2:], w[..., :ROPE // 2]], axis=-1)

    w_in = x["w_in"][0]
    mla = QL + KVL
    kr_cols = w_in[:, mla:mla + ROPE]
    w_lat = np.concatenate([w_in[:, :mla], np.zeros((D, 64), np.float32), kr_cols, swapped(kr_cols)], axis=1)
    w_rw = w_in[:, mla + ROPE:]
    gate, up = tiles(x["w_gate"][0]), tiles(x["w_up"][0])
    gate_up = np.stack([gate, up], axis=1).reshape(-1, P, KD * P)
    w_tiles = np.concatenate([tiles(w_lat), tiles(w_rw), tiles(x["w_out"][0]), gate_up])

    wuq = x["w_uq"][0].reshape(KQ, P, HEADS, DH + ROPE)
    wuq = np.concatenate([wuq, swapped(wuq[..., DH:])], axis=-1).reshape(KQ, P, PAIRS, 2, P).transpose(2, 1, 3, 0, 4).reshape(PAIRS, P, -1)
    by_pair = lambda w: w.reshape(KKV, P, PAIRS, P).transpose(2, 1, 0, 3).reshape(PAIRS, P, -1)
    att_w = np.concatenate([wuq, by_pair(x["w_uk"][0]), by_pair(x["w_uv"][0])], axis=2)

    c2 = np.stack([x["c_prompt"][0].reshape(KD, P), x["c_sample"][0].reshape(KD, P)]).transpose(2, 1, 0).reshape(P, 2 * KD)
    vectors = np.concatenate([columns(x[n][0]) for n in ("norm_g", "q_norm_g", "kv_norm_g", "rw_mu", "rw_w0", "rw_a0", "rw_kk", "rw_ka",
                                                       "rw_rk", "lnx_g", "lnx_b", "ada_b")] + [c2, columns(x["state_shift"][0, 0])], axis=1)
    arrays = {
        "table": shape_table(),
        "vectors": vectors,
        "x_t": np.concatenate([x["x_prompt"][0], x["x_sample"][0]]).T,
        "ada_w": x["ada_w"][0],
        "w_tiles": w_tiles,
        "att_w": att_w,
        "w2a2": np.concatenate([x["rw_w2"][0], x["rw_a2"][0]]),
        "g2": x["rw_g2"][0],
        "w_down": x["w_down"][0],
        "ckv_t": x["cache_ckv"][0, 0].T,
        "krope_t": x["cache_krope"][0, 0].T,
        "state0": x["state_wkv"][0, 0].reshape(PAIRS, 2, DH, DH).transpose(1, 3, 0, 2).reshape(P, PAIRS * DH),
    }
    outs = {"y": (D, T), "ckv_out": (KVL, T), "krope_out": (ROPE, T), "wkv": (2, P, PAIRS * DH), "shift": (P, 2 * RW_TILES)}
    nc = bacc.Bacc("TRN2", target_bir_lowering=False, num_devices=1)
    d, feed = {}, {}
    for name, a in arrays.items():
        feed[f"in_{name}"] = np.ascontiguousarray(a)
        d[name] = nc.dram_tensor(f"in_{name}", a.shape, F32, kind="ExternalInput").ap()
    for name, shape in outs.items():
        d[name] = nc.dram_tensor(f"out_{name}", shape, F32, kind="ExternalOutput").ap()
    for name, shape in {"scan": (CHUNKS + 1, P, SF, PAIRS, C), "y_chunks": (CHUNKS + 1, P, PAIRS * C),
                        "bonus_rows": (KR, P, T), "gate_rows": (KR, P, T)}.items():
        d[name] = nc.dram_tensor(name, shape, F32, kind="Internal").ap()
    d["x_mid"] = nc.dram_tensor("x_mid", (D, T), F32, kind="Internal").ap()
    build(nc, d)
    got = run_bass_kernel_spmd(nc, [feed], core_ids=[0]).results[0]
    y, ckv, krope = (got[f"out_{n}"].T for n in ("y", "ckv_out", "krope_out"))
    wkv = got["out_wkv"].reshape(2, 2, DH, PAIRS, DH).transpose(0, 3, 1, 4, 2).reshape(2, HEADS, DH, DH)
    shift = got["out_shift"].reshape(P, RW_TILES, 2).transpose(2, 1, 0).reshape(2, RW_TILES * P)
    c = np.ascontiguousarray
    return (c(y[None, :TP]), c(y[None, TP:]), c(ckv[None, None, :TP]), c(krope[None, None, :TP]), c(wkv[None, None, 0]), c(shift[None, None, 0]),
            c(ckv[None, None, TP:]), c(krope[None, None, TP:]), c(wkv[None, None, 1]), c(shift[None, None, 1]))
```
